# Optimizing a Trainium2 kernel written in Bass

```python
import math
import jax, jax.numpy as jnp
from jax import lax
import numpy as np

D_MODEL = 1024
BATCH = 1
SEQ = 512
DEPTH = 1

EPS = 1e-6
D_FF = 2816
MLA_HEADS = 8
QK_NOPE = 64
QK_ROPE = 32
V_DIM = 64
Q_LORA = 384
KV_LORA = 256
ROPE_THETA = 10000.0
DIL_PATTERNS = ((128, 1), (512, 4), (2048, 16))
DIL_GROUPS = len(DIL_PATTERNS)
DIL_HEADS_PER_GROUP = 8
DIL_HEADS = DIL_GROUPS * DIL_HEADS_PER_GROUP
DIL_HEAD_DIM = 64
MAX_DIL = max(r for _, r in DIL_PATTERNS)
NUM_BUCKETS = 32
MAX_DISTANCE = 2048
BLK = 128
MLA_WIDTH = MLA_HEADS * V_DIM
DIL_WIDTH = DIL_HEADS_PER_GROUP * DIL_HEAD_DIM
IN_SIZES = (Q_LORA, KV_LORA, QK_ROPE,
            DIL_HEADS * DIL_HEAD_DIM, DIL_HEADS * DIL_HEAD_DIM, DIL_HEADS * DIL_HEAD_DIM,
            D_MODEL, D_MODEL)
D_IN = int(sum(IN_SIZES))
IN_OFFSETS = tuple(int(v) for v in np.cumsum(IN_SIZES)[:-1])
NEG_INF = -1e30

kernel_name = "hybrid_mla_dilated_gated_macaron"

def rms_norm(x, g):
    x32 = x.astype(jnp.float32)
    y = x32 * lax.rsqrt(jnp.mean(x32 * x32, axis=-1, keepdims=True) + EPS)
    return (y * g.astype(jnp.float32)).astype(x.dtype)

def swiglu(h, w_gate, w_up, w_down):
    return (jax.nn.silu(h @ w_gate) * (h @ w_up)) @ w_down

def rope_tables(positions):
    inv_freq = 1.0 / (ROPE_THETA ** (jnp.arange(0, QK_ROPE, 2, dtype=jnp.float32) / QK_ROPE))
    ang = positions.astype(jnp.float32)[..., None] * inv_freq
    return jnp.cos(ang), jnp.sin(ang)

def apply_rope(x, cos, sin):
    x1, x2 = jnp.split(x, 2, axis=-1)
    cos = cos.astype(x.dtype)
    sin = sin.astype(x.dtype)
    return jnp.concatenate([x1 * cos - x2 * sin, x1 * sin + x2 * cos], axis=-1)

def t5_bucket(dist):
    max_exact = NUM_BUCKETS // 2
    d = jnp.maximum(dist, 1).astype(jnp.float32)
    large = max_exact + (jnp.log(d / max_exact) / math.log(MAX_DISTANCE / max_exact)
                         * (NUM_BUCKETS - max_exact)).astype(jnp.int32)
    large = jnp.minimum(large, NUM_BUCKETS - 1)
    return jnp.where(dist < max_exact, dist, large).astype(jnp.int32)

def causal_dense_attention(q, k, v, scale):
    b, s, h, dqk = q.shape
    dv = v.shape[-1]
    nq = s // BLK
    q_blocks = q.reshape(b, nq, BLK, h, dqk).transpose(1, 0, 2, 3, 4)
    q_pos = jnp.arange(s, dtype=jnp.int32).reshape(nq, BLK)
    k_pos = jnp.arange(s, dtype=jnp.int32)

    def one_block(args):
        qb, qp = args
        logits = jnp.einsum('bqhd,bkhd->bhqk', qb, k).astype(jnp.float32) * scale
        logits = jnp.where(k_pos[None, :] <= qp[:, None], logits, NEG_INF)
        p = jax.nn.softmax(logits, axis=-1)
        return jnp.einsum('bhqk,bkhd->bqhd', p.astype(v.dtype), v)

    out = lax.map(one_block, (q_blocks, q_pos))
    return out.transpose(1, 0, 2, 3, 4).reshape(b, s, h * dv)

def dilated_group_attention(q, k, v, rel_bias_g, dilation, steps):
    b, s_pad, hg, dh = q.shape
    length = s_pad // dilation
    nb = length // BLK

    def to_blocks(t):
        t = t.reshape(b, length, dilation, hg, dh).transpose(0, 2, 1, 3, 4)
        return t.reshape(b, dilation, nb, BLK, hg, dh)

    def with_prev(t):
        prev = jnp.concatenate([jnp.zeros_like(t[:, :, :1]), t[:, :, :-1]], axis=2)
        return jnp.concatenate([prev, t], axis=3)

    qb = to_blocks(q)
    kk = with_prev(to_blocks(k))
    vv = with_prev(to_blocks(v))

    qi = jnp.arange(BLK, dtype=jnp.int32)[:, None]
    kj = jnp.arange(2 * BLK, dtype=jnp.int32)[None, :]
    step = qi + BLK - kj
    band = (step >= 0) & (step <= steps)
    first_block = (jnp.arange(nb) == 0)[:, None, None]
    valid = band[None] & ~(first_block & (kj < BLK)[None])
    bias = rel_bias_g[t5_bucket(jnp.maximum(step, 0) * dilation)]
    bias = bias.transpose(2, 0, 1).astype(jnp.float32)

    scale = DIL_HEAD_DIM ** -0.5
    logits = jnp.einsum('brnqhd,brnkhd->brnhqk', qb, kk).astype(jnp.float32) * scale + bias
    logits = jnp.where(valid[None, None, :, None], logits, NEG_INF)
    m = jnp.max(logits, axis=-1, keepdims=True)
    p = jnp.exp(logits - m)
    den = jnp.sum(p, axis=-1, keepdims=True)
    out = jnp.einsum('brnhqk,brnkhd->brnqhd', (p / den).astype(v.dtype), vv)
    lse = (m + jnp.log(den))[..., 0]

    out = out.reshape(b, dilation, length, hg, dh).transpose(0, 2, 1, 3, 4).reshape(b, s_pad, hg, dh)
    lse = lse.transpose(0, 1, 2, 4, 3).reshape(b, dilation, length, hg)
    lse = lse.transpose(0, 2, 1, 3).reshape(b, s_pad, hg)
    return out, lse

def dilated_mixture(q_d, k_d, v_d, rel_bias):
    b, s, _ = q_d.shape
    unit = MAX_DIL * BLK
    s_pad = -(-s // unit) * unit

    def prep(t):
        t = t.reshape(b, s, DIL_HEADS, DIL_HEAD_DIM)
        return jnp.pad(t, ((0, 0), (0, s_pad - s), (0, 0), (0, 0)))

    qp, kp, vp = prep(q_d), prep(k_d), prep(v_d)
    outs, lses = [], []
    for g, (window, dilation) in enumerate(DIL_PATTERNS):
        hs = slice(g * DIL_HEADS_PER_GROUP, (g + 1) * DIL_HEADS_PER_GROUP)
        o, l = dilated_group_attention(qp[:, :, hs], kp[:, :, hs], vp[:, :, hs],
                                       rel_bias[:, hs], dilation, window // dilation)
        outs.append(o)
        lses.append(l)
    w = jax.nn.softmax(jnp.stack(lses, axis=0), axis=0)
    y = jnp.sum(w[..., None] * jnp.stack(outs, axis=0).astype(jnp.float32), axis=0)
    return y[:, :s].reshape(b, s, DIL_WIDTH).astype(q_d.dtype)

def hybrid_mixer(h, positions, rel_bias, w_in, b_gate, q_norm, w_uq, kv_norm, w_ukv,
                 w_br_mla, w_br_dil, w_out):
    b, s, _ = h.shape
    proj = h @ w_in
    c_q, c_kv, k_rope, q_d, k_d, v_d, g_a, g_b = jnp.split(proj, IN_OFFSETS, axis=-1)

    cos, sin = rope_tables(positions)
    q = (rms_norm(c_q, q_norm) @ w_uq).reshape(b, s, MLA_HEADS, QK_NOPE + QK_ROPE)
    q_nope, q_pe = q[..., :QK_NOPE], q[..., QK_NOPE:]
    q_pe = apply_rope(q_pe, cos[:, :, None], sin[:, :, None])
    kv = (rms_norm(c_kv, kv_norm) @ w_ukv).reshape(b, s, MLA_HEADS, QK_NOPE + V_DIM)
    k_nope, v = kv[..., :QK_NOPE], kv[..., QK_NOPE:]
    k_pe = jnp.broadcast_to(apply_rope(k_rope, cos, sin)[:, :, None], (b, s, MLA_HEADS, QK_ROPE))
    q_full = jnp.concatenate([q_nope, q_pe], axis=-1)
    k_full = jnp.concatenate([k_nope, k_pe], axis=-1)
    y_a = causal_dense_attention(q_full, k_full, v, (QK_NOPE + QK_ROPE) ** -0.5) @ w_br_mla

    y_b = dilated_mixture(q_d, k_d, v_d, rel_bias) @ w_br_dil

    gate_a = jax.nn.sigmoid(g_a + b_gate[:D_MODEL])
    gate_b = jax.nn.sigmoid(g_b + b_gate[D_MODEL:])
    return (gate_a * y_a + gate_b * y_b) @ w_out

def setup_inputs(seed: int = 0) -> dict:
    key = jax.random.key(seed)
    ks = jax.random.split(key, 24)

    def w(k, shape, fan_in):
        return jax.random.normal(k, shape, jnp.float32) * (fan_in ** -0.5)

    def gain(k, shape):
        return 1.0 + 0.02 * jax.random.normal(k, shape, jnp.float32)

    x = jax.random.normal(ks[0], (BATCH, SEQ, D_MODEL), jnp.float32)
    offset = jax.random.randint(ks[1], (BATCH, 1), 0, 4096, dtype=jnp.int32)
    positions = offset + jnp.arange(SEQ, dtype=jnp.int32)[None, :]
    L = DEPTH
    return {
        "x": x,
        "positions": positions,
        "rel_bias": 0.5 * jax.random.normal(ks[2], (NUM_BUCKETS, DIL_HEADS), jnp.float32),
        "norm_final": gain(ks[3], (D_MODEL,)),
        "ffn1_norm": gain(ks[4], (L, D_MODEL)),
        "ffn1_w_gate": w(ks[5], (L, D_MODEL, D_FF), D_MODEL),
        "ffn1_w_up": w(ks[6], (L, D_MODEL, D_FF), D_MODEL),
        "ffn1_w_down": w(ks[7], (L, D_FF, D_MODEL), D_FF),
        "mix_norm": gain(ks[8], (L, D_MODEL)),
        "w_in": w(ks[9], (L, D_MODEL, D_IN), D_MODEL),
        "b_gate": 0.01 * jax.random.normal(ks[10], (L, 2 * D_MODEL), jnp.float32),
        "q_norm": gain(ks[11], (L, Q_LORA)),
        "w_uq": w(ks[12], (L, Q_LORA, MLA_HEADS * (QK_NOPE + QK_ROPE)), Q_LORA),
        "kv_norm": gain(ks[13], (L, KV_LORA)),
        "w_ukv": w(ks[14], (L, KV_LORA, MLA_HEADS * (QK_NOPE + V_DIM)), KV_LORA),
        "w_br_mla": w(ks[15], (L, MLA_WIDTH, D_MODEL), MLA_WIDTH),
        "w_br_dil": w(ks[16], (L, DIL_WIDTH, D_MODEL), DIL_WIDTH),
        "w_out": w(ks[17], (L, D_MODEL, D_MODEL), D_MODEL),
        "ffn2_norm": gain(ks[18], (L, D_MODEL)),
        "ffn2_w_gate": w(ks[19], (L, D_MODEL, D_FF), D_MODEL),
        "ffn2_w_up": w(ks[20], (L, D_MODEL, D_FF), D_MODEL),
        "ffn2_w_down": w(ks[21], (L, D_FF, D_MODEL), D_FF),
    }

def reference(x, positions, rel_bias, norm_final, ffn1_norm, ffn1_w_gate, ffn1_w_up, ffn1_w_down,
              mix_norm, w_in, b_gate, q_norm, w_uq, kv_norm, w_ukv, w_br_mla, w_br_dil, w_out,
              ffn2_norm, ffn2_w_gate, ffn2_w_up, ffn2_w_down):
    for l in range(DEPTH):
        x = x + 0.5 * swiglu(rms_norm(x, ffn1_norm[l]), ffn1_w_gate[l], ffn1_w_up[l], ffn1_w_down[l])
        x = x + hybrid_mixer(rms_norm(x, mix_norm[l]), positions, rel_bias, w_in[l], b_gate[l],
                             q_norm[l], w_uq[l], kv_norm[l], w_ukv[l], w_br_mla[l], w_br_dil[l], w_out[l])
        x = x + 0.5 * swiglu(rms_norm(x, ffn2_norm[l]), ffn2_w_gate[l], ffn2_w_up[l], ffn2_w_down[l])
    return rms_norm(x, norm_final)


_drawn_inputs = setup_inputs


def setup_inputs(seed=0):
    import zlib

    import numpy as np

    out = dict(_drawn_inputs(seed))
    spreads = {}
    factors = {'norm_final': 8.997,
     'ffn1_norm': 6.653,
     'mix_norm': 8.0,
     'b_gate': 64.0,
     'q_norm': 8.0,
     'kv_norm': 8.0,
     'ffn2_norm': 20.25}
    for name, (base, spread) in spreads.items():
        noise = np.random.default_rng([zlib.crc32(name.encode()), seed]).standard_normal(out[name].shape)
        drawn = base * np.exp(spread * noise) if base else spread * noise
        out[name] = __import__('jax').numpy.asarray(drawn.astype(out[name].dtype))
    for name, factor in factors.items():
        out[name] = (out[name] * factor).astype(out[name].dtype)
    return out
```

```python
import math
from contextlib import ExitStack

import concourse.bass as bass
import numpy as np
from concourse import mybir

F32 = mybir.dt.float32
F32R = mybir.dt.float32r
I32 = mybir.dt.int32
ALU = mybir.AluOpType
ACT = mybir.ActivationFunctionType
AX = mybir.AxisListType

P = 128
SEQ = 512
BLOCKS = SEQ // P
D_MODEL = 1024
KM = D_MODEL // P
D_FF = 2816
KF = D_FF // P
EPS = 1e-6
MLA_HEADS, QK_NOPE, QK_ROPE, V_DIM = 8, 64, 32, 64
QK_DIM = QK_NOPE + QK_ROPE
Q_LORA, KV_LORA = 384, 256
KQ, KKV = Q_LORA // P, KV_LORA // P
ROPE_THETA = 10000.0
GROUPS, GROUP_HEADS, HEAD_DIM = 3, 8, 64
PAIRS = GROUP_HEADS // 2
DIL_QKV = GROUPS * GROUP_HEADS * HEAD_DIM
NUM_BUCKETS, MAX_DISTANCE = 32, 2048
STRIDES = (1, 4, 16)
NEG_INF = -1e30
MLA_SCALE = QK_DIM ** -0.5
DIL_SCALE = HEAD_DIM ** -0.5



def _few_bits(value, bits, parts):
    out = []
    for _ in range(parts - 1):
        unit = 2.0 ** (math.floor(math.log2(value)) + 1 - bits)
        out.append(math.floor(value / unit) * unit)
        value -= out[-1]
    return out + [value]


TWO_PI = _few_bits(2 * math.pi, 9, 4)

IN_KV = Q_LORA
IN_ROPE = IN_KV + KV_LORA
IN_Q = IN_ROPE + QK_ROPE
IN_K = IN_Q + DIL_QKV
IN_V = IN_K + DIL_QKV
IN_GATES = IN_V + DIL_QKV

TILES = 8
RAW, SPLIT = 4, 2
DOWN_PARTS = ((0, 8), (8, 15), (15, 22))
MLA_TILES = (8, 2, 4, 4, 5, 5, 4, 4)
PIECES = {}
CHUNKS = {}


def _lay_out_stream():
    n = c = 0
    for name, pieces, chunks in (
        ("up1", 2 * KF, 2 * KF), ("down1", 3 * KM, KM), ("latent", 6, 6), ("mla", 16, 20),
        ("dil", 12 * PAIRS, 12 * PAIRS), ("merge", KM, 2 * KM), ("out", KM, KM),
        ("up2", 2 * KF, 2 * KF), ("down2", 3 * KM, KM),
    ):
        PIECES[name], CHUNKS[name] = n, c
        n, c = n + pieces, c + chunks
    PIECES["end"], CHUNKS["end"] = n, c


_lay_out_stream()

C_IDENT, C_ONES, C_EXPAND, C_FOLD = 0, P, 2 * P, 2 * P + SEQ
C_MOD = C_FOLD + SEQ
C_DIV = C_MOD + BLOCKS
C_CAUSAL = C_DIV + BLOCKS
C_FREQ = C_CAUSAL + P
C_TURN, C_PHASE, C_SIGN, C_EPS = C_FREQ + 1, C_FREQ + 2, C_FREQ + 3, C_FREQ + 4
C_END = C_FREQ + 5
G_FFN1, G_MIX, G_FFN2, G_FINAL, G_Q, G_KV = 0, KM, 2 * KM, 3 * KM, 4 * KM, 4 * KM + KQ
G_BIAS = G_KV + KKV
G_END = G_BIAS + 2 * KM
T5_LEN = (3 * P - 1, 2 * P - 1, 2 * P - 1)
T5_AT = (0, T5_LEN[0], T5_LEN[0] + T5_LEN[1])
T5_END = sum(T5_LEN)


def t5_bucket(distance):
    exact = NUM_BUCKETS // 2
    d = np.maximum(distance, 1).astype(np.float32)
    scaled = np.log(d / np.float32(exact)) / np.float32(math.log(MAX_DISTANCE / exact))
    large = exact + (scaled * np.float32(NUM_BUCKETS - exact)).astype(np.int32)
    return np.where(distance < exact, distance, np.minimum(large, NUM_BUCKETS - 1))


def shape_constants():
    c = np.zeros((P, C_END), np.float32)
    p = np.arange(P)
    j = np.arange(SEQ)
    c[:, C_IDENT:C_IDENT + P] = np.eye(P)
    c[:, C_ONES:C_ONES + P] = 1.0
    c[:, C_EXPAND:C_EXPAND + SEQ] = p[:, None] == j[None, :] // 4
    c[:, C_MOD:C_MOD + BLOCKS] = p[:, None] % 4 == np.arange(4)
    c[:, C_FOLD:C_FOLD + SEQ] = p[:, None] == (4 * (j % P) + j // P)[None, :] % P
    c[:, C_DIV:C_DIV + BLOCKS] = p[:, None] // 32 == np.arange(4)
    c[:, C_CAUSAL:C_CAUSAL + P] = np.where(p[None, :] <= p[:, None], 0.0, NEG_INF)
    freq = 1.0 / ROPE_THETA ** (np.arange(0, QK_ROPE, 2, dtype=np.float32) / np.float32(QK_ROPE))
    for row in range(QK_NOPE, P):
        c[row, C_FREQ] = freq.astype(np.float32)[row % 16]
        cosine = row < QK_DIM
        c[row, C_TURN] = 0.25 if cosine else 0.0
        c[row, C_PHASE] = math.pi / 2 if cosine else 0.0
        c[row, C_SIGN] = -1.0 if QK_DIM <= row < QK_DIM + 16 else 1.0
    c[:, C_EPS] = EPS
    onehot = np.zeros((NUM_BUCKETS, T5_END), np.float32)
    mask = np.full((GROUP_HEADS, T5_END), NEG_INF, np.float32)
    for g, stride in enumerate(STRIDES):
        apart = (T5_LEN[g] + 1) // 2 + (P // 2 if g == 0 else 0) - 1 - np.arange(T5_LEN[g])
        unit = 4 if g == 2 else 1
        ok = (apart >= 0) & (apart <= P) & (apart % unit == 0)
        bucket = t5_bucket(np.maximum(apart, 0) // unit * stride)
        at = T5_AT[g] + np.arange(T5_LEN[g])
        onehot[bucket[ok], at[ok]] = 1.0
        mask[:, at[ok]] = 0.0
    return c, onehot, mask


def decoder_layer(nc, x_t, positions, rel_bias, gains_in, tables, onehot_in, mask_in, ffn, w_latent, w_lora_up,
                  w_mla_gates, w_dil, w_branches, w_out, skew, y_t):
    ctx = ExitStack()
    held = []

    def sb(name, shape, dt=F32):
        return ctx.enter_context(nc.sbuf_tensor(name, shape, dt))

    def shared(name, shape, dt=F32):
        manager = nc.sbuf_tensor(name, shape, dt)
        held.append(manager)
        return manager.__enter__()

    def give_back(n):
        for _ in range(n):
            held.pop().__exit__(None, None, None)

    def sem(name):
        return ctx.enter_context(nc.semaphore(name))

    with ctx:
        x = sb("x", [P, KM, SEQ])
        act_hi = sb("act_hi", [P, KM, SEQ], F32R)
        act_lo = sb("act_lo", [P, KM, SEQ], F32R)
        raw = sb("raw", [P, RAW, TILES * P])
        w_hi = sb("w_hi", [P, SPLIT, TILES * P], F32R)
        w_lo = sb("w_lo", [P, SPLIT, TILES * P], F32R)
        const = sb("const", [P, C_END])
        gains = sb("gains", [P, G_END])
        neg_bias = sb("neg_bias", [P, 2 * KM])
        rstd = sb("rstd", [P, SEQ])
        sumsq = sb("sumsq", [P, SEQ])
        square = sb("square", [P, SEQ])
        work = sb("work", [P, 4, SEQ])
        rope = sb("rope", [P, SEQ])
        ident = const[:, C_IDENT:C_IDENT + P]
        ones = const[:, C_ONES:C_ONES + P]
        causal = const[:, C_CAUSAL:C_CAUSAL + P]

        stats = sb("stats", [P, 2, GROUPS, 2, 2 * BLOCKS])
        exchanged = work[:, 3, 0:6 * 4 * 2 * BLOCKS]
        weight = sb("weight", [P, GROUPS, 4 * BLOCKS])
        neg_top = sb("neg_top", [P, 4 * BLOCKS])
        total = sb("total", [P, 4 * BLOCKS])
        mla_stats = sb("mla_stats", [P, 4, BLOCKS])

        hid_hi = shared("hid_hi", [P, KF, SEQ], F32R)
        hid_lo = shared("hid_lo", [P, KF, SEQ], F32R)
        give_back(2)
        shared("hid_head", [P, KF + KF // 2, SEQ])
        position_i = shared("position_i", [P, SEQ], I32)
        angle = shared("angle", [P, SEQ])
        turns = shared("turns", [P, SEQ])
        t5_onehot = shared("t5_onehot", [NUM_BUCKETS, T5_END])
        t5_mask = shared("t5_mask", [GROUP_HEADS, T5_END])
        t5_row = shared("t5_row", [GROUP_HEADS, T5_END])
        t5_rel = shared("t5_rel", [NUM_BUCKETS, GROUPS * GROUP_HEADS])
        give_back(8)
        mixed = shared("mixed", [P, 2 * PAIRS, SEQ])
        gates = shared("gates", [P, 2 * KM, SEQ])
        probs_t = shared("probs_t", [P, 2, SEQ])
        lat_hi = shared("lat_hi", [P, KQ + KKV, SEQ], F32R)
        lat_lo = shared("lat_lo", [P, KQ + KKV, SEQ], F32R)
        sumsq_kv = shared("sumsq_kv", [P, SEQ])
        rstd_q = shared("rstd_q", [P, SEQ])
        rstd_kv = shared("rstd_kv", [P, SEQ])
        rope_q = shared("rope_q", [P, SEQ])
        rotated = shared("rotated", [P, SEQ])
        mla_q = shared("mla_q", [P, 2, SEQ])
        mla_k = shared("mla_k", [P, 2, SEQ])
        mla_vt = shared("mla_vt", [P, SEQ])
        mla_v = shared("mla_v", [P, BLOCKS, V_DIM])
        mla_p = shared("mla_p", [P, 10 * P])
        give_back(12)
        bias0 = shared("bias0", [P, GROUP_HEADS, 2 * P])
        bias12 = shared("bias12", [P, 2, GROUP_HEADS, P])
        dil_q = shared("dil_q", [P, GROUPS, SEQ])
        dil_k = shared("dil_k", [P, GROUPS, SEQ])
        dil_vt = shared("dil_vt", [P, 2, SEQ])
        dil_v = shared("dil_v", [P, GROUPS, BLOCKS, P])
        dil_p = shared("dil_p", [P, 2, 15 * P])
        give_back(7)
        merged_hi = shared("merged_hi", [P, KM, SEQ], F32R)
        merged_lo = shared("merged_lo", [P, KM, SEQ], F32R)
        give_back(2)
        give_back(3)
        bank = [ctx.enter_context(nc.psum_tensor(f"bank{i}", [P, SEQ], F32)) for i in range(8)]

        raw_loaded = [sem(f"raw_loaded{i}") for i in range(RAW)]
        hi_ready, lo_ready = sem("hi_ready"), sem("lo_ready")
        piece_done = sem("piece_done")
        inner_done, chunk_taken = sem("inner_done"), sem("chunk_taken")
        x_loaded = [sem(f"x_loaded{k}") for k in range(KM)]
        const_loaded, table_loaded = sem("const_loaded"), sem("table_loaded")
        act_rounded, act_split = sem("act_rounded"), sem("act_split")
        squared, sumsq_added = sem("squared"), sem("sumsq_added")
        norm_full, root_ready, rstd_ready = sem("norm_full"), sem("root_ready"), sem("rstd_ready")
        silu_ready, hid_rounded, hid_split = sem("silu_ready"), sem("hid_rounded"), sem("hid_split")
        setup_dve, setup_act, setup_pe = sem("setup_dve"), sem("setup_act"), sem("setup_pe")
        skew_stored, bias_loaded = sem("skew_stored"), sem("bias_loaded")
        own = sem("own")
        gate_exp = sem("gate_exp")
        mla_q_ready = sem("mla_q_ready")
        mla_scores, mla_max, mla_exp, mla_scaled = sem("mla_scores"), sem("mla_max"), sem("mla_exp"), sem("mla_scaled")
        turned, turned_taken, pv_done = sem("turned"), sem("turned_taken"), sem("pv_done")
        mixed_taken = sem("mixed_taken")
        dil_scores, dil_taken = sem("dil_scores"), sem("dil_taken")
        dil_max, dil_exp, dil_scaled = sem("dil_max"), sem("dil_exp"), sem("dil_scaled")
        v_turned, v_taken = sem("v_turned"), sem("v_taken")
        stats_moved, weight_ready, weight_exp = sem("stats_moved"), sem("weight_ready"), sem("weight_exp")
        mixed_rounded, mixed_split = sem("mixed_rounded"), sem("mixed_split")
        merge_ready, merged_rounded, merged_split = sem("merge_ready"), sem("merged_rounded"), sem("merged_split")
        y_ready, stored = sem("y_ready"), sem("stored")


        def load(sp, s, d, source, tiles):
            if s >= RAW:
                sp.wait_ge(lo_ready, s + d - (RAW - 1))
            sp.dma_start(raw[:, s % RAW, 0:tiles * P], source).then_inc(raw_loaded[s % RAW], 16)

        def split_hi(act, s, d, tiles):
            act.wait_ge(raw_loaded[s % RAW], 16 * (s // RAW + 1) + 16 // RAW * d)
            if s >= SPLIT:
                act.wait_ge(piece_done, s + d - (SPLIT - 1))
            nc.scalar.activation(w_hi[:, s % SPLIT, 0:tiles * P], raw[:, s % RAW, 0:tiles * P],
                                 ACT.Copy).then_inc(hi_ready, 1)

        def split_lo(dve, s, d, tiles):
            dve.wait_ge(hi_ready, s + d + 1)
            nc.vector.tensor_tensor(w_lo[:, s % SPLIT, 0:tiles * P], raw[:, s % RAW, 0:tiles * P],
                                    w_hi[:, s % SPLIT, 0:tiles * P].bitcast(F32),
                                    ALU.subtract).then_inc(lo_ready, 1)

        def multiply(s, tiles, out, hi, lo, start=True, stop=True, before=None):
            last = None
            for k, t in enumerate(tiles):
                if before is not None:
                    before(k)
                a = w_hi[:, s % SPLIT, t * P:(t + 1) * P]
                b = w_lo[:, s % SPLIT, t * P:(t + 1) * P]
                first, end = start and k == 0, stop and k == len(tiles) - 1
                nc.tensor.matmul(out, a, hi(k), start=first, stop=False)
                nc.tensor.matmul(out, a, lo(k), start=False, stop=False)
                last = nc.tensor.matmul(out, b, hi(k), start=False, stop=end)
            return last

        def free_chunk(pe, c):
            pe.wait_ge(chunk_taken, c - 1)

        def act_of(k):
            return act_hi[:, k, :], act_lo[:, k, :]

        block = ctx.enter_context(nc.Block())

        @block.sync
        def _(sp):
            def load_up_turn(f, turn, i):
                for q in range(4):
                    source = ffn[f][q % 2][bass.ds(2 * (turn + i) + q // 2, 1)]
                    load(sp, PIECES[f"up{f + 1}"] + 4 * turn + q, 4 * i, source.rearrange("a p n -> p (a n)"), TILES)

            def load_down(f):
                with sp.Fori(0, KM // 4) as i:
                    for m in range(4):
                        row = ffn[f][2][bass.ds(4 * i + m, 1)].rearrange("a p n -> p (a n)")
                        for part, (a, b) in enumerate(DOWN_PARTS):
                            load(sp, PIECES[f"down{f + 1}"] + 3 * m + part, 12 * i, row[:, a * P:b * P], b - a)

            def load_ffn(f):
                load_up_turn(f, 0, 0)
                with sp.Fori(0, KF // 2 - 1) as i:
                    load_up_turn(f, 1, i)
                load_down(f)

            load_ffn(0)
            for q in range(6):
                load(sp, PIECES["latent"] + q, 0, w_latent[q], TILES)
            with sp.Fori(0, 2) as i:
                up = w_lora_up[bass.ds(i, 1)].rearrange("a p n -> p (a n)")
                gate = [w_mla_gates[bass.ds(2 * i + g, 1)].rearrange("a p n -> p (a n)") for g in range(2)]
                half = TILES // 2
                sources = (up[:, 0:8 * P], up[:, 8 * P:10 * P], gate[0][:, 0:half * P], gate[0][:, half * P:],
                           up[:, 10 * P:15 * P], up[:, 15 * P:20 * P], gate[1][:, 0:half * P], gate[1][:, half * P:])
                for q, source in enumerate(sources):
                    load(sp, PIECES["mla"] + q, 8 * i, source, MLA_TILES[q])
            with sp.Fori(0, PAIRS) as i:
                for q in range(12):
                    load(sp, PIECES["dil"] + q, 12 * i, w_dil[bass.ds(i, 1), q].rearrange("a p n -> p (a n)"), TILES)
            for phase, source in (("merge", w_branches), ("out", w_out)):
                with sp.Fori(0, KM // 4) as i:
                    for q in range(4):
                        load(sp, PIECES[phase] + q, 4 * i, source[bass.ds(4 * i + q, 1)].rearrange("a p n -> p (a n)"), TILES)
            load_ffn(1)
            for k in range(KM):
                sp.wait_ge(y_ready, k + 1)
                sp.dma_start(y_t[k], x[:, k, :]).then_inc(stored, 16)
            sp.wait_ge(stored, 16 * KM)

        @block.gpsimd
        def _(pool):
            pool.dma_start(gains[:, :], gains_in).then_inc(const_loaded, 16)
            pool.dma_start(const[:, :], tables).then_inc(const_loaded, 16)
            pool.dma_start(position_i[QK_NOPE:P, :], positions.to_broadcast([P - QK_NOPE, SEQ])).then_inc(table_loaded, 16)
            pool.dma_start(t5_onehot[:, :], onehot_in).then_inc(table_loaded, 16)
            pool.dma_start(t5_mask[:, :], mask_in).then_inc(table_loaded, 16)
            pool.dma_start(t5_rel[:, :], rel_bias).then_inc(table_loaded, 16)
            pool.wait_ge(setup_dve, 2)
            copies = skew.rearrange("h (p n) -> h p n", p=P)[:, :, 0:T5_END]
            row = t5_row[:, :].rearrange("h (a n) -> h a n", a=1).to_broadcast([GROUP_HEADS, P, T5_END])
            pool.dma_start(copies, row).then_inc(skew_stored, 16)
            pool.wait_ge(skew_stored, 16)
            pool.wait_ge(mixed_taken, PAIRS)
            for g, width in enumerate((2 * P, P, P)):
                source = bass.AP(skew.tensor, T5_AT[g] + P - 1,
                                 [[T5_END, P], [P * (T5_END + 1), GROUP_HEADS], [1, width]])
                table = bias0[:, :, :] if g == 0 else bias12[:, g - 1, :, :]
                pool.dma_start(table, source).then_inc(bias_loaded, 16)

        @block.tensor
        def _(pe):
            def norm(k, source, out):
                pe.wait_ge(sumsq_added, k)
                nc.tensor.matmul(out, ones, source, start=True, stop=True).then_inc(norm_full, 1)

            def up_turn(f, turn, i, first=False):
                for q in range(4):
                    s = PIECES[f"up{f + 1}"] + 4 * turn + q
                    c = CHUNKS[f"up{f + 1}"] + 4 * turn + q
                    if c >= 2:
                        free_chunk(pe, c + 4 * i)
                    pe.wait_ge(lo_ready, s + 4 * i + 1)

                    def act_chunk(k):
                        pe.wait_ge(act_split, (0, 2 * KM + KQ + KKV)[f] + k + 1)

                    multiply(s, range(TILES), bank[c % 2][:, :], lambda k: act_hi[:, k, :], lambda k: act_lo[:, k, :],
                             before=act_chunk if first and q == 0 else None).then_inc(piece_done, 1)
                    if first and q == 0:
                        norm((KM, 3 * KM + KQ + KKV)[f], sumsq[:, :], bank[7][:, :])
                    if first and f == 0 and q == 1:
                        pe.wait_ge(table_loaded, 64)
                        for g in range(GROUPS):
                            last = nc.tensor.matmul(bank[4 + g][0:GROUP_HEADS, 0:T5_LEN[g]],
                                                    t5_rel[:, g * GROUP_HEADS:(g + 1) * GROUP_HEADS],
                                                    t5_onehot[:, T5_AT[g]:T5_AT[g] + T5_LEN[g]], start=True, stop=True)
                        last.then_inc(setup_pe, 1)

            def down_turn(f, turn, i):
                for m in range(4):
                    c = CHUNKS[f"down{f + 1}"] + 4 * turn + m
                    free_chunk(pe, c + 4 * i)
                    for part, (a, b) in enumerate(DOWN_PARTS):
                        s = PIECES[f"down{f + 1}"] + 12 * turn + 3 * m + part
                        pe.wait_ge(lo_ready, s + 12 * i + 1)
                        pe.wait_ge(hid_split, KF * f + b)
                        multiply(s, range(b - a), bank[c % 2][:, :], lambda k: hid_hi[:, a + k, :],
                                 lambda k: hid_lo[:, a + k, :], start=part == 0, stop=part == 2).then_inc(piece_done, 1)

            def ffn_products(f):
                up_turn(f, 0, 0, first=True)
                with pe.Fori(0, KF // 2 - 1) as i:
                    up_turn(f, 1, i)
                with pe.Fori(0, 2) as i:
                    down_turn(f, 0, i)

            def project(s, d, c, bank_of, before=None):
                free_chunk(pe, c)
                pe.wait_ge(lo_ready, s + d + 1)
                multiply(s, range(TILES), bank_of, lambda k: act_hi[:, k, :], lambda k: act_lo[:, k, :],
                         before=before).then_inc(piece_done, 1)

            pe.wait_ge(const_loaded, 32)
            ffn_products(0)

            for q in range(6):
                c = CHUNKS["latent"] + q
                project(PIECES["latent"] + q, 0, c, bank[c % 2][:, :],
                        (lambda k: pe.wait_ge(act_split, KM + k + 1)) if q == 0 else None)
                if q == 0:
                    norm(2 * KM, sumsq[:, :], bank[7][:, :])
            norm(2 * KM + KQ, sumsq[:, :], bank[7][:, :])
            norm(2 * KM + KQ + KKV, sumsq_kv[:, :], bank[4][:, :])

            def lora(s, tiles, c, first_chunk):
                free_chunk(pe, c)
                out = bank[first_chunk % 2][:, :]
                base = 0 if len(tiles) == KQ else KQ
                return multiply(s, tiles, out, lambda k: lat_hi[:, base + k, :], lambda k: lat_lo[:, base + k, :])

            def turn_values(h, i):
                unit = 4 * h
                for b in range(BLOCKS):
                    last = nc.tensor.transpose(bank[5 + unit % 2][:, b * V_DIM:(b + 1) * V_DIM],
                                               mla_vt[QK_NOPE:P, b * P:(b + 1) * P], ident[QK_NOPE:P, QK_NOPE:P])
                last.then_inc(turned, 1)

            def score(h, i):
                pe.wait_ge(mla_q_ready, h + 4 * i + 1)
                pe.wait_ge(chunk_taken, CHUNKS["mla"] + (1, 3, 6, 8)[h] + 10 * i + 1)
                if h:
                    pe.wait_ge(mla_exp, 4 * h + 16 * i)
                for b, out in enumerate((bank[2][:, 0:P], bank[3][:, 0:2 * P], bank[2][:, P:SEQ], bank[4][:, :])):
                    last = nc.tensor.matmul(out, mla_q[0:QK_DIM, h % 2, b * P:(b + 1) * P],
                                            mla_k[0:QK_DIM, h % 2, 0:(b + 1) * P], start=True, stop=True,
                                            skip_group_check=True)
                last.then_inc(mla_scores, 1)

            def turn_probs(h, i, part):
                unit = 4 * h + 1 + part
                pe.wait_ge(mla_scaled, 4 * h + 16 * i + 4)
                pe.wait_ge(turned_taken, unit + 16 * i - 1)
                at = 0
                for key in ((0,), (1,), (2, 3))[part]:
                    for b in range(key, BLOCKS):
                        row = b * (b + 1) // 2 + key
                        last = nc.tensor.transpose(bank[5 + unit % 2][:, at:at + P], mla_p[:, row * P:(row + 1) * P], ident)
                        at += P
                last.then_inc(turned, 1)

            def attend(h, i, part):
                unit = 4 * h + 1 + part
                pe.wait_ge(turned_taken, unit + 16 * i + 1)
                if h % 2 == 0 and part == 0:
                    pe.wait_ge(mixed_taken, 2 * i + h // 2)
                row = V_DIM * (h % 2)
                at = 0
                for key in ((0,), (1,), (2, 3))[part]:
                    width = SEQ - key * P
                    last = nc.tensor.matmul(bank[7][row:row + V_DIM, key * P:SEQ], mla_v[:, key, :],
                                            probs_t[:, (3 * h + part) % 2, at:at + width],
                                            start=key == 0, stop=key == 3, skip_group_check=True)
                    at += width
                last.then_inc(pv_done, 1)

            def values(h, i):
                turn_probs(h, i, 0)
                turn_probs(h, i, 1)
                attend(h, i, 0)
                turn_probs(h, i, 2)
                attend(h, i, 1)
                attend(h, i, 2)

            with pe.Fori(0, 2) as i:
                s, d, c, e = PIECES["mla"], 8 * i, CHUNKS["mla"], 10 * i

                def gate_half(piece, chunk, part):
                    pe.wait_ge(lo_ready, s + d + piece + 1)
                    if part == 0:
                        free_chunk(pe, c + e + chunk)
                    base = part * TILES // 2
                    multiply(s + piece, range(TILES // 2), bank[(c + chunk) % 2][:, :],
                             lambda k: act_hi[:, base + k, :], lambda k: act_lo[:, base + k, :],
                             start=part == 0, stop=part == 1).then_inc(piece_done, 1)

                pe.wait_ge(lo_ready, s + d + 1)
                pe.wait_ge(act_split, 2 * KM + KQ + KKV)
                lora(s, (0, 1, 2), c + e, c).then_inc(inner_done, 1)
                lora(s, (3, 4), c + e + 1, c + 1).then_inc(inner_done, 1)
                lora(s, (5, 6, 7), c + e + 2, c).then_inc(piece_done, 1)
                score(0, i)
                turn_values(0, i)
                pe.wait_ge(lo_ready, s + d + 2)
                lora(s + 1, (0, 1), c + e + 3, c + 3).then_inc(piece_done, 1)
                gate_half(2, 4, 0)
                gate_half(3, 4, 1)
                values(0, i)
                score(1, i)
                turn_values(1, i)
                for h in (2, 3):
                    pe.wait_ge(lo_ready, s + d + h + 3)
                    lora(s + h + 2, (0, 1, 2), c + e + 2 * h + 1, c + 2 * h + 1).then_inc(inner_done, 1)
                    lora(s + h + 2, (3, 4), c + e + 2 * h + 2, c + 2 * h + 2).then_inc(piece_done, 1)
                    values(h - 1, i)
                    score(h, i)
                    turn_values(h, i)
                gate_half(6, 9, 0)
                gate_half(7, 9, 1)
                values(3, i)

            def tokens(g, b):
                return slice(b * P, (b + 1) * P) if g == 0 else slice(b, SEQ, BLOCKS)

            def dil_score(g, i):
                for e in range(2):
                    unit = 2 * g + e
                    if unit >= 2:
                        pe.wait_ge(dil_taken, unit + 6 * i - 1)
                    rows = slice(HEAD_DIM * e, HEAD_DIM * (e + 1))
                    one, two = (bank[2], bank[3]) if e == 0 else (bank[4], bank[7])
                    for b in range(BLOCKS):
                        if g == 0:
                            out = (one[:, 0:P], one[:, P:3 * P], two[:, 0:2 * P], two[:, 2 * P:SEQ])[b]
                            keys = slice(max(b - 1, 0) * P, (b + 1) * P)
                        else:
                            out, keys = one[:, b * P:(b + 1) * P], tokens(g, b)
                        last = nc.tensor.matmul(out, dil_q[rows, g, tokens(g, b)], dil_k[rows, g, keys],
                                                start=True, stop=True, skip_group_check=True)
                    last.then_inc(dil_scores, 1)

            def turn_dil_values(g, i):
                if g:
                    pe.wait_ge(v_taken, g + 3 * i)
                for b in range(BLOCKS):
                    last = nc.tensor.transpose(bank[3][:, b * P:(b + 1) * P], dil_vt[:, g % 2, tokens(g, b)], ident)
                last.then_inc(v_turned, 1)

            def turn_dil(e, part, i):
                unit = 4 * e + part
                pe.wait_ge(turned_taken, 4 * MLA_HEADS + unit + 8 * i - 1)
                pe.wait_ge(dil_scaled, (4 * e + (2, 2, 3, 4)[part]) + 8 * i)
                if part < 2:
                    columns = [(0, P, 2 * P, 3 * P), (4 * P, 5 * P, 6 * P)][part]
                else:
                    columns = [(7 + 4 * (part - 2) + b) * P for b in range(BLOCKS)]
                for at, column in enumerate(columns):
                    last = nc.tensor.transpose(bank[5 + unit % 2][:, at * P:(at + 1) * P],
                                               dil_p[:, e, column:column + P], ident)
                last.then_inc(turned, 1)

            def attend_dil(e, part, i):
                unit = 4 * e + part
                pe.wait_ge(turned_taken, 4 * MLA_HEADS + unit + 8 * i + 1)
                rows = slice(HEAD_DIM * e, HEAD_DIM * (e + 1))
                pt = probs_t[:, unit % 2, :]
                if part < 2:
                    for n in range(2):
                        key = 2 * part + n
                        width = min(2 * P, SEQ - key * P)
                        last = nc.tensor.matmul(bank[2][rows, key * P:key * P + width], dil_v[:, 0, key, rows],
                                                pt[:, 2 * n * P:2 * n * P + width], start=key == 0, stop=False,
                                                skip_group_check=True)
                else:
                    for b in range(BLOCKS):
                        last = nc.tensor.matmul(bank[2][rows, b:SEQ:BLOCKS], dil_v[:, part - 1, b, rows],
                                                pt[:, b * P:(b + 1) * P], start=False,
                                                stop=part == 3 and b == BLOCKS - 1, skip_group_check=True)
                last.then_inc(pv_done, 1)

            with pe.Fori(0, PAIRS) as i:
                s, d, c = PIECES["dil"], 12 * i, CHUNKS["dil"]

                def dil_project(q):
                    project(s + q, d, c + d + q, bank[(c + q) % 2][:, :])

                dil_project(0)
                dil_project(1)
                dil_project(2)
                pe.wait_ge(mixed_taken, PAIRS + i)
                pe.wait_ge(chunk_taken, c + d + 2)
                dil_score(0, i)
                dil_project(3)
                dil_project(4)
                pe.wait_ge(chunk_taken, c + d + 4)
                dil_score(1, i)
                dil_project(5)
                dil_project(6)
                pe.wait_ge(chunk_taken, c + d + 6)
                dil_score(2, i)
                dil_project(7)
                pe.wait_ge(chunk_taken, c + d + 7)
                turn_dil_values(0, i)
                dil_project(8)
                pe.wait_ge(chunk_taken, c + d + 8)
                turn_dil_values(1, i)
                dil_project(9)
                pe.wait_ge(chunk_taken, c + d + 9)
                turn_dil_values(2, i)
                dil_project(10)
                pe.wait_ge(dil_exp, 24 * i + 24)
                for b in range(BLOCKS):
                    nc.tensor.matmul(bank[7][:, b * 16:(b + 1) * 16], const[:, C_FOLD + b * P:C_FOLD + (b + 1) * P],
                                     stats[:, :, 0, 0, :], start=True, stop=True, skip_group_check=True)
                for b in range(BLOCKS):
                    last = nc.tensor.matmul(bank[7][:, 64 + b * 32:96 + b * 32],
                                            const[:, C_EXPAND + b * P:C_EXPAND + (b + 1) * P],
                                            stats[:, :, 1:3, 1, :], start=True, stop=True, skip_group_check=True)
                last.then_inc(stats_moved, 1)
                dil_project(11)
                pe.wait_ge(v_taken, 3 * i + 3)
                for e in range(2):
                    turn_dil(e, 0, i)
                    for part in range(4):
                        if part < 3:
                            turn_dil(e, part + 1, i)
                        attend_dil(e, part, i)

            with pe.Fori(0, KM // 4) as i:
                for q in range(4):
                    s, c = PIECES["merge"] + q, CHUNKS["merge"] + 2 * q
                    pe.wait_ge(lo_ready, s + 4 * i + 1)
                    for branch in range(2):
                        base = branch * PAIRS
                        free_chunk(pe, c + branch + 8 * i)
                        last = multiply(s, range(base, base + PAIRS), bank[branch][:, :], lambda k: act_hi[:, base + k, :],
                                        lambda k: act_lo[:, base + k, :],
                                        before=(lambda k: pe.wait_ge(mixed_split, base + k + 1)) if q == 0 else None)
                        last.then_inc(piece_done if branch else inner_done, 1)
            with pe.Fori(0, KM // 4) as i:
                for q in range(4):
                    s, c = PIECES["out"] + q, CHUNKS["out"] + q
                    free_chunk(pe, c + 4 * i)
                    pe.wait_ge(lo_ready, s + 4 * i + 1)
                    multiply(s, range(TILES), bank[c % 2][:, :], lambda k: merged_hi[:, k, :], lambda k: merged_lo[:, k, :],
                             before=(lambda k: pe.wait_ge(merged_split, k + 1)) if q == 0 else None).then_inc(piece_done, 1)
            ffn_products(1)
            norm(4 * KM + KQ + KKV, sumsq[:, :], bank[7][:, :])

        @block.scalar
        def _(act):
            for k in range(KM):
                act.dma_start(x[:, k, :], x_t[k]).then_inc(x_loaded[k], 16)

            def round_chunk(k, source, gain, hi):
                if hi is not None:
                    act.wait_ge(const_loaded, 32)
                    nc.scalar.activation(hi, source, ACT.Copy, scale=gain).then_inc(act_rounded, 1)
                act.wait_ge(const_loaded, 32)
                if not isinstance(k, int) or k:
                    act.wait_ge(sumsq_added, k)
                nc.scalar.activation(square[:, :], source, ACT.Square).then_inc(squared, 1)

            def root(n, sums, features):
                act.wait_ge(norm_full, n + 1)
                nc.scalar.activation(square[:, :], sums, ACT.Sqrt, bias=const[:, C_EPS:C_EPS + 1],
                                     scale=1.0 / features).then_inc(root_ready, 1)

            def up_turn(f, turn, i, first=False):
                for q in range(4):
                    s = PIECES[f"up{f + 1}"] + 4 * turn + q
                    c = CHUNKS[f"up{f + 1}"] + 4 * turn + q
                    split_hi(act, s + 1, 4 * i, TILES)
                    if first and q == 0:
                        root((0, 4)[f], bank[7][:, :], D_MODEL)
                    j = 2 * turn + q // 2
                    act.wait_ge(chunk_taken, c + 4 * i + 1)
                    act.wait_ge(const_loaded, 32)
                    if q % 2 == 0:
                        nc.scalar.activation(work[:, 1, :], work[:, 0, :], ACT.Silu).then_inc(silu_ready, 1)
                    else:
                        nc.scalar.activation(hid_hi[:, bass.ds(2 * i + j, 1), :],
                                             work[:, 3:4, :], ACT.Copy).then_inc(hid_rounded, 1)
                    if first and f == 0 and q == 1:
                        act.wait_ge(setup_dve, 1)
                        nc.scalar.activation(rope[QK_NOPE:P, :], angle[QK_NOPE:P, :], ACT.Sin,
                                             scale=const[QK_NOPE:P, C_SIGN:C_SIGN + 1]).then_inc(setup_act, 1)

            def down_turn(f, turn, i, gain, final):
                for m in range(4):
                    for part in range(3):
                        s = PIECES[f"down{f + 1}"] + 12 * turn + 3 * m + part
                        if not (final and m == 3 and part == 2):
                            following = DOWN_PARTS[(part + 1) % 3]
                            split_hi(act, s + 1, 12 * i, following[1] - following[0])
                    act.wait_ge(chunk_taken, CHUNKS[f"down{f + 1}"] + 4 * turn + m + 4 * i + 1)
                    k = 4 * turn + m
                    chunk = bass.ds(4 * i + k, 1)
                    before = (KM, 3 * KM + KQ + KKV)[f]
                    if gain is None:
                        round_chunk(4 * i + k + before, x[:, chunk, :], None, None)
                    else:
                        round_chunk(4 * i + k + before, x[:, chunk, :], gains[:, bass.ds(4 * i + k + gain, 1)],
                                    act_hi[:, chunk, :])

            act.wait_ge(const_loaded, 32)
            for k in range(KM):
                act.wait_ge(x_loaded[k], 16)
                round_chunk(k, x[:, k, :], gains[:, G_FFN1 + k:G_FFN1 + k + 1], act_hi[:, k, :])
                if k == 0:
                    split_hi(act, 0, 0, TILES)
            nc.scalar.mul(neg_bias[:, :], gains[:, G_BIAS:G_BIAS + 2 * KM], -1.0).then_inc(setup_act, 1)
            up_turn(0, 0, 0, first=True)
            with act.Fori(0, KF // 2 - 1) as i:
                up_turn(0, 1, i)
            with act.Fori(0, 2) as i:
                down_turn(0, 0, i, G_MIX, False)

            for q in range(6):
                split_hi(act, PIECES["latent"] + q + 1, 0, TILES)
                if q == 0:
                    root(1, bank[7][:, :], D_MODEL)
                if q < 5:
                    act.wait_ge(chunk_taken, CHUNKS["latent"] + q + 1)
                    round_chunk(2 * KM + q, work[:, q % 2, :], gains[:, G_Q + q:G_Q + q + 1], lat_hi[:, q, :])
            act.wait_ge(sumsq_added, 2 * KM + KQ + KKV)
            root(2, bank[7][:, :], Q_LORA)
            act.wait_ge(rstd_ready, 3)
            root(3, bank[4][:, :], KV_LORA)

            def gate_sigmoid(c, b):
                act.wait_ge(chunk_taken, c + 1)
                act.wait_ge(setup_act, 1)
                nc.scalar.activation(work[:, 1, :], work[:, 0, :], ACT.Exp, bias=neg_bias[:, bass.ds(b, 1)],
                                     scale=-1.0).then_inc(gate_exp, 1)

            def take_values(h, i):
                act.wait_ge(turned, 4 * h + 16 * i + 1)
                nc.scalar.copy(mla_v[:, :, :].rearrange("p b n -> p (b n)"),
                               bank[5 + (4 * h) % 2][:, 0:BLOCKS * V_DIM]).then_inc(turned_taken, 1)

            def exponentials(h, i):
                for b, source in enumerate((bank[2][:, 0:P], bank[3][:, 0:2 * P], bank[2][:, P:SEQ], bank[4][:, :])):
                    if b == 0:
                        act.wait_ge(mla_max, h + 4 * i + 1)
                    row = b * (b + 1) // 2
                    nc.scalar.activation(mla_p[:, row * P:(row + b + 1) * P], source, ACT.Exp,
                                         bias=mla_stats[:, 1, b:b + 1], scale=MLA_SCALE,
                                         accum_out=mla_stats[:, 2, b:b + 1]).then_inc(mla_exp, 1)

            def take_probs(h, i):
                for part, width in enumerate((4 * P, 3 * P, 3 * P)):
                    unit = 4 * h + 1 + part
                    act.wait_ge(turned, unit + 16 * i + 1)
                    n = 3 * h + part
                    if n >= 2:
                        act.wait_ge(pv_done, n + 12 * i - 1)
                    nc.scalar.copy(probs_t[:, n % 2, 0:width], bank[5 + unit % 2][:, 0:width]).then_inc(turned_taken, 1)

            with act.Fori(0, 2) as i:
                s, d, c, e = PIECES["mla"], 8 * i, CHUNKS["mla"], 10 * i
                split_hi(act, s + 1, d, MLA_TILES[1])
                take_values(0, i)
                split_hi(act, s + 2, d, MLA_TILES[2])
                exponentials(0, i)
                split_hi(act, s + 3, d, MLA_TILES[3])
                split_hi(act, s + 4, d, MLA_TILES[4])
                gate_sigmoid(c + e + 4, 2 * i)
                take_probs(0, i)
                take_values(1, i)
                split_hi(act, s + 5, d, MLA_TILES[5])
                exponentials(1, i)
                take_probs(1, i)
                take_values(2, i)
                split_hi(act, s + 6, d, MLA_TILES[6])
                exponentials(2, i)
                take_probs(2, i)
                take_values(3, i)
                split_hi(act, s + 7, d, MLA_TILES[7])
                exponentials(3, i)
                split_hi(act, s + 8, d, TILES)
                gate_sigmoid(c + e + 9, 2 * i + 1)
                take_probs(3, i)

            def dil_exponentials(g, i):
                for e in range(2):
                    unit = 2 * g + e
                    act.wait_ge(dil_max, unit + 6 * i + 1)
                    for b in range(BLOCKS):
                        first, blocks = ((0, 1), (1, 2), (3, 2), (5, 2))[b] if g == 0 else (3 + 4 * g + b, 1)
                        p = dil_p[:, e, first * P:(first + blocks) * P]
                        order, at = min(g, 1), 2 * b + e
                        nc.scalar.activation(p, p, ACT.Exp, bias=stats[:, 0, g, order, at:at + 1],
                                             accum_out=stats[:, 1, g, order, at:at + 1]).then_inc(dil_exp, 1)

            def take_dil_values(g, i):
                act.wait_ge(v_turned, g + 3 * i + 1)
                nc.scalar.copy(dil_v[:, g, :, :].rearrange("p b n -> p (b n)"), bank[3][:, :]).then_inc(v_taken, 1)

            with act.Fori(0, PAIRS) as i:
                s, d, c = PIECES["dil"], 12 * i, CHUNKS["dil"]
                for q in range(12):
                    split_hi(act, s + q + 1, d, TILES)
                    if q in (3, 5, 7):
                        dil_exponentials(q // 2 - 1, i)
                    if q == 11:
                        act.wait_ge(weight_ready, i + 1)
                        nc.scalar.activation(weight[:, :, :], weight[:, :, :], ACT.Exp).then_inc(weight_exp, 1)
                    if q >= 9:
                        gate_sigmoid(c + d + q, 3 * i + 4 + q - 9)
                    if q in (7, 8, 9):
                        take_dil_values(q - 7, i)
                for unit in range(8):
                    width = 3 * P if unit % 4 == 1 else SEQ
                    act.wait_ge(turned, 4 * MLA_HEADS + unit + 8 * i + 1)
                    act.wait_ge(pv_done, 3 * MLA_HEADS + unit + 8 * i - 1)
                    nc.scalar.copy(probs_t[:, unit % 2, 0:width], bank[5 + unit % 2][:, 0:width]).then_inc(turned_taken, 1)

            act.wait_ge(piece_done, PIECES["merge"])
            for k in range(2 * PAIRS):
                act.wait_ge(mixed_taken, k + 1)
                nc.scalar.copy(act_hi[:, k, :], mixed[:, k, :]).then_inc(mixed_rounded, 1)
            with act.Fori(0, KM // 4) as i:
                for q in range(4):
                    split_hi(act, PIECES["merge"] + q + 1, 4 * i, TILES)
                    act.wait_ge(merge_ready, q + 4 * i + 1)
                    act.wait_ge(const_loaded, 32)
                    nc.scalar.copy(merged_hi[:, bass.ds(4 * i + q, 1), :], work[:, 2:3, :]).then_inc(merged_rounded, 1)
            for k in range(KM):
                split_hi(act, PIECES["out"] + k + 1, 0, TILES)
                act.wait_ge(chunk_taken, CHUNKS["out"] + k + 1)
                round_chunk(2 * KM + KQ + KKV + k, x[:, k, :], gains[:, G_FFN2 + k:G_FFN2 + k + 1], act_hi[:, k, :])
            up_turn(1, 0, 0, first=True)
            with act.Fori(0, KF // 2 - 1) as i:
                up_turn(1, 1, i)
            down_turn(1, 0, 0, None, False)
            down_turn(1, 1, 0, None, True)
            root(5, bank[7][:, :], D_MODEL)

        @block.vector
        def _(dve):
            count = {"before": 0, "turn": 0, "earlier": 0, "per": 0}

            def one():
                count["turn"] += 1
                return 1

            def so_far():
                return count["before"] + count["turn"] + count["earlier"]

            def enter_loop(i, per):
                count.update(before=count["before"] + count["turn"], turn=0, earlier=i * per, per=per)

            def leave_loop(turns):
                assert count["turn"] == count["per"], count
                count.update(before=count["before"] + turns * count["per"], turn=0, earlier=0)

            def split_chunk(k, source, gain, hi, lo, sums, first):
                if lo is not None:
                    dve.wait_ge(act_rounded, k + 1)
                    nc.vector.scalar_tensor_tensor(out=lo, in0=source, scalar=gain, in1=hi.bitcast(F32),
                                                   op0=ALU.mult, op1=ALU.subtract).then_inc(act_split, 1)
                dve.wait_ge(squared, k + 1)
                if first:
                    nc.vector.tensor_copy(sums, square[:, :]).then_inc(sumsq_added, 1)
                else:
                    dve.wait_ge(sumsq_added, k)
                    nc.vector.tensor_tensor(sums, sums, square[:, :], ALU.add).then_inc(sumsq_added, 1)

            def reciprocal_root(n, out):
                dve.wait_ge(root_ready, n + 1)
                nc.vector.reciprocal(out, square[:, :]).then_inc(rstd_ready, 1)
                dve.wait_ge(rstd_ready, n + 1)

            def rotation_angles():
                dve.wait_ge(table_loaded, 64)
                rows = slice(QK_NOPE, P)
                a, n = angle[rows, :], turns[rows, :]
                nc.vector.tensor_copy(n, position_i[rows, :]).then_inc(own, one())
                dve.wait_ge(own, so_far())
                nc.vector.tensor_scalar(a, n, const[rows, C_FREQ:C_FREQ + 1], None, ALU.mult).then_inc(own, one())
                dve.wait_ge(own, so_far())
                nc.vector.tensor_scalar(n, a, 1.0 / (2 * math.pi), const[rows, C_TURN:C_TURN + 1],
                                                    ALU.mult, ALU.add).then_inc(own, one())
                for magic in (1.5 * 2 ** 23, -1.5 * 2 ** 23):
                    dve.wait_ge(own, so_far())
                    nc.vector.tensor_scalar(n, n, magic, None, ALU.add).then_inc(own, one())
                for part in TWO_PI:
                    dve.wait_ge(own, so_far())
                    nc.vector.scalar_tensor_tensor(out=a, in0=n, scalar=-part, in1=a,
                                                               op0=ALU.mult, op1=ALU.add).then_inc(own, one())
                dve.wait_ge(own, so_far())
                nc.vector.tensor_scalar(a, a, const[rows, C_PHASE:C_PHASE + 1], None, ALU.add).then_inc(own, one())
                dve.wait_ge(own, so_far())
                nc.vector.tensor_scalar(a, a, 3.1415925, -3.1415925, ALU.min, ALU.max).then_inc(setup_dve, 1)

            def bias_rows():
                dve.wait_ge(setup_pe, 1)
                for g in range(GROUPS):
                    at = slice(T5_AT[g], T5_AT[g] + T5_LEN[g])
                    last = nc.vector.tensor_tensor(t5_row[:, at], bank[4 + g][0:GROUP_HEADS, 0:T5_LEN[g]],
                                                   t5_mask[:, at], ALU.add)
                last.then_inc(setup_dve, 1)

            def up_turn(f, turn, i, first=False):
                for q in range(4):
                    s = PIECES[f"up{f + 1}"] + 4 * turn + q
                    j = 2 * turn + q // 2
                    hidden = KF * f + j
                    split_lo(dve, s + 1, 4 * i, TILES)
                    if first and q == 0:
                        reciprocal_root((0, 4)[f], rstd[:, :])
                    if q % 2 == 0:
                        dve.wait_ge(piece_done, s + 4 * i + 1)
                        nc.vector.tensor_tensor(work[:, 0, :], bank[s % 2][:, :], rstd[:, :], ALU.mult).then_inc(chunk_taken, 1)
                    else:
                        dve.wait_ge(silu_ready, hidden + 2 * i + 1)
                        nc.vector.tensor_tensor(work[:, 2, :], work[:, 1, :], rstd[:, :], ALU.mult).then_inc(own, one())
                        dve.wait_ge(piece_done, s + 4 * i + 1)
                        dve.wait_ge(own, so_far())
                        nc.vector.tensor_tensor(work[:, 3, :], bank[s % 2][:, :], work[:, 2, :], ALU.mult).then_inc(chunk_taken, 1)
                        chunk = bass.ds(2 * i + j, 1)
                        dve.wait_ge(chunk_taken, CHUNKS[f"up{f + 1}"] + 4 * turn + q + 4 * i + 1)
                        dve.wait_ge(hid_rounded, hidden + 2 * i + 1)
                        nc.vector.tensor_tensor(hid_lo[:, chunk, :], work[:, 3:4, :], hid_hi[:, chunk, :].bitcast(F32),
                                                ALU.subtract).then_inc(hid_split, 1)
                    if first and f == 0:
                        if q == 1:
                            rotation_angles()
                        if q == 2:
                            bias_rows()

            def down_turn(f, turn, i, gain, final):
                for m in range(4):
                    for part in range(3):
                        s = PIECES[f"down{f + 1}"] + 12 * turn + 3 * m + part
                        if not (final and m == 3 and part == 2):
                            following = DOWN_PARTS[(part + 1) % 3]
                            split_lo(dve, s + 1, 12 * i, following[1] - following[0])
                    c = CHUNKS[f"down{f + 1}"] + 4 * turn + m
                    k = 4 * turn + m
                    chunk = bass.ds(4 * i + k, 1)
                    dve.wait_ge(piece_done, s + 12 * i + 1)
                    nc.vector.scalar_tensor_tensor(out=x[:, chunk, :], in0=bank[c % 2][:, :].rearrange("p (a n) -> p a n", a=1),
                                                   scalar=0.5, in1=x[:, chunk, :],
                                                   op0=ALU.mult, op1=ALU.add).then_inc(chunk_taken, 1)
                    dve.wait_ge(chunk_taken, c + 4 * i + 1)
                    before = (KM, 3 * KM + KQ + KKV)[f]
                    hi, lo, g = None, None, None
                    if gain is not None:
                        hi, lo, g = act_hi[:, chunk, :], act_lo[:, chunk, :], gains[:, bass.ds(4 * i + k + gain, 1)]
                    split_chunk(4 * i + k + before, x[:, chunk, :], g, hi, lo, sumsq[:, :], False)

            def clear_sums():
                nc.vector.memset(sumsq[:, :], 0.0).then_inc(own, one())
                dve.wait_ge(own, so_far())

            def gate_finish(k):
                dve.wait_ge(gate_exp, k + 1)
                nc.vector.tensor_scalar(work[:, 2, :], work[:, 1, :], 1.0, None, ALU.add).then_inc(own, one())
                dve.wait_ge(own, so_far())
                nc.vector.reciprocal(gates[:, bass.ds(k, 1), :], work[:, 2:3, :]).then_inc(own, one())

            def gate_take(s, d, parity):
                dve.wait_ge(piece_done, s + d + 1)
                nc.vector.tensor_tensor(work[:, 0, :], bank[parity][:, :], rstd[:, :], ALU.mult).then_inc(chunk_taken, 1)

            for k in range(KM):
                split_chunk(k, x[:, k, :], gains[:, G_FFN1 + k:G_FFN1 + k + 1], act_hi[:, k, :], act_lo[:, k, :],
                            sumsq[:, :], k == 0)
                if k == 0:
                    split_lo(dve, 0, 0, TILES)
            up_turn(0, 0, 0, first=True)
            dve.wait_ge(skew_stored, 16)
            dve.wait_ge(setup_act, 2)
            with dve.Fori(0, KF // 2 - 1) as i:
                enter_loop(i, 2)
                up_turn(0, 1, i)
            leave_loop(KF // 2 - 1)
            clear_sums()
            with dve.Fori(0, 2) as i:
                down_turn(0, 0, i, G_MIX, False)

            for q in range(6):
                s, c = PIECES["latent"] + q, CHUNKS["latent"] + q
                split_lo(dve, s + 1, 0, TILES)
                if q == 0:
                    reciprocal_root(1, rstd[:, :])
                dve.wait_ge(piece_done, s + 1)
                if q < 5:
                    latent = work[:, q % 2, :]
                    nc.vector.tensor_tensor(latent, bank[c % 2][:, :], rstd[:, :], ALU.mult).then_inc(chunk_taken, 1)
                    dve.wait_ge(chunk_taken, c + 1)
                    split_chunk(2 * KM + q, latent, gains[:, G_Q + q:G_Q + q + 1], lat_hi[:, q, :], lat_lo[:, q, :],
                                sumsq[:, :] if q < KQ else sumsq_kv[:, :], q in (0, KQ))
                else:
                    low, high = slice(QK_NOPE, QK_DIM), slice(QK_DIM, P)
                    nc.vector.tensor_tensor(work[low, 2, :], rope[low, :], rstd[low, :], ALU.mult).then_inc(own, one())
                    nc.vector.tensor_tensor(work[high, 2, :], rope[high, :], rstd[high, :], ALU.mult).then_inc(own, one())
                    dve.wait_ge(own, so_far())
                    nc.vector.tensor_tensor(mla_k[low, 0, :], bank[c % 2][low, :], work[low, 2, :], ALU.mult).then_inc(own, one())
                    nc.vector.tensor_tensor(rotated[low, :], bank[c % 2][high, :], work[high, 2, :], ALU.mult)\
                      .then_inc(chunk_taken, 1)
                    dve.wait_ge(chunk_taken, c + 1)
                    dve.wait_ge(own, so_far())
                    nc.vector.tensor_tensor(mla_k[low, 0, :], mla_k[low, 0, :], rotated[low, :], ALU.add).then_inc(own, one())
                    dve.wait_ge(own, so_far())
                    nc.vector.tensor_copy(mla_k[low, 1, :], mla_k[low, 0, :]).then_inc(own, one())
            reciprocal_root(2, rstd_q[:, :])
            nc.vector.tensor_tensor(rope_q[QK_NOPE:P, :], rope[QK_NOPE:P, :], rstd_q[QK_NOPE:P, :], ALU.mult).then_inc(own, one())
            reciprocal_root(3, rstd_kv[:, :])
            dve.wait_ge(own, so_far())

            def take_query(h, i, parity):
                low, high = slice(QK_NOPE, QK_DIM), slice(QK_DIM, P)
                out = mla_q[:, h % 2, :]
                nc.vector.tensor_tensor(out[0:QK_NOPE, :], bank[parity][0:QK_NOPE, :], rstd_q[0:QK_NOPE, :], ALU.mult)
                nc.vector.tensor_tensor(out[low, :], bank[parity][low, :], rope_q[low, :], ALU.mult)
                if h:
                    dve.wait_ge(mla_q_ready, h + 4 * i)
                nc.vector.tensor_tensor(rotated[low, :], bank[parity][high, :], rope_q[high, :], ALU.mult)\
                  .then_inc(chunk_taken, 1)

            def add_rotated(h, c):
                low = slice(QK_NOPE, QK_DIM)
                dve.wait_ge(chunk_taken, c + 1)
                out = mla_q[low, h % 2, :]
                nc.vector.tensor_tensor(out, out, rotated[low, :], ALU.add).then_inc(mla_q_ready, 1)

            def take_key_value(h, parity):
                nc.vector.tensor_tensor(mla_k[0:QK_NOPE, h % 2, :], bank[parity][0:QK_NOPE, :], rstd_kv[0:QK_NOPE, :], ALU.mult)
                nc.vector.tensor_tensor(mla_vt[QK_NOPE:P, :], bank[parity][QK_NOPE:P, :], rstd_kv[QK_NOPE:P, :], ALU.mult)\
                  .then_inc(chunk_taken, 1)

            def maxima(h, i):
                dve.wait_ge(mla_scores, h + 4 * i + 1)
                for out in (bank[2][:, 0:P], bank[3][:, P:2 * P], bank[2][:, 3 * P:SEQ], bank[4][:, 3 * P:SEQ]):
                    last = nc.vector.tensor_tensor(out, out, causal, ALU.add)
                last.then_inc(own, one())
                dve.wait_ge(own, so_far())
                for b, source in enumerate((bank[2][:, 0:P], bank[3][:, 0:2 * P], bank[2][:, P:SEQ], bank[4][:, :])):
                    last = nc.vector.tensor_reduce(mla_stats[:, 0, b:b + 1], source, AX.X, ALU.max)
                last.then_inc(own, one())
                dve.wait_ge(own, so_far())
                nc.vector.tensor_scalar(mla_stats[:, 1, :], mla_stats[:, 0, :], -MLA_SCALE, None, ALU.mult).then_inc(mla_max, 1)

            def normalize(h, i):
                dve.wait_ge(mla_exp, 4 * h + 16 * i + 4)
                nc.vector.reciprocal(mla_stats[:, 3, :], mla_stats[:, 2, :]).then_inc(own, one())
                dve.wait_ge(own, so_far())
                for b in range(BLOCKS):
                    row = b * (b + 1) // 2
                    p = mla_p[:, row * P:(row + b + 1) * P]
                    nc.vector.tensor_scalar(p, p, mla_stats[:, 3, b:b + 1], None, ALU.mult).then_inc(mla_scaled, 1)

            def take_mixed(k, units, source):
                dve.wait_ge(pv_done, units)
                nc.vector.tensor_copy(mixed[:, bass.ds(k, 1), :], source.rearrange("p (a n) -> p a n", a=1)).then_inc(mixed_taken, 1)

            with dve.Fori(0, 2) as i:
                enter_loop(i, 4 * 3 + 2 * 2)
                s, d, c, e = PIECES["mla"], 8 * i, CHUNKS["mla"], 10 * i
                split_lo(dve, s + 1, d, MLA_TILES[1])
                dve.wait_ge(inner_done, 4 * i + 1)
                take_query(0, i, c % 2)
                add_rotated(0, c + e)
                dve.wait_ge(inner_done, 4 * i + 2)
                take_key_value(0, (c + 1) % 2)
                dve.wait_ge(piece_done, s + d + 1)
                take_query(1, i, c % 2)
                add_rotated(1, c + e + 2)
                split_lo(dve, s + 2, d, MLA_TILES[2])
                maxima(0, i)
                dve.wait_ge(piece_done, s + d + 2)
                take_key_value(1, (c + 3) % 2)
                split_lo(dve, s + 3, d, MLA_TILES[3])
                normalize(0, i)
                split_lo(dve, s + 4, d, MLA_TILES[4])
                gate_take(s + 3, d, (c + 4) % 2)
                split_lo(dve, s + 5, d, MLA_TILES[5])
                gate_finish(2 * i)
                for h in (1, 2):
                    maxima(h, i)
                    dve.wait_ge(inner_done, 4 * i + h + 2)
                    first = 2 * h + 3
                    take_query(h + 1, i, (c + first) % 2)
                    add_rotated(h + 1, c + e + first)
                    dve.wait_ge(piece_done, s + d + h + 4)
                    take_key_value(h + 1, (c + first + 1) % 2)
                    normalize(h, i)
                    split_lo(dve, s + h + 5, d, MLA_TILES[h + 5])
                    if h == 1:
                        take_mixed(2 * i, 12 * i + 6, bank[7][:, :])
                maxima(3, i)
                split_lo(dve, s + 8, d, TILES)
                normalize(3, i)
                gate_take(s + 7, d, (c + 9) % 2)
                gate_finish(2 * i + 1)
                take_mixed(2 * i + 1, 12 * i + 12, bank[7][:, :])
            leave_loop(2)

            def dil_maxima(g, i):
                dve.wait_ge(bias_loaded, 16 * GROUPS)
                for e in range(2):
                    dve.wait_ge(dil_scores, 2 * g + e + 6 * i + 1)
                    one, two = (bank[2], bank[3]) if e == 0 else (bank[4], bank[7])
                    head = bass.ds(2 * i + e, 1)

                    def biased(out, source, bias):
                        return nc.vector.scalar_tensor_tensor(out=out, in0=source, scalar=DIL_SCALE, in1=bias,
                                                              op0=ALU.mult, op1=ALU.add)

                    p = dil_p[:, e, :]
                    if g == 0:
                        biased(p[:, 0:P].rearrange("p (a n) -> p a n", a=1), one[:, 0:P].rearrange("p (a n) -> p a n", a=1),
                               bias0[:, head, P:2 * P])
                        biased(p[:, P:3 * P].rearrange("p (a n) -> p a n", a=1),
                               one[:, P:3 * P].rearrange("p (a n) -> p a n", a=1), bias0[:, head, :])
                        last = biased(p[:, 3 * P:7 * P].rearrange("p (a n) -> p a n", a=2),
                                      two[:, :].rearrange("p (a n) -> p a n", a=2),
                                      bias0[:, head, :].to_broadcast([P, 2, 2 * P]))
                        spans = ((0, p[:, 0:P].rearrange("p (a n) -> p a n", a=1)),
                                 (1, p[:, P:7 * P].rearrange("p (a n) -> p a n", a=3)))
                    else:
                        first = (3 + 4 * g) * P
                        view = p[:, first:first + SEQ].rearrange("p (a n) -> p a n", a=BLOCKS)
                        last = biased(view, one[:, :].rearrange("p (a n) -> p a n", a=BLOCKS),
                                      bias12[:, g - 1, head, :].to_broadcast([P, BLOCKS, P]))
                        spans = ((0, view),)
                    last.then_inc(dil_taken, 1)
                    dve.wait_ge(dil_taken, 2 * g + e + 6 * i + 1)
                    for b, view in spans:
                        last = nc.vector.tensor_reduce(stats[:, 0, g, min(g, 1), 2 * b + e:2 * (b + view.shape[1]) + e - 1:2],
                                                       view, AX.X, ALU.max, negate=True)
                    last.then_inc(dil_max, 1)

            def take_projection(out, s, d, parity):
                dve.wait_ge(piece_done, s + d + 1)
                nc.vector.tensor_tensor(out, bank[parity][:, :], rstd[:, :], ALU.mult).then_inc(chunk_taken, 1)

            def group_weights(i):
                dve.wait_ge(stats_moved, i + 1)
                moved = exchanged
                mod, div = const[:, C_MOD:C_MOD + BLOCKS], const[:, C_DIV:C_DIV + BLOCKS]
                for at, n, mask in ((0, 8, div), (64, 16, mod)):
                    size = n * 8
                    view = "p (r k e) -> p r k e"
                    nc.vector.tensor_tensor(
                        moved[:, at:at + size].rearrange(view, k=BLOCKS, e=2),
                        bank[7][:, at:at + size].rearrange(view, k=BLOCKS, e=2),
                        mask.rearrange("p (a k e) -> p a k e", a=1, e=1).to_broadcast([P, n, BLOCKS, 2]), ALU.mult).then_inc(own, one())
                dve.wait_ge(own, so_far())
                for t in range(2):
                    for e in range(2):
                        source = moved[:, 0:64].rearrange("p (a t k e) -> p t e a k", a=BLOCKS, t=2, e=2)[:, t, e]
                        nc.vector.tensor_reduce(stats[:, t, 0, 1, e:8:2], source, AX.X, ALU.add)
                        for g in (1, 2):
                            source = moved[:, 64:192].rearrange("p (b t g k e) -> p t g e b k", b=BLOCKS, t=2, g=2, e=2)
                            last = nc.vector.tensor_reduce(stats[:, t, g, 0, e:8:2], source[:, t, g - 1, e], AX.X, ALU.add)
                last.then_inc(own, one())
                dve.wait_ge(own, so_far())
                maxima_of = stats[:, 0, :, :, :].rearrange("p g o n -> p g (o n)")
                sums_of = stats[:, 1, :, :, :].rearrange("p g o n -> p g (o n)")
                nc.vector.tensor_tensor(neg_top[:, :], maxima_of[:, 0], maxima_of[:, 1], ALU.min).then_inc(own, one())
                dve.wait_ge(own, so_far())
                nc.vector.tensor_tensor(neg_top[:, :], neg_top[:, :], maxima_of[:, 2], ALU.min).then_inc(own, one())
                dve.wait_ge(own, so_far())
                top = neg_top[:, :].rearrange("p (a n) -> p a n", a=1).to_broadcast([P, GROUPS, 4 * BLOCKS])
                nc.vector.tensor_tensor(weight[:, :, :], top, maxima_of, ALU.subtract).then_inc(weight_ready, 1)
                dve.wait_ge(weight_exp, i + 1)
                parts = exchanged[:, 0:GROUPS * 4 * BLOCKS]
                nc.vector.tensor_tensor(parts.rearrange("p (g n) -> p g n", g=GROUPS), weight[:, :, :],
                                                    sums_of, ALU.mult).then_inc(own, one())
                dve.wait_ge(own, so_far())
                nc.vector.tensor_reduce(total[:, :], parts.rearrange("p (g n) -> p n g", g=GROUPS), AX.X, ALU.add).then_inc(own, one())
                dve.wait_ge(own, so_far())
                nc.vector.reciprocal(total[:, :], total[:, :]).then_inc(own, one())
                dve.wait_ge(own, so_far())
                inverse = total[:, :].rearrange("p (a n) -> p a n", a=1).to_broadcast([P, GROUPS, 4 * BLOCKS])
                nc.vector.tensor_tensor(weight[:, :, :], weight[:, :, :], inverse, ALU.mult).then_inc(own, one())
                dve.wait_ge(own, so_far())

            def scale_probs(e):
                for g, order, b, blocks, first, width in ((0, 0, 0, 1, 0, P), (0, 0, 1, 3, P, 2 * P),
                                                          (1, 1, 0, 4, 7 * P, P), (2, 1, 0, 4, 11 * P, P)):
                    view = dil_p[:, e, first:first + blocks * width].rearrange("p (b n) -> p b n", b=blocks)
                    at = 8 * order + 2 * b + e
                    by = weight[:, g, at:at + 2 * blocks - 1:2].rearrange("p (b n) -> p b n", n=1)
                    nc.vector.tensor_tensor(view, view, by.to_broadcast([P, blocks, width]), ALU.mult).then_inc(dil_scaled, 1)

            with dve.Fori(0, PAIRS) as i:
                enter_loop(i, 2 + 1 + 2 + 4 + 6)
                s, d, c = PIECES["dil"], 12 * i, CHUNKS["dil"]
                for q in range(12):
                    split_lo(dve, s + q + 1, d, TILES)
                    if q in (3, 5, 7):
                        dil_maxima(q // 2 - 1, i)
                    if q < 6:
                        out = (dil_q, dil_k)[q % 2][:, q // 2, :]
                    else:
                        out = dil_vt[:, q % 2, :]
                    if q < 9:
                        take_projection(out, s + q, d, (c + q) % 2)
                        continue
                    if q == 11:
                        group_weights(i)
                        scale_probs(0)
                        scale_probs(1)
                    gate_take(s + q, d, (c + q) % 2)
                    gate_finish(4 + 3 * i + q - 9)
                take_mixed(PAIRS + i, 3 * MLA_HEADS + 8 * i + 8, bank[2][:, :])
            leave_loop(PAIRS)

            for k in range(2 * PAIRS):
                dve.wait_ge(mixed_rounded, k + 1)
                nc.vector.tensor_tensor(act_lo[:, k, :], mixed[:, k, :], act_hi[:, k, :].bitcast(F32),
                                        ALU.subtract).then_inc(mixed_split, 1)
            with dve.Fori(0, KM // 4) as i:
                for q in range(4):
                    s, c = PIECES["merge"] + q, CHUNKS["merge"] + 2 * q
                    m = 4 * i + q
                    split_lo(dve, s + 1, 4 * i, TILES)
                    dve.wait_ge(inner_done, MLA_HEADS + q + 4 * i + 1)
                    nc.vector.tensor_tensor(work[:, 0:1, :], bank[0][:, :].rearrange("p (a n) -> p a n", a=1),
                                            gates[:, bass.ds(m, 1), :], ALU.mult).then_inc(chunk_taken, 1)
                    dve.wait_ge(piece_done, s + 4 * i + 1)
                    nc.vector.tensor_tensor(work[:, 1:2, :], bank[1][:, :].rearrange("p (a n) -> p a n", a=1),
                                            gates[:, bass.ds(m + KM, 1), :], ALU.mult).then_inc(chunk_taken, 1)
                    dve.wait_ge(chunk_taken, c + 8 * i + 2)
                    nc.vector.tensor_tensor(work[:, 2, :], work[:, 0, :], work[:, 1, :], ALU.add).then_inc(merge_ready, 1)
                    dve.wait_ge(merge_ready, q + 4 * i + 1)
                    dve.wait_ge(merged_rounded, q + 4 * i + 1)
                    nc.vector.tensor_tensor(merged_lo[:, bass.ds(m, 1), :], work[:, 2:3, :],
                                            merged_hi[:, bass.ds(m, 1), :].bitcast(F32), ALU.subtract).then_inc(merged_split, 1)
            clear_sums()
            with dve.Fori(0, KM // 4) as i:
                for q in range(4):
                    s, c = PIECES["out"] + q, CHUNKS["out"] + q
                    chunk = bass.ds(4 * i + q, 1)
                    split_lo(dve, s + 1, 4 * i, TILES)
                    dve.wait_ge(piece_done, s + 4 * i + 1)
                    nc.vector.tensor_tensor(x[:, chunk, :], bank[c % 2][:, :].rearrange("p (a n) -> p a n", a=1),
                                            x[:, chunk, :], ALU.add).then_inc(chunk_taken, 1)
                    dve.wait_ge(chunk_taken, c + 4 * i + 1)
                    split_chunk(4 * i + q + 2 * KM + KQ + KKV, x[:, chunk, :], gains[:, bass.ds(4 * i + q + G_FFN2, 1)],
                                act_hi[:, chunk, :], act_lo[:, chunk, :], sumsq[:, :], False)
            up_turn(1, 0, 0, first=True)
            with dve.Fori(0, KF // 2 - 1) as i:
                enter_loop(i, 2)
                up_turn(1, 1, i)
            leave_loop(KF // 2 - 1)
            clear_sums()
            down_turn(1, 0, 0, None, False)
            down_turn(1, 1, 0, None, True)
            reciprocal_root(5, rstd[:, :])
            for k in range(KM):
                nc.vector.scalar_tensor_tensor(out=x[:, k, :], in0=x[:, k, :], scalar=gains[:, G_FINAL + k:G_FINAL + k + 1],
                                               in1=rstd[:, :], op0=ALU.mult, op1=ALU.mult).then_inc(y_ready, 1)


def _tiles(w):
    k, n = w.shape
    return w.reshape(k // P, P, n // P, P).transpose(2, 1, 0, 3).reshape(n // P, P, k)


def _swapped(w):
    half = QK_ROPE // 2
    return np.concatenate([w, w[:, half:], w[:, :half]], axis=1)


def kernel(**inputs):
    import concourse.bacc as bacc
    from concourse.bass_utils import run_bass_kernel_spmd

    given = {k: np.asarray(v) for k, v in inputs.items()}
    arrays = {}

    def put(name, a):
        arrays[name] = np.ascontiguousarray(a)

    put("x_t", given["x"][0].T.reshape(KM, P, SEQ))
    put("positions", given["positions"])
    put("rel_bias", given["rel_bias"])
    columns = [given[n].reshape(-1, P).T for n in
               ("ffn1_norm", "mix_norm", "ffn2_norm", "norm_final", "q_norm", "kv_norm", "b_gate")]
    put("gains", np.concatenate(columns, axis=1))
    for name, a in zip(("tables", "onehot", "t5_masks"), shape_constants()):
        put(name, a)
    for f in ("ffn1", "ffn2"):
        for w in ("gate", "up", "down"):
            put(f"{f}_{w}", _tiles(given[f"{f}_w_{w}"][0]))
    w_in = given["w_in"][0]
    rotary = _swapped(w_in[:, IN_ROPE:IN_Q])
    put("w_latent", _tiles(np.concatenate([w_in[:, :IN_ROPE], rotary, rotary], axis=1)))
    gates = _tiles(w_in[:, IN_GATES:])
    put("w_mla_gates", gates[:4])
    pairs = []
    for pair in range(PAIRS):
        def heads(start, g):
            at = start + (g * GROUP_HEADS + 2 * pair) * HEAD_DIM
            return _tiles(w_in[:, at:at + 2 * HEAD_DIM])
        qk = [heads(start, g) for g in range(GROUPS) for start in (IN_Q, IN_K)]
        pairs.append(np.concatenate([*qk, *(heads(IN_V, g) for g in range(GROUPS)), gates[4 + 3 * pair:7 + 3 * pair]]))
    put("w_dil", np.stack(pairs))
    up_q = given["w_uq"][0].reshape(Q_LORA, MLA_HEADS, QK_DIM)
    up_kv = _tiles(given["w_ukv"][0])
    rows = []
    for h in range(MLA_HEADS):
        query = np.concatenate([up_q[:, h, :QK_NOPE], _swapped(up_q[:, h, QK_NOPE:])], axis=1)
        rows += [_tiles(query)[0], up_kv[h]]
    put("w_lora_up", np.stack([np.concatenate(rows[8 * n:8 * n + 8], axis=1) for n in range(2)]))
    put("w_branches", np.concatenate([_tiles(given["w_br_mla"][0]), _tiles(given["w_br_dil"][0])], axis=2))
    put("w_out", _tiles(given["w_out"][0]))

    nc = bacc.Bacc("TRN2", target_bir_lowering=False, num_devices=1)
    a = {n: nc.dram_tensor("in_" + n, v.shape, mybir.dt.from_np(v.dtype), kind="ExternalInput").ap() for n, v in arrays.items()}
    skew = nc.dram_tensor("skew", (GROUP_HEADS, P * (T5_END + 1)), F32, kind="Internal").ap()
    y_t = nc.dram_tensor("y_t", (KM, P, SEQ), F32, kind="ExternalOutput").ap()
    ffn = [[a[f"{f}_{w}"] for w in ("gate", "up", "down")] for f in ("ffn1", "ffn2")]
    decoder_layer(nc, a["x_t"], a["positions"], a["rel_bias"], a["gains"], a["tables"], a["onehot"], a["t5_masks"],
                  ffn, a["w_latent"], a["w_lora_up"], a["w_mla_gates"], a["w_dil"], a["w_branches"], a["w_out"],
                  skew, y_t)
    result = run_bass_kernel_spmd(nc, [{"in_" + n: v for n, v in arrays.items()}], core_ids=[0]).results[0]["y_t"]
    return np.ascontiguousarray(result.reshape(D_MODEL, SEQ).T).reshape(1, SEQ, D_MODEL)
```

```python
import math
from contextlib import ExitStack

import concourse.bass as bass
import numpy as np
from concourse import mybir

F32 = mybir.dt.float32
F32R = mybir.dt.float32r
I32 = mybir.dt.int32
ALU = mybir.AluOpType
ACT = mybir.ActivationFunctionType
AX = mybir.AxisListType

P = 128
SEQ = 512
BLOCKS = SEQ // P
D_MODEL = 1024
KM = D_MODEL // P
D_FF = 2816
KF = D_FF // P
EPS = 1e-6
MLA_HEADS, QK_NOPE, QK_ROPE, V_DIM = 8, 64, 32, 64
QK_DIM = QK_NOPE + QK_ROPE
Q_LORA, KV_LORA = 384, 256
KQ, KKV = Q_LORA // P, KV_LORA // P
ROPE_THETA = 10000.0
GROUPS, GROUP_HEADS, HEAD_DIM = 3, 8, 64
PAIRS = GROUP_HEADS // 2
DIL_QKV = GROUPS * GROUP_HEADS * HEAD_DIM
NUM_BUCKETS, MAX_DISTANCE = 32, 2048
STRIDES = (1, 4, 16)
NEG_INF = -1e30
MLA_SCALE = QK_DIM ** -0.5
DIL_SCALE = HEAD_DIM ** -0.5



def _few_bits(value, bits, parts):
    out = []
    for _ in range(parts - 1):
        unit = 2.0 ** (math.floor(math.log2(value)) + 1 - bits)
        out.append(math.floor(value / unit) * unit)
        value -= out[-1]
    return out + [value]


TWO_PI = _few_bits(2 * math.pi, 9, 4)

IN_KV = Q_LORA
IN_ROPE = IN_KV + KV_LORA
IN_Q = IN_ROPE + QK_ROPE
IN_K = IN_Q + DIL_QKV
IN_V = IN_K + DIL_QKV
IN_GATES = IN_V + DIL_QKV

TILES = 8
HALF = TILES // 2
RAW, SPLIT = 4, 2
DOWN_PARTS = ((0, 8), (8, 15), (15, 22))
LORA_TILES = KQ + KKV
PIECES = {}
CHUNKS = {}


def _lay_out_stream():
    n = c = 0
    for name, pieces, chunks in (
        ("up1", 2 * KF, 2 * KF), ("down1", 3 * KM, KM), ("latent", 6, 6), ("mla", 2 * MLA_HEADS, 3 * MLA_HEADS),
        ("dil", 12 * PAIRS, 11 * PAIRS), ("merge", KM, 2 * KM), ("out", KM, KM),
        ("up2", 2 * KF, 2 * KF), ("down2", 3 * KM, KM),
    ):
        PIECES[name], CHUNKS[name] = n, c
        n, c = n + pieces, c + chunks
    PIECES["end"], CHUNKS["end"] = n, c


_lay_out_stream()



def first_chunk(h):
    return CHUNKS["mla"] + max(3 * h, 1)


def gate_chunk(h):
    return CHUNKS["mla"] + 3 * h + 5


C_IDENT, C_ONES, C_EXPAND, C_FOLD = 0, P, 2 * P, 2 * P + SEQ
C_MOD = C_FOLD + SEQ
C_DIV = C_MOD + BLOCKS
C_CAUSAL = C_DIV + BLOCKS
C_FREQ = C_CAUSAL + P
C_TURN, C_PHASE, C_SIGN, C_EPS = C_FREQ + 1, C_FREQ + 2, C_FREQ + 3, C_FREQ + 4
C_END = C_FREQ + 5
G_FFN1, G_MIX, G_FFN2, G_FINAL, G_Q, G_KV = 0, KM, 2 * KM, 3 * KM, 4 * KM, 4 * KM + KQ
G_BIAS = G_KV + KKV
G_END = G_BIAS + 2 * KM
T5_LEN = (3 * P - 1, 2 * P - 1, 2 * P - 1)
T5_AT = (0, T5_LEN[0], T5_LEN[0] + T5_LEN[1])
T5_END = sum(T5_LEN)


def t5_bucket(distance):
    exact = NUM_BUCKETS // 2
    d = np.maximum(distance, 1).astype(np.float32)
    scaled = np.log(d / np.float32(exact)) / np.float32(math.log(MAX_DISTANCE / exact))
    large = exact + (scaled * np.float32(NUM_BUCKETS - exact)).astype(np.int32)
    return np.where(distance < exact, distance, np.minimum(large, NUM_BUCKETS - 1))


def shape_constants():
    c = np.zeros((P, C_END), np.float32)
    p = np.arange(P)
    j = np.arange(SEQ)
    c[:, C_IDENT:C_IDENT + P] = np.eye(P)
    c[:, C_ONES:C_ONES + P] = 1.0
    c[:, C_EXPAND:C_EXPAND + SEQ] = p[:, None] == j[None, :] // 4
    c[:, C_MOD:C_MOD + BLOCKS] = p[:, None] % 4 == np.arange(4)
    c[:, C_FOLD:C_FOLD + SEQ] = p[:, None] == (4 * (j % P) + j // P)[None, :] % P
    c[:, C_DIV:C_DIV + BLOCKS] = p[:, None] // 32 == np.arange(4)
    c[:, C_CAUSAL:C_CAUSAL + P] = np.where(p[None, :] <= p[:, None], 0.0, NEG_INF)
    freq = 1.0 / ROPE_THETA ** (np.arange(0, QK_ROPE, 2, dtype=np.float32) / np.float32(QK_ROPE))
    for row in range(QK_NOPE, P):
        c[row, C_FREQ] = freq.astype(np.float32)[row % 16]
        cosine = row < QK_DIM
        c[row, C_TURN] = 0.25 if cosine else 0.0
        c[row, C_PHASE] = math.pi / 2 if cosine else 0.0
        c[row, C_SIGN] = -1.0 if QK_DIM <= row < QK_DIM + 16 else 1.0
    c[:, C_EPS] = EPS
    onehot = np.zeros((NUM_BUCKETS, T5_END), np.float32)
    mask = np.full((GROUP_HEADS, T5_END), NEG_INF, np.float32)
    for g, stride in enumerate(STRIDES):
        apart = (T5_LEN[g] + 1) // 2 + (P // 2 if g == 0 else 0) - 1 - np.arange(T5_LEN[g])
        unit = 4 if g == 2 else 1
        ok = (apart >= 0) & (apart <= P) & (apart % unit == 0)
        bucket = t5_bucket(np.maximum(apart, 0) // unit * stride)
        at = T5_AT[g] + np.arange(T5_LEN[g])
        onehot[bucket[ok], at[ok]] = 1.0
        mask[:, at[ok]] = 0.0
    return c, onehot, mask


def decoder_layer(nc, x_t, positions, rel_bias, gains_in, tables, onehot_in, mask_in, ffn, w_latent, w_lora_up,
                  w_mla_gates, w_dil, w_branches, w_out, skew, y_t):
    ctx = ExitStack()
    held = []

    def sb(name, shape, dt=F32):
        return ctx.enter_context(nc.sbuf_tensor(name, shape, dt))

    def shared(name, shape, dt=F32):
        manager = nc.sbuf_tensor(name, shape, dt)
        held.append(manager)
        return manager.__enter__()

    def give_back(n):
        for _ in range(n):
            held.pop().__exit__(None, None, None)

    def sem(name):
        return ctx.enter_context(nc.semaphore(name))

    with ctx:
        x = sb("x", [P, KM, SEQ])
        act_hi = sb("act_hi", [P, KM, SEQ], F32R)
        act_lo = sb("act_lo", [P, KM, SEQ], F32R)
        raw = sb("raw", [P, RAW, TILES * P])
        w_hi = sb("w_hi", [P, SPLIT, TILES * P], F32R)
        w_lo = sb("w_lo", [P, SPLIT, TILES * P], F32R)
        const = sb("const", [P, C_END])
        gains = sb("gains", [P, G_END])
        half_bias = sb("half_bias", [P, 2 * KM])
        rstd = sb("rstd", [P, SEQ])
        sumsq = sb("sumsq", [P, SEQ])
        square = sb("square", [P, SEQ])
        work = sb("work", [P, 4, SEQ])
        rope = sb("rope", [P, SEQ])
        ident = const[:, C_IDENT:C_IDENT + P]
        ones = const[:, C_ONES:C_ONES + P]
        causal = const[:, C_CAUSAL:C_CAUSAL + P]

        stats = sb("stats", [P, 2, GROUPS, 2, 2 * BLOCKS])
        exchanged = work[:, 3, 0:6 * 4 * 2 * BLOCKS]
        weight = sb("weight", [P, GROUPS, 4 * BLOCKS])
        neg_top = sb("neg_top", [P, 4 * BLOCKS])
        total = sb("total", [P, 4 * BLOCKS])
        mla_stats = sb("mla_stats", [P, 4, BLOCKS])

        hid_hi = shared("hid_hi", [P, KF, SEQ], F32R)
        hid_lo = shared("hid_lo", [P, KF, SEQ], F32R)
        give_back(2)
        shared("hid_head", [P, KF + KF // 2, SEQ])
        position_i = shared("position_i", [P, SEQ], I32)
        angle = shared("angle", [P, SEQ])
        turns = shared("turns", [P, SEQ])
        t5_onehot = shared("t5_onehot", [NUM_BUCKETS, T5_END])
        t5_mask = shared("t5_mask", [GROUP_HEADS, T5_END])
        t5_row = shared("t5_row", [GROUP_HEADS, T5_END])
        t5_rel = shared("t5_rel", [NUM_BUCKETS, GROUPS * GROUP_HEADS])
        give_back(8)
        mixed = shared("mixed", [P, 2 * PAIRS, SEQ])
        gates = shared("gates", [P, 2 * KM, SEQ])
        probs_t = shared("probs_t", [P, 2, SEQ])
        lat_hi = shared("lat_hi", [P, KQ + KKV, SEQ], F32R)
        lat_lo = shared("lat_lo", [P, KQ + KKV, SEQ], F32R)
        sumsq_kv = shared("sumsq_kv", [P, SEQ])
        rstd_q = shared("rstd_q", [P, SEQ])
        rstd_kv = shared("rstd_kv", [P, SEQ])
        rope_q = shared("rope_q", [P, SEQ])
        rotated = shared("rotated", [P, SEQ])
        mla_q = shared("mla_q", [P, 2, SEQ])
        mla_k = shared("mla_k", [P, 2, SEQ])
        mla_vt = shared("mla_vt", [P, SEQ])
        mla_v = shared("mla_v", [P, BLOCKS, V_DIM])
        mla_p = shared("mla_p", [P, 10 * P])
        mask_ident = shared("mask_ident", [P, P], F32R)
        mask_causal = shared("mask_causal", [P, P], F32R)
        give_back(14)
        bias0 = shared("bias0", [P, GROUP_HEADS, 2 * P])
        bias12 = shared("bias12", [P, 2, GROUP_HEADS, P])
        dil_q = shared("dil_q", [P, GROUPS, SEQ])
        dil_k = shared("dil_k", [P, GROUPS, SEQ])
        dil_vt = shared("dil_vt", [P, 2, SEQ])
        dil_v = shared("dil_v", [P, GROUPS, BLOCKS, P])
        dil_p = shared("dil_p", [P, 2, 15 * P])
        give_back(7)
        merged_hi = shared("merged_hi", [P, KM, SEQ], F32R)
        merged_lo = shared("merged_lo", [P, KM, SEQ], F32R)
        give_back(2)
        give_back(3)
        bank = [ctx.enter_context(nc.psum_tensor(f"bank{i}", [P, SEQ], F32)) for i in range(8)]

        raw_loaded = [sem(f"raw_loaded{i}") for i in range(RAW)]
        hi_ready, lo_ready = sem("hi_ready"), sem("lo_ready")
        piece_done = sem("piece_done")
        inner_done, chunk_taken = sem("inner_done"), sem("chunk_taken")
        x_loaded = [sem(f"x_loaded{k}") for k in range(KM)]
        gains_loaded, scalars_loaded = sem("gains_loaded"), sem("scalars_loaded")
        position_loaded = sem("position_loaded")
        const_loaded, table_loaded = sem("const_loaded"), sem("table_loaded")
        act_rounded, act_split = sem("act_rounded"), sem("act_split")
        squared, sumsq_added = sem("squared"), sem("sumsq_added")
        norm_full, root_ready, rstd_ready = sem("norm_full"), sem("root_ready"), sem("rstd_ready")
        silu_ready, hid_rounded, hid_split = sem("silu_ready"), sem("hid_rounded"), sem("hid_split")
        setup_dve, setup_act, setup_pe = sem("setup_dve"), sem("setup_act"), sem("setup_pe")
        skew_stored, bias_loaded = sem("skew_stored"), sem("bias_loaded")
        own = sem("own")
        gate_ready = sem("gate_ready")
        head_ready, mask_ready = sem("head_ready"), sem("mask_ready")
        mla_scores, mla_max, mla_exp, mla_scaled = sem("mla_scores"), sem("mla_max"), sem("mla_exp"), sem("mla_scaled")
        turned, turned_taken, pv_done = sem("turned"), sem("turned_taken"), sem("pv_done")
        mixed_taken = sem("mixed_taken")
        dil_scores, dil_taken = sem("dil_scores"), sem("dil_taken")
        dil_max, dil_exp, dil_scaled = sem("dil_max"), sem("dil_exp"), sem("dil_scaled")
        v_turned, v_taken = sem("v_turned"), sem("v_taken")
        stats_moved, weight_ready, weight_exp = sem("stats_moved"), sem("weight_ready"), sem("weight_exp")
        mixed_rounded, mixed_split = sem("mixed_rounded"), sem("mixed_split")
        merge_ready, merged_rounded, merged_split = sem("merge_ready"), sem("merged_rounded"), sem("merged_split")
        y_ready, stored = sem("y_ready"), sem("stored")


        def load(sp, s, d, source, tiles):
            if s >= RAW:
                sp.wait_ge(lo_ready, s + d - (RAW - 1))
            sp.dma_start(raw[:, s % RAW, 0:tiles * P], source).then_inc(raw_loaded[s % RAW], 16)

        def split_hi(act, s, d, tiles):
            act.wait_ge(raw_loaded[s % RAW], 16 * (s // RAW + 1) + 16 // RAW * d)
            if s >= SPLIT:
                act.wait_ge(piece_done, s + d - (SPLIT - 1))
            nc.scalar.activation(w_hi[:, s % SPLIT, 0:tiles * P], raw[:, s % RAW, 0:tiles * P],
                                 ACT.Copy).then_inc(hi_ready, 1)

        def split_lo(dve, s, d, tiles):
            dve.wait_ge(hi_ready, s + d + 1)
            nc.vector.tensor_tensor(w_lo[:, s % SPLIT, 0:tiles * P], raw[:, s % RAW, 0:tiles * P],
                                    w_hi[:, s % SPLIT, 0:tiles * P].bitcast(F32),
                                    ALU.subtract).then_inc(lo_ready, 1)

        def multiply(s, tiles, out, hi, lo, start=True, stop=True, before=None):
            last = None
            for k, t in enumerate(tiles):
                if before is not None:
                    before(k)
                a = w_hi[:, s % SPLIT, t * P:(t + 1) * P]
                b = w_lo[:, s % SPLIT, t * P:(t + 1) * P]
                first, end = start and k == 0, stop and k == len(tiles) - 1
                nc.tensor.matmul(out, a, hi(k), start=first, stop=False)
                nc.tensor.matmul(out, a, lo(k), start=False, stop=False)
                last = nc.tensor.matmul(out, b, hi(k), start=False, stop=end)
            return last

        def free_chunk(pe, c):
            pe.wait_ge(chunk_taken, c - 1)

        block = ctx.enter_context(nc.Block())

        @block.sync
        def _(sp):
            def load_up_turn(f, turn, i):
                for q in range(4):
                    source = ffn[f][q % 2][bass.ds(2 * (turn + i) + q // 2, 1)]
                    load(sp, PIECES[f"up{f + 1}"] + 4 * turn + q, 4 * i, source.rearrange("a p n -> p (a n)"), TILES)

            def load_down(f):
                with sp.Fori(0, KM // 4) as i:
                    for m in range(4):
                        row = ffn[f][2][bass.ds(4 * i + m, 1)].rearrange("a p n -> p (a n)")
                        for part, (a, b) in enumerate(DOWN_PARTS):
                            load(sp, PIECES[f"down{f + 1}"] + 3 * m + part, 12 * i, row[:, a * P:b * P], b - a)

            def load_ffn(f):
                load_up_turn(f, 0, 0)
                with sp.Fori(0, KF // 2 - 1) as i:
                    load_up_turn(f, 1, i)
                load_down(f)

            load_ffn(0)
            for q in range(6):
                load(sp, PIECES["latent"] + q, 0, w_latent[q], TILES)
            s = PIECES["mla"]
            load(sp, s, 0, w_mla_gates[0], TILES)
            load(sp, s + 1, 0, w_lora_up[0], LORA_TILES)
            with sp.Fori(0, PAIRS - 1) as i:
                for h in range(2):
                    up, gate = (w[bass.ds(2 * i + h + 1, 1)].rearrange("a p n -> p (a n)") for w in (w_lora_up, w_mla_gates))
                    load(sp, s + 2 + 2 * h, 4 * i, up, LORA_TILES)
                    load(sp, s + 3 + 2 * h, 4 * i, gate, TILES)
            load(sp, s + 2 * MLA_HEADS - 2, 0, w_lora_up[MLA_HEADS - 1], LORA_TILES)
            load(sp, s + 2 * MLA_HEADS - 1, 0, w_mla_gates[MLA_HEADS - 1], TILES)
            with sp.Fori(0, PAIRS) as i:
                for q in range(10):
                    load(sp, PIECES["dil"] + q, 12 * i, w_dil[bass.ds(i, 1), q].rearrange("a p n -> p (a n)"), TILES)
                last_gate = w_dil[bass.ds(i, 1), 10].rearrange("a p n -> p (a n)")
                for part in range(2):
                    load(sp, PIECES["dil"] + 10 + part, 12 * i, last_gate[:, part * HALF * P:(part + 1) * HALF * P], HALF)
            for phase, source in (("merge", w_branches), ("out", w_out)):
                with sp.Fori(0, KM // 4) as i:
                    for q in range(4):
                        load(sp, PIECES[phase] + q, 4 * i, source[bass.ds(4 * i + q, 1)].rearrange("a p n -> p (a n)"), TILES)
            load_ffn(1)
            for k in range(KM):
                sp.wait_ge(y_ready, k + 1)
                sp.dma_start(y_t[k], x[:, k, :]).then_inc(stored, 16)
            sp.wait_ge(stored, 16 * KM)

        @block.gpsimd
        def _(pool):
            pool.dma_start(position_i[QK_NOPE:P, :], positions.to_broadcast([P - QK_NOPE, SEQ])).then_inc(position_loaded, 16)
            pool.dma_start(const[:, 0:C_FREQ], tables[:, 0:C_FREQ]).then_inc(const_loaded, 16)
            pool.dma_start(t5_onehot[:, :], onehot_in).then_inc(table_loaded, 16)
            pool.dma_start(t5_mask[:, :], mask_in).then_inc(table_loaded, 16)
            pool.dma_start(t5_rel[:, :], rel_bias).then_inc(table_loaded, 16)
            pool.wait_ge(setup_dve, 2)
            copies = skew.rearrange("h (p n) -> h p n", p=P)[:, :, 0:T5_END]
            row = t5_row[:, :].rearrange("h (a n) -> h a n", a=1).to_broadcast([GROUP_HEADS, P, T5_END])
            pool.dma_start(copies, row).then_inc(skew_stored, 16)
            pool.wait_ge(skew_stored, 16)
            pool.wait_ge(mixed_taken, PAIRS)
            for g, width in enumerate((2 * P, P, P)):
                source = bass.AP(skew.tensor, T5_AT[g] + P - 1,
                                 [[T5_END, P], [P * (T5_END + 1), GROUP_HEADS], [1, width]])
                table = bias0[:, :, :] if g == 0 else bias12[:, g - 1, :, :]
                pool.dma_start(table, source).then_inc(bias_loaded, 16)

        @block.tensor
        def _(pe):
            def norm(k, source, out):
                pe.wait_ge(const_loaded, 16)
                pe.wait_ge(sumsq_added, k)
                nc.tensor.matmul(out, ones, source, start=True, stop=True).then_inc(norm_full, 1)

            def up_turn(f, turn, i, first=False):
                for q in range(4):
                    s = PIECES[f"up{f + 1}"] + 4 * turn + q
                    c = CHUNKS[f"up{f + 1}"] + 4 * turn + q
                    if c >= 2:
                        free_chunk(pe, c + 4 * i)
                    pe.wait_ge(lo_ready, s + 4 * i + 1)

                    def act_chunk(k):
                        pe.wait_ge(act_split, (0, 2 * KM + KQ + KKV)[f] + k + 1)

                    multiply(s, range(TILES), bank[c % 2][:, :], lambda k: act_hi[:, k, :], lambda k: act_lo[:, k, :],
                             before=act_chunk if first and q == 0 else None).then_inc(piece_done, 1)
                    if first and q == 0:
                        norm((KM, 3 * KM + KQ + KKV)[f], sumsq[:, :], bank[7][:, :])
                    if first and f == 0 and q == 1:
                        pe.wait_ge(table_loaded, 48)
                        for g in range(GROUPS):
                            last = nc.tensor.matmul(bank[4 + g][0:GROUP_HEADS, 0:T5_LEN[g]],
                                                    t5_rel[:, g * GROUP_HEADS:(g + 1) * GROUP_HEADS],
                                                    t5_onehot[:, T5_AT[g]:T5_AT[g] + T5_LEN[g]], start=True, stop=True)
                        last.then_inc(setup_pe, 1)

            def down_turn(f, turn, i):
                for m in range(4):
                    c = CHUNKS[f"down{f + 1}"] + 4 * turn + m
                    free_chunk(pe, c + 4 * i)
                    for part, (a, b) in enumerate(DOWN_PARTS):
                        s = PIECES[f"down{f + 1}"] + 12 * turn + 3 * m + part
                        pe.wait_ge(lo_ready, s + 12 * i + 1)
                        pe.wait_ge(hid_split, KF * f + b)
                        multiply(s, range(b - a), bank[c % 2][:, :], lambda k: hid_hi[:, a + k, :],
                                 lambda k: hid_lo[:, a + k, :], start=part == 0, stop=part == 2).then_inc(piece_done, 1)

            def ffn_products(f):
                up_turn(f, 0, 0, first=True)
                with pe.Fori(0, KF // 2 - 1) as i:
                    up_turn(f, 1, i)
                with pe.Fori(0, 2) as i:
                    down_turn(f, 0, i)

            def project(s, d, c, bank_of, before=None):
                free_chunk(pe, c)
                pe.wait_ge(lo_ready, s + d + 1)
                multiply(s, range(TILES), bank_of, lambda k: act_hi[:, k, :], lambda k: act_lo[:, k, :],
                         before=before).then_inc(piece_done, 1)

            ffn_products(0)

            for q in range(6):
                c = CHUNKS["latent"] + q
                project(PIECES["latent"] + q, 0, c, bank[c % 2][:, :],
                        (lambda k: pe.wait_ge(act_split, KM + k + 1)) if q == 0 else None)
                if q == 0:
                    norm(2 * KM, sumsq[:, :], bank[7][:, :])
                if q == 4:
                    norm(2 * KM + KQ, sumsq[:, :], bank[7][:, :])
            norm(2 * KM + KQ + KKV, sumsq_kv[:, :], bank[4][:, :])

            def lora(s, d, h, i):
                pe.wait_ge(lo_ready, s + d + 1)
                c = first_chunk(h)
                for part, tiles in enumerate((range(KQ), range(KQ, LORA_TILES))):
                    free_chunk(pe, c + part + 6 * i)
                    base = tiles[0]
                    multiply(s, tiles, bank[(c + part) % 2][:, :], lambda k: lat_hi[:, base + k, :],
                             lambda k: lat_lo[:, base + k, :]).then_inc(piece_done if part else inner_done, 1)

            def turn_values(h, i):
                unit = 4 * h
                for b in range(BLOCKS):
                    last = nc.tensor.transpose(bank[5 + unit % 2][:, b * V_DIM:(b + 1) * V_DIM],
                                               mla_vt[QK_NOPE:P, b * P:(b + 1) * P], ident[QK_NOPE:P, QK_NOPE:P])
                last.then_inc(turned, 1)

            def score(h, i):
                pe.wait_ge(head_ready, h + 2 * i + 1)
                for b, (out, diagonal) in enumerate(((bank[2][:, 0:P], bank[2][:, 0:P]),
                                                     (bank[3][:, 0:2 * P], bank[3][:, P:2 * P]),
                                                     (bank[2][:, P:SEQ], bank[2][:, 3 * P:SEQ]),
                                                     (bank[4][:, :], bank[4][:, 3 * P:SEQ]))):
                    nc.tensor.matmul(out, mla_q[0:QK_DIM, h % 2, b * P:(b + 1) * P],
                                     mla_k[0:QK_DIM, h % 2, 0:(b + 1) * P], start=True, stop=False, skip_group_check=True)
                    last = nc.tensor.matmul(diagonal, mask_ident[:, :], mask_causal[:, :], start=False, stop=True,
                                            skip_group_check=True)
                last.then_inc(mla_scores, 1)

            def turn_probs(h, i, part):
                unit = 4 * h + 1 + part
                pe.wait_ge(mla_scaled, 4 * h + 8 * i + 4)
                pe.wait_ge(turned_taken, unit + 8 * i - (1 if part else 0))
                at = 0
                for key in ((0,), (1,), (2, 3))[part]:
                    for b in range(key, BLOCKS):
                        row = b * (b + 1) // 2 + key
                        last = nc.tensor.transpose(bank[5 + unit % 2][:, at:at + P], mla_p[:, row * P:(row + 1) * P], ident)
                        at += P
                last.then_inc(turned, 1)

            def attend(h, i, part):
                unit = 4 * h + 1 + part
                pe.wait_ge(turned_taken, unit + 8 * i + 1)
                row = V_DIM * (h % 2)
                at = 0
                for key in ((0,), (1,), (2, 3))[part]:
                    width = SEQ - key * P
                    last = nc.tensor.matmul(bank[7][row:row + V_DIM, key * P:SEQ], mla_v[:, key, :],
                                            probs_t[:, (3 * h + part) % 2, at:at + width],
                                            start=key == 0, stop=key == 3, skip_group_check=True)
                    at += width
                last.then_inc(pv_done, 1)

            def attention(h, i, s, d):
                score(h, i)
                turn_values(h, i)

                def turn_early(k):
                    if k == 6:
                        turn_probs(h, i, 0)
                        turn_probs(h, i, 1)

                if h < MLA_HEADS - 1:
                    lora(s, d, h + 1, i)
                    c = gate_chunk(h)
                    project(s + 1, d, c + 6 * i, bank[c % 2][:, :], turn_early)
                else:
                    turn_early(6)
                attend(h, i, 0)
                turn_probs(h, i, 2)
                attend(h, i, 1)
                attend(h, i, 2)

            s = PIECES["mla"]
            pe.wait_ge(mask_ready, 2)
            project(s, 0, CHUNKS["mla"], bank[CHUNKS["mla"] % 2][:, :])
            pe.wait_ge(act_split, 2 * KM + KQ + KKV)
            lora(s + 1, 0, 0, 0)
            with pe.Fori(0, PAIRS - 1) as i:
                attention(0, i, s + 2, 4 * i)
                attention(1, i, s + 4, 4 * i)
            attention(MLA_HEADS - 2, 0, s + 2 * MLA_HEADS - 2, 0)
            attention(MLA_HEADS - 1, 0, None, 0)

            def tokens(g, b):
                return slice(b * P, (b + 1) * P) if g == 0 else slice(b, SEQ, BLOCKS)

            def dil_score(g, i):
                for e in range(2):
                    unit = 2 * g + e
                    if unit >= 2:
                        pe.wait_ge(dil_taken, unit + 6 * i - 1)
                    rows = slice(HEAD_DIM * e, HEAD_DIM * (e + 1))
                    one, two = (bank[2], bank[3]) if e == 0 else (bank[4], bank[7])
                    for b in range(BLOCKS):
                        if g == 0:
                            out = (one[:, 0:P], one[:, P:3 * P], two[:, 0:2 * P], two[:, 2 * P:SEQ])[b]
                            keys = slice(max(b - 1, 0) * P, (b + 1) * P)
                        else:
                            out, keys = one[:, b * P:(b + 1) * P], tokens(g, b)
                        last = nc.tensor.matmul(out, dil_q[rows, g, tokens(g, b)], dil_k[rows, g, keys],
                                                start=True, stop=True, skip_group_check=True)
                    last.then_inc(dil_scores, 1)

            def turn_dil_values(g, i):
                if g:
                    pe.wait_ge(v_taken, g + 3 * i)
                for b in range(BLOCKS):
                    last = nc.tensor.transpose(bank[3][:, b * P:(b + 1) * P], dil_vt[:, g % 2, tokens(g, b)], ident)
                last.then_inc(v_turned, 1)

            def turn_dil(e, part, i):
                unit = 4 * e + part
                pe.wait_ge(turned_taken, 4 * MLA_HEADS + unit + 8 * i - 1)
                pe.wait_ge(dil_scaled, (4 * e + (2, 2, 3, 4)[part]) + 8 * i)
                if part < 2:
                    columns = [(0, P, 2 * P, 3 * P), (4 * P, 5 * P, 6 * P)][part]
                else:
                    columns = [(7 + 4 * (part - 2) + b) * P for b in range(BLOCKS)]
                for at, column in enumerate(columns):
                    last = nc.tensor.transpose(bank[5 + unit % 2][:, at * P:(at + 1) * P],
                                               dil_p[:, e, column:column + P], ident)
                last.then_inc(turned, 1)

            def attend_dil(e, part, i):
                unit = 4 * e + part
                pe.wait_ge(turned_taken, 4 * MLA_HEADS + unit + 8 * i + 1)
                rows = slice(HEAD_DIM * e, HEAD_DIM * (e + 1))
                pt = probs_t[:, unit % 2, :]
                if part < 2:
                    for n in range(2):
                        key = 2 * part + n
                        width = min(2 * P, SEQ - key * P)
                        last = nc.tensor.matmul(bank[2][rows, key * P:key * P + width], dil_v[:, 0, key, rows],
                                                pt[:, 2 * n * P:2 * n * P + width], start=key == 0, stop=False,
                                                skip_group_check=True)
                else:
                    for b in range(BLOCKS):
                        last = nc.tensor.matmul(bank[2][rows, b:SEQ:BLOCKS], dil_v[:, part - 1, b, rows],
                                                pt[:, b * P:(b + 1) * P], start=False,
                                                stop=part == 3 and b == BLOCKS - 1, skip_group_check=True)
                last.then_inc(pv_done, 1)

            with pe.Fori(0, PAIRS) as i:
                s, d, c, e = PIECES["dil"], 12 * i, CHUNKS["dil"], 11 * i

                def dil_project(q):
                    free_chunk(pe, c + e + max(q, 1))
                    pe.wait_ge(lo_ready, s + d + q + 1)
                    multiply(s + q, range(TILES), bank[(c + q) % 2][:, :], lambda k: act_hi[:, k, :],
                             lambda k: act_lo[:, k, :]).then_inc(piece_done, 1)

                def last_gate(part):
                    if part == 0:
                        free_chunk(pe, c + e + 10)
                    pe.wait_ge(lo_ready, s + d + 10 + part + 1)
                    base = part * HALF
                    multiply(s + 10 + part, range(HALF), bank[(c + 10) % 2][:, :], lambda k: act_hi[:, base + k, :],
                             lambda k: act_lo[:, base + k, :], start=part == 0, stop=part == 1).then_inc(piece_done, 1)

                dil_project(0)
                dil_project(1)
                dil_project(2)
                pe.wait_ge(mixed_taken, PAIRS + i)
                pe.wait_ge(chunk_taken, c + e + 2)
                dil_score(0, i)
                dil_project(3)
                dil_project(4)
                pe.wait_ge(chunk_taken, c + e + 4)
                dil_score(1, i)
                dil_project(5)
                dil_project(6)
                pe.wait_ge(chunk_taken, c + e + 6)
                dil_score(2, i)
                dil_project(7)
                pe.wait_ge(chunk_taken, c + e + 7)
                turn_dil_values(0, i)
                dil_project(8)
                pe.wait_ge(chunk_taken, c + e + 8)
                turn_dil_values(1, i)
                pe.wait_ge(dil_exp, 24 * i + 24)
                for b in range(BLOCKS):
                    nc.tensor.matmul(bank[7][:, b * 16:(b + 1) * 16], const[:, C_FOLD + b * P:C_FOLD + (b + 1) * P],
                                     stats[:, :, 0, 0, :], start=True, stop=True, skip_group_check=True)
                for b in range(BLOCKS):
                    last = nc.tensor.matmul(bank[7][:, 64 + b * 32:96 + b * 32],
                                            const[:, C_EXPAND + b * P:C_EXPAND + (b + 1) * P],
                                            stats[:, :, 1:3, 1, :], start=True, stop=True, skip_group_check=True)
                last.then_inc(stats_moved, 1)
                dil_project(9)
                pe.wait_ge(chunk_taken, c + e + 9)
                turn_dil_values(2, i)
                turn_dil(0, 0, i)
                turn_dil(0, 1, i)
                last_gate(0)
                pe.wait_ge(v_taken, 3 * i + 3)
                for unit in range(8):
                    attend_dil(unit // 4, unit % 4, i)
                    if unit < 6:
                        turn_dil((unit + 2) // 4, (unit + 2) % 4, i)
                    if unit == 3:
                        last_gate(1)

            with pe.Fori(0, KM // 4) as i:
                for q in range(4):
                    s, c = PIECES["merge"] + q, CHUNKS["merge"] + 2 * q
                    pe.wait_ge(lo_ready, s + 4 * i + 1)
                    for branch in range(2):
                        base = branch * PAIRS
                        free_chunk(pe, c + branch + 8 * i)
                        last = multiply(s, range(base, base + PAIRS), bank[branch][:, :], lambda k: act_hi[:, base + k, :],
                                        lambda k: act_lo[:, base + k, :],
                                        before=(lambda k: pe.wait_ge(mixed_split, base + k + 1)) if q == 0 else None)
                        last.then_inc(piece_done if branch else inner_done, 1)
            with pe.Fori(0, KM // 4) as i:
                for q in range(4):
                    s, c = PIECES["out"] + q, CHUNKS["out"] + q
                    free_chunk(pe, c + 4 * i)
                    pe.wait_ge(lo_ready, s + 4 * i + 1)
                    multiply(s, range(TILES), bank[c % 2][:, :], lambda k: merged_hi[:, k, :], lambda k: merged_lo[:, k, :],
                             before=(lambda k: pe.wait_ge(merged_split, k + 1)) if q == 0 else None).then_inc(piece_done, 1)
            ffn_products(1)
            norm(4 * KM + KQ + KKV, sumsq[:, :], bank[7][:, :])

        @block.scalar
        def _(act):
            act.dma_start(gains[:, :], gains_in).then_inc(gains_loaded, 16)
            act.dma_start(const[:, C_FREQ:C_END], tables[:, C_FREQ:C_END]).then_inc(scalars_loaded, 16)
            for k in range(KM):
                act.dma_start(x[:, k, :], x_t[k]).then_inc(x_loaded[k], 16)

            def round_chunk(k, source, gain, hi):
                if hi is not None:
                    act.wait_ge(gains_loaded, 16)
                    nc.scalar.activation(hi, source, ACT.Copy, scale=gain).then_inc(act_rounded, 1)
                act.wait_ge(gains_loaded, 16)
                if not isinstance(k, int) or k:
                    act.wait_ge(sumsq_added, k)
                nc.scalar.activation(square[:, :], source, ACT.Square).then_inc(squared, 1)

            def root(n, sums, features, out):
                act.wait_ge(scalars_loaded, 16)
                act.wait_ge(norm_full, n + 1)
                nc.scalar.activation(out, sums, ACT.Sqrt, bias=const[:, C_EPS:C_EPS + 1],
                                     scale=1.0 / features).then_inc(root_ready, 1)

            def up_turn(f, turn, i, first=False):
                for q in range(4):
                    s = PIECES[f"up{f + 1}"] + 4 * turn + q
                    c = CHUNKS[f"up{f + 1}"] + 4 * turn + q
                    split_hi(act, s + 1, 4 * i, TILES)
                    if first and q == 0:
                        root((0, 4)[f], bank[7][:, :], D_MODEL, square[:, :])
                    if first and f == 0 and q == 0:
                        act.wait_ge(setup_dve, 1)
                        nc.scalar.activation(rope[QK_NOPE:P, :], angle[QK_NOPE:P, :], ACT.Sin,
                                             scale=const[QK_NOPE:P, C_SIGN:C_SIGN + 1]).then_inc(setup_act, 1)
                    j = 2 * turn + q // 2
                    act.wait_ge(chunk_taken, c + 4 * i + 1)
                    act.wait_ge(gains_loaded, 16)
                    if q % 2 == 0:
                        nc.scalar.activation(work[:, 1, :], work[:, 0, :], ACT.Silu).then_inc(silu_ready, 1)
                    else:
                        nc.scalar.activation(hid_hi[:, bass.ds(2 * i + j, 1), :],
                                             work[:, 3:4, :], ACT.Copy).then_inc(hid_rounded, 1)

            def down_turn(f, turn, i, gain, final):
                for m in range(4):
                    for part in range(3):
                        s = PIECES[f"down{f + 1}"] + 12 * turn + 3 * m + part
                        if not (final and m == 3 and part == 2):
                            following = DOWN_PARTS[(part + 1) % 3]
                            split_hi(act, s + 1, 12 * i, following[1] - following[0])
                    act.wait_ge(chunk_taken, CHUNKS[f"down{f + 1}"] + 4 * turn + m + 4 * i + 1)
                    k = 4 * turn + m
                    chunk = bass.ds(4 * i + k, 1)
                    before = (KM, 3 * KM + KQ + KKV)[f]
                    if gain is None:
                        round_chunk(4 * i + k + before, x[:, chunk, :], None, None)
                    else:
                        round_chunk(4 * i + k + before, x[:, chunk, :], gains[:, bass.ds(4 * i + k + gain, 1)],
                                    act_hi[:, chunk, :])

            for k in range(KM):
                act.wait_ge(x_loaded[k], 16)
                round_chunk(k, x[:, k, :], gains[:, G_FFN1 + k:G_FFN1 + k + 1], act_hi[:, k, :])
                if k == 0:
                    split_hi(act, 0, 0, TILES)
            nc.scalar.mul(half_bias[:, :], gains[:, G_BIAS:G_BIAS + 2 * KM], 0.5).then_inc(setup_act, 1)
            up_turn(0, 0, 0, first=True)
            with act.Fori(0, KF // 2 - 1) as i:
                up_turn(0, 1, i)
            with act.Fori(0, 2) as i:
                down_turn(0, 0, i, G_MIX, False)

            for q in range(6):
                split_hi(act, PIECES["latent"] + q + 1, 0, TILES)
                if q == 0:
                    root(1, bank[7][:, :], D_MODEL, square[:, :])
                if q < 5:
                    act.wait_ge(chunk_taken, CHUNKS["latent"] + q + 1)
                    round_chunk(2 * KM + q, work[:, q % 2, :], gains[:, G_Q + q:G_Q + q + 1], lat_hi[:, q, :])
                if q == 0:
                    act.wait_ge(const_loaded, 16)
                    nc.scalar.copy(mask_ident[:, :], ident).then_inc(mask_ready, 1)
                    nc.scalar.copy(mask_causal[:, :], causal).then_inc(mask_ready, 1)
                if q == 4:
                    act.wait_ge(sumsq_added, 2 * KM + KQ + KKV)
                    root(2, bank[7][:, :], Q_LORA, square[:, :])
            root(3, bank[4][:, :], KV_LORA, sumsq_kv[:, :])

            def gate_tanh(c, k):
                act.wait_ge(chunk_taken, c + 1)
                act.wait_ge(setup_act, 1)
                nc.scalar.activation(gates[:, bass.ds(k, 1), :], work[:, 0:1, :], ACT.Tanh,
                                     bias=half_bias[:, bass.ds(k, 1)], scale=0.5).then_inc(gate_ready, 1)

            def take_values(h, i):
                act.wait_ge(turned, 4 * h + 8 * i + 1)
                nc.scalar.copy(mla_v[:, :, :].rearrange("p b n -> p (b n)"),
                               bank[5 + (4 * h) % 2][:, 0:BLOCKS * V_DIM]).then_inc(turned_taken, 1)

            def exponentials(h, i):
                for b, source in enumerate((bank[2][:, 0:P], bank[3][:, 0:2 * P], bank[2][:, P:SEQ], bank[4][:, :])):
                    if b == 0:
                        act.wait_ge(mla_max, h + 2 * i + 1)
                    row = b * (b + 1) // 2
                    nc.scalar.activation(mla_p[:, row * P:(row + b + 1) * P], source, ACT.Exp,
                                         bias=mla_stats[:, 1, b:b + 1], scale=MLA_SCALE,
                                         accum_out=mla_stats[:, 2, b:b + 1]).then_inc(mla_exp, 1)

            def take_probs(h, i):
                for part, width in enumerate((4 * P, 3 * P, 3 * P)):
                    unit = 4 * h + 1 + part
                    act.wait_ge(turned, unit + 8 * i + 1)
                    n = 3 * h + part
                    if n >= 2:
                        act.wait_ge(pv_done, n + 6 * i - 1)
                    nc.scalar.copy(probs_t[:, n % 2, 0:width], bank[5 + unit % 2][:, 0:width]).then_inc(turned_taken, 1)

            def attention(h, i, s, d, following):
                take_values(h, i)
                exponentials(h, i)
                if following[0]:
                    split_hi(act, s + 2, d, following[0])
                take_probs(h, i)
                if h < MLA_HEADS - 1:
                    gate_tanh(gate_chunk(h) + 6 * i, h + 1 + 2 * i)
                if following[1]:
                    split_hi(act, s + 3, d, following[1])

            s = PIECES["mla"]
            split_hi(act, s + 1, 0, LORA_TILES)
            split_hi(act, s + 2, 0, LORA_TILES)
            gate_tanh(CHUNKS["mla"], 0)
            split_hi(act, s + 3, 0, TILES)
            with act.Fori(0, PAIRS - 1) as i:
                attention(0, i, s + 2, 4 * i, (LORA_TILES, TILES))
                attention(1, i, s + 4, 4 * i, (LORA_TILES, TILES))
            attention(MLA_HEADS - 2, 0, s + 2 * MLA_HEADS - 2, 0, (TILES, 0))
            attention(MLA_HEADS - 1, 0, None, 0, (0, 0))

            def dil_exponentials(g, i):
                for e in range(2):
                    unit = 2 * g + e
                    act.wait_ge(dil_max, unit + 6 * i + 1)
                    for b in range(BLOCKS):
                        first, blocks = ((0, 1), (1, 2), (3, 2), (5, 2))[b] if g == 0 else (3 + 4 * g + b, 1)
                        p = dil_p[:, e, first * P:(first + blocks) * P]
                        order, at = min(g, 1), 2 * b + e
                        nc.scalar.activation(p, p, ACT.Exp, bias=stats[:, 0, g, order, at:at + 1],
                                             accum_out=stats[:, 1, g, order, at:at + 1]).then_inc(dil_exp, 1)

            def take_dil_values(g, i):
                act.wait_ge(v_turned, g + 3 * i + 1)
                nc.scalar.copy(dil_v[:, g, :, :].rearrange("p b n -> p (b n)"), bank[3][:, :]).then_inc(v_taken, 1)

            def take_dil_probs(unit, i):
                width = 3 * P if unit % 4 == 1 else SEQ
                act.wait_ge(turned, 4 * MLA_HEADS + unit + 8 * i + 1)
                act.wait_ge(pv_done, 3 * MLA_HEADS + unit + 8 * i - 1)
                nc.scalar.copy(probs_t[:, unit % 2, 0:width], bank[5 + unit % 2][:, 0:width]).then_inc(turned_taken, 1)

            with act.Fori(0, PAIRS) as i:
                s, d, c, e = PIECES["dil"], 12 * i, CHUNKS["dil"], 11 * i
                for q in range(10):
                    split_hi(act, s + q + 1, d, HALF if q == 9 else TILES)
                    if q in (3, 5, 7):
                        dil_exponentials(q // 2 - 1, i)
                    if q in (7, 8):
                        take_dil_values(q - 7, i)
                act.wait_ge(weight_ready, i + 1)
                nc.scalar.activation(weight[:, :, :], weight[:, :, :], ACT.Exp).then_inc(weight_exp, 1)
                take_dil_values(2, i)
                split_hi(act, s + 11, d, HALF)
                gate_tanh(c + e + 9, MLA_HEADS + 2 * i)
                for unit in range(8):
                    take_dil_probs(unit, i)
                    if unit == 4:
                        split_hi(act, s + 12, d, TILES)
                gate_tanh(c + e + 10, MLA_HEADS + 2 * i + 1)

            act.wait_ge(piece_done, PIECES["merge"])
            for k in range(2 * PAIRS):
                act.wait_ge(mixed_taken, k + 1)
                nc.scalar.copy(act_hi[:, k, :], mixed[:, k, :]).then_inc(mixed_rounded, 1)
            with act.Fori(0, KM // 4) as i:
                for q in range(4):
                    split_hi(act, PIECES["merge"] + q + 1, 4 * i, TILES)
                    act.wait_ge(merge_ready, q + 4 * i + 1)
                    act.wait_ge(gains_loaded, 16)
                    nc.scalar.copy(merged_hi[:, bass.ds(4 * i + q, 1), :], work[:, 2:3, :]).then_inc(merged_rounded, 1)
            for k in range(KM):
                split_hi(act, PIECES["out"] + k + 1, 0, TILES)
                act.wait_ge(chunk_taken, CHUNKS["out"] + k + 1)
                round_chunk(2 * KM + KQ + KKV + k, x[:, k, :], gains[:, G_FFN2 + k:G_FFN2 + k + 1], act_hi[:, k, :])
            up_turn(1, 0, 0, first=True)
            with act.Fori(0, KF // 2 - 1) as i:
                up_turn(1, 1, i)
            down_turn(1, 0, 0, None, False)
            down_turn(1, 1, 0, None, True)
            root(5, bank[7][:, :], D_MODEL, square[:, :])

        @block.vector
        def _(dve):
            count = {"before": 0, "turn": 0, "earlier": 0, "per": 0}

            def one():
                count["turn"] += 1
                return 1

            def so_far():
                return count["before"] + count["turn"] + count["earlier"]

            def enter_loop(i, per):
                count.update(before=count["before"] + count["turn"], turn=0, earlier=i * per, per=per)

            def leave_loop(turns):
                assert count["turn"] == count["per"], count
                count.update(before=count["before"] + turns * count["per"], turn=0, earlier=0)

            def split_chunk(k, source, gain, hi, lo, sums, first):
                if lo is not None:
                    dve.wait_ge(act_rounded, k + 1)
                    nc.vector.scalar_tensor_tensor(out=lo, in0=source, scalar=gain, in1=hi.bitcast(F32),
                                                   op0=ALU.mult, op1=ALU.subtract).then_inc(act_split, 1)
                dve.wait_ge(squared, k + 1)
                if first:
                    nc.vector.tensor_copy(sums, square[:, :]).then_inc(sumsq_added, 1)
                else:
                    dve.wait_ge(sumsq_added, k)
                    nc.vector.tensor_tensor(sums, sums, square[:, :], ALU.add).then_inc(sumsq_added, 1)

            def reciprocal_root(n, root, out):
                dve.wait_ge(root_ready, n + 1)
                nc.vector.reciprocal(out, root).then_inc(rstd_ready, 1)
                dve.wait_ge(rstd_ready, n + 1)

            def rotation_angles():
                dve.wait_ge(position_loaded, 16)
                dve.wait_ge(scalars_loaded, 16)
                rows = slice(QK_NOPE, P)
                a, n = angle[rows, :], turns[rows, :]
                nc.vector.tensor_copy(n, position_i[rows, :]).then_inc(own, one())
                dve.wait_ge(own, so_far())
                nc.vector.tensor_scalar(a, n, const[rows, C_FREQ:C_FREQ + 1], None, ALU.mult).then_inc(own, one())
                dve.wait_ge(own, so_far())
                nc.vector.tensor_scalar(n, a, 1.0 / (2 * math.pi), const[rows, C_TURN:C_TURN + 1],
                                                    ALU.mult, ALU.add).then_inc(own, one())
                for magic in (1.5 * 2 ** 23, -1.5 * 2 ** 23):
                    dve.wait_ge(own, so_far())
                    nc.vector.tensor_scalar(n, n, magic, None, ALU.add).then_inc(own, one())
                for part in TWO_PI:
                    dve.wait_ge(own, so_far())
                    nc.vector.scalar_tensor_tensor(out=a, in0=n, scalar=-part, in1=a,
                                                               op0=ALU.mult, op1=ALU.add).then_inc(own, one())
                dve.wait_ge(own, so_far())
                nc.vector.tensor_scalar(a, a, const[rows, C_PHASE:C_PHASE + 1], None, ALU.add).then_inc(own, one())
                dve.wait_ge(own, so_far())
                nc.vector.tensor_scalar(a, a, 3.1415925, -3.1415925, ALU.min, ALU.max).then_inc(setup_dve, 1)

            def bias_rows():
                dve.wait_ge(setup_pe, 1)
                for g in range(GROUPS):
                    at = slice(T5_AT[g], T5_AT[g] + T5_LEN[g])
                    last = nc.vector.tensor_tensor(t5_row[:, at], bank[4 + g][0:GROUP_HEADS, 0:T5_LEN[g]],
                                                   t5_mask[:, at], ALU.add)
                last.then_inc(setup_dve, 1)

            def up_turn(f, turn, i, first=False):
                for q in range(4):
                    s = PIECES[f"up{f + 1}"] + 4 * turn + q
                    j = 2 * turn + q // 2
                    hidden = KF * f + j
                    split_lo(dve, s + 1, 4 * i, TILES)
                    if first and q == 0:
                        reciprocal_root((0, 4)[f], square[:, :], rstd[:, :])
                    if q % 2 == 0:
                        dve.wait_ge(piece_done, s + 4 * i + 1)
                        nc.vector.tensor_tensor(work[:, 0, :], bank[s % 2][:, :], rstd[:, :], ALU.mult).then_inc(chunk_taken, 1)
                    else:
                        dve.wait_ge(silu_ready, hidden + 2 * i + 1)
                        nc.vector.tensor_tensor(work[:, 2, :], work[:, 1, :], rstd[:, :], ALU.mult).then_inc(own, one())
                        dve.wait_ge(piece_done, s + 4 * i + 1)
                        dve.wait_ge(own, so_far())
                        nc.vector.tensor_tensor(work[:, 3, :], bank[s % 2][:, :], work[:, 2, :], ALU.mult).then_inc(chunk_taken, 1)
                        chunk = bass.ds(2 * i + j, 1)
                        dve.wait_ge(chunk_taken, CHUNKS[f"up{f + 1}"] + 4 * turn + q + 4 * i + 1)
                        dve.wait_ge(hid_rounded, hidden + 2 * i + 1)
                        nc.vector.tensor_tensor(hid_lo[:, chunk, :], work[:, 3:4, :], hid_hi[:, chunk, :].bitcast(F32),
                                                ALU.subtract).then_inc(hid_split, 1)
                    if first and f == 0 and q == 2:
                        bias_rows()

            def down_turn(f, turn, i, gain, final):
                for m in range(4):
                    for part in range(3):
                        s = PIECES[f"down{f + 1}"] + 12 * turn + 3 * m + part
                        if not (final and m == 3 and part == 2):
                            following = DOWN_PARTS[(part + 1) % 3]
                            split_lo(dve, s + 1, 12 * i, following[1] - following[0])
                    c = CHUNKS[f"down{f + 1}"] + 4 * turn + m
                    k = 4 * turn + m
                    chunk = bass.ds(4 * i + k, 1)
                    dve.wait_ge(piece_done, s + 12 * i + 1)
                    nc.vector.scalar_tensor_tensor(out=x[:, chunk, :], in0=bank[c % 2][:, :].rearrange("p (a n) -> p a n", a=1),
                                                   scalar=0.5, in1=x[:, chunk, :],
                                                   op0=ALU.mult, op1=ALU.add).then_inc(chunk_taken, 1)
                    dve.wait_ge(chunk_taken, c + 4 * i + 1)
                    before = (KM, 3 * KM + KQ + KKV)[f]
                    hi, lo, g = None, None, None
                    if gain is not None:
                        hi, lo, g = act_hi[:, chunk, :], act_lo[:, chunk, :], gains[:, bass.ds(4 * i + k + gain, 1)]
                    split_chunk(4 * i + k + before, x[:, chunk, :], g, hi, lo, sumsq[:, :], False)

            def clear_sums():
                nc.vector.memset(sumsq[:, :], 0.0).then_inc(own, one())
                dve.wait_ge(own, so_far())

            def gate_take(p, parity, before):
                dve.wait_ge(piece_done, p)
                if before is not None:
                    dve.wait_ge(gate_ready, before)
                nc.vector.tensor_tensor(work[:, 0, :], bank[parity][:, :], rstd[:, :], ALU.mult).then_inc(chunk_taken, 1)

            rotation_angles()
            for k in range(KM):
                split_chunk(k, x[:, k, :], gains[:, G_FFN1 + k:G_FFN1 + k + 1], act_hi[:, k, :], act_lo[:, k, :],
                            sumsq[:, :], k == 0)
                if k == 0:
                    split_lo(dve, 0, 0, TILES)
            up_turn(0, 0, 0, first=True)
            dve.wait_ge(skew_stored, 16)
            dve.wait_ge(setup_act, 2)
            with dve.Fori(0, KF // 2 - 1) as i:
                enter_loop(i, 2)
                up_turn(0, 1, i)
            leave_loop(KF // 2 - 1)
            clear_sums()
            with dve.Fori(0, 2) as i:
                down_turn(0, 0, i, G_MIX, False)

            for q in range(6):
                s, c = PIECES["latent"] + q, CHUNKS["latent"] + q
                split_lo(dve, s + 1, 0, TILES)
                if q == 0:
                    reciprocal_root(1, square[:, :], rstd[:, :])
                if q == 5:
                    reciprocal_root(2, square[:, :], rstd_q[:, :])
                dve.wait_ge(piece_done, s + 1)
                if q < 5:
                    latent = work[:, q % 2, :]
                    nc.vector.tensor_tensor(latent, bank[c % 2][:, :], rstd[:, :], ALU.mult).then_inc(chunk_taken, 1)
                    dve.wait_ge(chunk_taken, c + 1)
                    split_chunk(2 * KM + q, latent, gains[:, G_Q + q:G_Q + q + 1], lat_hi[:, q, :], lat_lo[:, q, :],
                                sumsq[:, :] if q < KQ else sumsq_kv[:, :], q in (0, KQ))
                else:
                    low, high = slice(QK_NOPE, QK_DIM), slice(QK_DIM, P)
                    nc.vector.tensor_tensor(work[low, 2, :], rope[low, :], rstd[low, :], ALU.mult).then_inc(own, one())
                    nc.vector.tensor_tensor(work[high, 2, :], rope[high, :], rstd[high, :], ALU.mult).then_inc(own, one())
                    dve.wait_ge(own, so_far())
                    nc.vector.tensor_tensor(mla_k[low, 0, :], bank[c % 2][low, :], work[low, 2, :], ALU.mult).then_inc(own, one())
                    nc.vector.tensor_tensor(rotated[low, :], bank[c % 2][high, :], work[high, 2, :], ALU.mult)\
                      .then_inc(chunk_taken, 1)
                    dve.wait_ge(chunk_taken, c + 1)
                    dve.wait_ge(own, so_far())
                    nc.vector.tensor_tensor(mla_k[low, 0, :], mla_k[low, 0, :], rotated[low, :], ALU.add).then_inc(own, one())
                    dve.wait_ge(own, so_far())
                    nc.vector.tensor_copy(mla_k[low, 1, :], mla_k[low, 0, :]).then_inc(own, one())
            nc.vector.tensor_tensor(rope_q[QK_NOPE:P, :], rope[QK_NOPE:P, :], rstd_q[QK_NOPE:P, :], ALU.mult).then_inc(own, one())
            reciprocal_root(3, sumsq_kv[:, :], rstd_kv[:, :])
            dve.wait_ge(own, so_far())

            def take_query(h, i, parity):
                low, high = slice(QK_NOPE, QK_DIM), slice(QK_DIM, P)
                out = mla_q[:, h % 2, :]
                nc.vector.tensor_tensor(out[0:QK_NOPE, :], bank[parity][0:QK_NOPE, :], rstd_q[0:QK_NOPE, :], ALU.mult)
                nc.vector.tensor_tensor(out[low, :], bank[parity][low, :], rope_q[low, :], ALU.mult)
                if h:
                    dve.wait_ge(head_ready, h + 2 * i)
                nc.vector.tensor_tensor(rotated[low, :], bank[parity][high, :], rope_q[high, :], ALU.mult)\
                  .then_inc(chunk_taken, 1)

            def add_rotated(h, c):
                low = slice(QK_NOPE, QK_DIM)
                dve.wait_ge(chunk_taken, c)
                out = mla_q[low, h % 2, :]
                nc.vector.tensor_tensor(out, out, rotated[low, :], ALU.add).then_inc(head_ready, 1)

            def take_key_value(h, parity):
                nc.vector.tensor_tensor(mla_k[0:QK_NOPE, h % 2, :], bank[parity][0:QK_NOPE, :], rstd_kv[0:QK_NOPE, :], ALU.mult)
                nc.vector.tensor_tensor(mla_vt[QK_NOPE:P, :], bank[parity][QK_NOPE:P, :], rstd_kv[QK_NOPE:P, :], ALU.mult)\
                  .then_inc(chunk_taken, 1)

            def maxima(h, i):
                dve.wait_ge(mla_scores, h + 2 * i + 1)
                for b, source in enumerate((bank[2][:, 0:P], bank[3][:, 0:2 * P], bank[2][:, P:SEQ], bank[4][:, :])):
                    last = nc.vector.tensor_reduce(mla_stats[:, 0, b:b + 1], source, AX.X, ALU.max)
                last.then_inc(own, one())
                dve.wait_ge(own, so_far())
                nc.vector.tensor_scalar(mla_stats[:, 1, :], mla_stats[:, 0, :], -MLA_SCALE, None, ALU.mult).then_inc(mla_max, 1)

            def normalize(h, i):
                dve.wait_ge(mla_exp, 4 * h + 8 * i + 4)
                nc.vector.reciprocal(mla_stats[:, 3, :], mla_stats[:, 2, :]).then_inc(own, one())
                dve.wait_ge(own, so_far())
                for b in range(BLOCKS):
                    row = b * (b + 1) // 2
                    p = mla_p[:, row * P:(row + b + 1) * P]
                    nc.vector.tensor_scalar(p, p, mla_stats[:, 3, b:b + 1], None, ALU.mult).then_inc(mla_scaled, 1)

            def take_mixed(k, units, source):
                dve.wait_ge(pv_done, units)
                nc.vector.tensor_copy(mixed[:, bass.ds(k, 1), :], source.rearrange("p (a n) -> p a n", a=1)).then_inc(mixed_taken, 1)

            def take_lora(s, d, h, i, between=None):
                c = first_chunk(h)
                dve.wait_ge(inner_done, h + 2 * i + 1)
                take_query(h, i, c % 2)
                if between is not None:
                    between()
                dve.wait_ge(piece_done, s + d + 1)
                take_key_value(h, (c + 1) % 2)
                add_rotated(h, c + 6 * i + 2)

            def attention(h, i, s, d, following):
                maxima(h, i)
                if h < MLA_HEADS - 1:
                    take_lora(s, d, h + 1, i, lambda: normalize(h, i))
                    split_lo(dve, s + 2, d, following[0])
                    gate_take(s + d + 2, gate_chunk(h) % 2, h + 1 + 2 * i)
                    if following[1]:
                        split_lo(dve, s + 3, d, following[1])
                else:
                    normalize(h, i)
                if h % 2:
                    take_mixed(h // 2 + i, 3 * h + 3 + 6 * i, bank[7][:, :])

            s = PIECES["mla"]
            split_lo(dve, s + 1, 0, LORA_TILES)
            gate_take(s + 1, CHUNKS["mla"] % 2, None)
            take_lora(s + 1, 0, 0, 0)
            split_lo(dve, s + 2, 0, LORA_TILES)
            split_lo(dve, s + 3, 0, TILES)
            with dve.Fori(0, PAIRS - 1) as i:
                enter_loop(i, 2 * 2)
                attention(0, i, s + 2, 4 * i, (LORA_TILES, TILES))
                attention(1, i, s + 4, 4 * i, (LORA_TILES, TILES))
            leave_loop(PAIRS - 1)
            attention(MLA_HEADS - 2, 0, s + 2 * MLA_HEADS - 2, 0, (TILES, 0))
            attention(MLA_HEADS - 1, 0, None, 0, (0, 0))

            def dil_maxima(g, i):
                dve.wait_ge(bias_loaded, 16 * GROUPS)
                for e in range(2):
                    dve.wait_ge(dil_scores, 2 * g + e + 6 * i + 1)
                    one, two = (bank[2], bank[3]) if e == 0 else (bank[4], bank[7])
                    head = bass.ds(2 * i + e, 1)

                    def biased(out, source, bias):
                        return nc.vector.scalar_tensor_tensor(out=out, in0=source, scalar=DIL_SCALE, in1=bias,
                                                              op0=ALU.mult, op1=ALU.add)

                    p = dil_p[:, e, :]
                    if g == 0:
                        biased(p[:, 0:P].rearrange("p (a n) -> p a n", a=1), one[:, 0:P].rearrange("p (a n) -> p a n", a=1),
                               bias0[:, head, P:2 * P])
                        biased(p[:, P:3 * P].rearrange("p (a n) -> p a n", a=1),
                               one[:, P:3 * P].rearrange("p (a n) -> p a n", a=1), bias0[:, head, :])
                        last = biased(p[:, 3 * P:7 * P].rearrange("p (a n) -> p a n", a=2),
                                      two[:, :].rearrange("p (a n) -> p a n", a=2),
                                      bias0[:, head, :].to_broadcast([P, 2, 2 * P]))
                        spans = ((0, p[:, 0:P].rearrange("p (a n) -> p a n", a=1)),
                                 (1, p[:, P:7 * P].rearrange("p (a n) -> p a n", a=3)))
                    else:
                        first = (3 + 4 * g) * P
                        view = p[:, first:first + SEQ].rearrange("p (a n) -> p a n", a=BLOCKS)
                        last = biased(view, one[:, :].rearrange("p (a n) -> p a n", a=BLOCKS),
                                      bias12[:, g - 1, head, :].to_broadcast([P, BLOCKS, P]))
                        spans = ((0, view),)
                    last.then_inc(dil_taken, 1)
                    dve.wait_ge(dil_taken, 2 * g + e + 6 * i + 1)
                    for b, view in spans:
                        last = nc.vector.tensor_reduce(stats[:, 0, g, min(g, 1), 2 * b + e:2 * (b + view.shape[1]) + e - 1:2],
                                                       view, AX.X, ALU.max, negate=True)
                    last.then_inc(dil_max, 1)

            def take_projection(out, s, d, parity):
                dve.wait_ge(piece_done, s + d + 1)
                nc.vector.tensor_tensor(out, bank[parity][:, :], rstd[:, :], ALU.mult).then_inc(chunk_taken, 1)

            def group_weights(i):
                dve.wait_ge(stats_moved, i + 1)
                moved = exchanged
                mod, div = const[:, C_MOD:C_MOD + BLOCKS], const[:, C_DIV:C_DIV + BLOCKS]
                for at, n, mask in ((0, 8, div), (64, 16, mod)):
                    size = n * 8
                    view = "p (r k e) -> p r k e"
                    nc.vector.tensor_tensor(
                        moved[:, at:at + size].rearrange(view, k=BLOCKS, e=2),
                        bank[7][:, at:at + size].rearrange(view, k=BLOCKS, e=2),
                        mask.rearrange("p (a k e) -> p a k e", a=1, e=1).to_broadcast([P, n, BLOCKS, 2]), ALU.mult).then_inc(own, one())
                dve.wait_ge(own, so_far())
                for t in range(2):
                    for e in range(2):
                        source = moved[:, 0:64].rearrange("p (a t k e) -> p t e a k", a=BLOCKS, t=2, e=2)[:, t, e]
                        nc.vector.tensor_reduce(stats[:, t, 0, 1, e:8:2], source, AX.X, ALU.add)
                        for g in (1, 2):
                            source = moved[:, 64:192].rearrange("p (b t g k e) -> p t g e b k", b=BLOCKS, t=2, g=2, e=2)
                            last = nc.vector.tensor_reduce(stats[:, t, g, 0, e:8:2], source[:, t, g - 1, e], AX.X, ALU.add)
                last.then_inc(own, one())
                dve.wait_ge(own, so_far())
                maxima_of = stats[:, 0, :, :, :].rearrange("p g o n -> p g (o n)")
                sums_of = stats[:, 1, :, :, :].rearrange("p g o n -> p g (o n)")
                nc.vector.tensor_tensor(neg_top[:, :], maxima_of[:, 0], maxima_of[:, 1], ALU.min).then_inc(own, one())
                dve.wait_ge(own, so_far())
                nc.vector.tensor_tensor(neg_top[:, :], neg_top[:, :], maxima_of[:, 2], ALU.min).then_inc(own, one())
                dve.wait_ge(own, so_far())
                top = neg_top[:, :].rearrange("p (a n) -> p a n", a=1).to_broadcast([P, GROUPS, 4 * BLOCKS])
                nc.vector.tensor_tensor(weight[:, :, :], top, maxima_of, ALU.subtract).then_inc(weight_ready, 1)
                dve.wait_ge(weight_exp, i + 1)
                parts = exchanged[:, 0:GROUPS * 4 * BLOCKS]
                nc.vector.tensor_tensor(parts.rearrange("p (g n) -> p g n", g=GROUPS), weight[:, :, :],
                                                    sums_of, ALU.mult).then_inc(own, one())
                dve.wait_ge(own, so_far())
                nc.vector.tensor_reduce(total[:, :], parts.rearrange("p (g n) -> p n g", g=GROUPS), AX.X, ALU.add).then_inc(own, one())
                dve.wait_ge(own, so_far())
                nc.vector.reciprocal(total[:, :], total[:, :]).then_inc(own, one())
                dve.wait_ge(own, so_far())
                inverse = total[:, :].rearrange("p (a n) -> p a n", a=1).to_broadcast([P, GROUPS, 4 * BLOCKS])
                nc.vector.tensor_tensor(weight[:, :, :], weight[:, :, :], inverse, ALU.mult).then_inc(own, one())
                dve.wait_ge(own, so_far())

            def scale_probs(e):
                for g, order, b, blocks, first, width in ((0, 0, 0, 1, 0, P), (0, 0, 1, 3, P, 2 * P),
                                                          (1, 1, 0, 4, 7 * P, P), (2, 1, 0, 4, 11 * P, P)):
                    view = dil_p[:, e, first:first + blocks * width].rearrange("p (b n) -> p b n", b=blocks)
                    at = 8 * order + 2 * b + e
                    by = weight[:, g, at:at + 2 * blocks - 1:2].rearrange("p (b n) -> p b n", n=1)
                    nc.vector.tensor_tensor(view, view, by.to_broadcast([P, blocks, width]), ALU.mult).then_inc(dil_scaled, 1)

            with dve.Fori(0, PAIRS) as i:
                enter_loop(i, 2 + 1 + 2 + 4)
                s, d, c, e = PIECES["dil"], 12 * i, CHUNKS["dil"], 11 * i
                for q in range(12):
                    tiles = HALF if q in (9, 10) else TILES
                    split_lo(dve, s + q + 1, d, tiles)
                    if q in (3, 5, 7):
                        dil_maxima(q // 2 - 1, i)
                    if q < 6:
                        out = (dil_q, dil_k)[q % 2][:, q // 2, :]
                    else:
                        out = dil_vt[:, q % 2, :]
                    if q < 9:
                        take_projection(out, s + q, d, (c + q) % 2)
                    if q == 9:
                        group_weights(i)
                        scale_probs(0)
                        gate_take(s + d + 10, (c + 9) % 2, MLA_HEADS + 2 * i)
                        scale_probs(1)
                gate_take(s + d + 12, (c + 10) % 2, MLA_HEADS + 2 * i + 1)
                take_mixed(PAIRS + i, 3 * MLA_HEADS + 8 * i + 8, bank[2][:, :])
            leave_loop(PAIRS)

            for k in range(2 * PAIRS):
                dve.wait_ge(mixed_rounded, k + 1)
                nc.vector.tensor_tensor(act_lo[:, k, :], mixed[:, k, :], act_hi[:, k, :].bitcast(F32),
                                        ALU.subtract).then_inc(mixed_split, 1)
            with dve.Fori(0, KM // 4) as i:
                for q in range(4):
                    s, c = PIECES["merge"] + q, CHUNKS["merge"] + 2 * q
                    m = 4 * i + q
                    split_lo(dve, s + 1, 4 * i, TILES)
                    dve.wait_ge(inner_done, MLA_HEADS + q + 4 * i + 1)
                    nc.vector.scalar_tensor_tensor(out=work[:, 0:1, :], in0=gates[:, bass.ds(m, 1), :], scalar=1.0,
                                                   in1=bank[0][:, :].rearrange("p (a n) -> p a n", a=1),
                                                   op0=ALU.add, op1=ALU.mult).then_inc(chunk_taken, 1)
                    dve.wait_ge(piece_done, s + 4 * i + 1)
                    nc.vector.scalar_tensor_tensor(out=work[:, 1:2, :], in0=gates[:, bass.ds(m + KM, 1), :], scalar=1.0,
                                                   in1=bank[1][:, :].rearrange("p (a n) -> p a n", a=1),
                                                   op0=ALU.add, op1=ALU.mult).then_inc(chunk_taken, 1)
                    dve.wait_ge(chunk_taken, c + 8 * i + 2)
                    nc.vector.tensor_tensor(work[:, 2, :], work[:, 0, :], work[:, 1, :], ALU.add).then_inc(merge_ready, 1)
                    dve.wait_ge(merge_ready, q + 4 * i + 1)
                    dve.wait_ge(merged_rounded, q + 4 * i + 1)
                    nc.vector.tensor_tensor(merged_lo[:, bass.ds(m, 1), :], work[:, 2:3, :],
                                            merged_hi[:, bass.ds(m, 1), :].bitcast(F32), ALU.subtract).then_inc(merged_split, 1)
            clear_sums()
            with dve.Fori(0, KM // 4) as i:
                for q in range(4):
                    s, c = PIECES["out"] + q, CHUNKS["out"] + q
                    chunk = bass.ds(4 * i + q, 1)
                    split_lo(dve, s + 1, 4 * i, TILES)
                    dve.wait_ge(piece_done, s + 4 * i + 1)
                    nc.vector.scalar_tensor_tensor(out=x[:, chunk, :], in0=bank[c % 2][:, :].rearrange("p (a n) -> p a n", a=1),
                                                   scalar=0.5, in1=x[:, chunk, :],
                                                   op0=ALU.mult, op1=ALU.add).then_inc(chunk_taken, 1)
                    dve.wait_ge(chunk_taken, c + 4 * i + 1)
                    split_chunk(4 * i + q + 2 * KM + KQ + KKV, x[:, chunk, :], gains[:, bass.ds(4 * i + q + G_FFN2, 1)],
                                act_hi[:, chunk, :], act_lo[:, chunk, :], sumsq[:, :], False)
            up_turn(1, 0, 0, first=True)
            with dve.Fori(0, KF // 2 - 1) as i:
                enter_loop(i, 2)
                up_turn(1, 1, i)
            leave_loop(KF // 2 - 1)
            clear_sums()
            down_turn(1, 0, 0, None, False)
            down_turn(1, 1, 0, None, True)
            reciprocal_root(5, square[:, :], rstd[:, :])
            for k in range(KM):
                nc.vector.scalar_tensor_tensor(out=x[:, k, :], in0=x[:, k, :], scalar=gains[:, G_FINAL + k:G_FINAL + k + 1],
                                               in1=rstd[:, :], op0=ALU.mult, op1=ALU.mult).then_inc(y_ready, 1)


def _tiles(w):
    k, n = w.shape
    return w.reshape(k // P, P, n // P, P).transpose(2, 1, 0, 3).reshape(n // P, P, k)


def _swapped(w):
    half = QK_ROPE // 2
    return np.concatenate([w, w[:, half:], w[:, :half]], axis=1)


def kernel(**inputs):
    import concourse.bacc as bacc
    from concourse.bass_utils import run_bass_kernel_spmd

    given = {k: np.asarray(v) for k, v in inputs.items()}
    arrays = {}

    def put(name, a):
        arrays[name] = np.ascontiguousarray(a)

    put("x_t", given["x"][0].T.reshape(KM, P, SEQ))
    put("positions", given["positions"])
    put("rel_bias", given["rel_bias"])
    columns = [given[n].reshape(-1, P).T for n in
               ("ffn1_norm", "mix_norm", "ffn2_norm", "norm_final", "q_norm", "kv_norm", "b_gate")]
    put("gains", np.concatenate(columns, axis=1))
    for name, a in zip(("tables", "onehot", "t5_masks"), shape_constants()):
        put(name, a)
    for f in ("ffn1", "ffn2"):
        for w in ("gate", "up", "down"):
            put(f"{f}_{w}", _tiles(given[f"{f}_w_{w}"][0]))
    w_in = given["w_in"][0]
    rotary = _swapped(w_in[:, IN_ROPE:IN_Q])
    put("w_latent", _tiles(np.concatenate([w_in[:, :IN_ROPE], rotary, rotary], axis=1)))
    gates = _tiles(w_in[:, IN_GATES:])
    put("w_mla_gates", gates[:MLA_HEADS])
    pairs = []
    for pair in range(PAIRS):
        def heads(start, g):
            at = start + (g * GROUP_HEADS + 2 * pair) * HEAD_DIM
            return _tiles(w_in[:, at:at + 2 * HEAD_DIM])
        qk = [heads(start, g) for g in range(GROUPS) for start in (IN_Q, IN_K)]
        pairs.append(np.concatenate([*qk, *(heads(IN_V, g) for g in range(GROUPS)), gates[MLA_HEADS + 2 * pair:MLA_HEADS + 2 * pair + 2]]))
    put("w_dil", np.stack(pairs))
    up_q = given["w_uq"][0].reshape(Q_LORA, MLA_HEADS, QK_DIM)
    up_kv = _tiles(given["w_ukv"][0])
    rows = []
    for h in range(MLA_HEADS):
        query = np.concatenate([up_q[:, h, :QK_NOPE], _swapped(up_q[:, h, QK_NOPE:])], axis=1)
        rows.append(np.concatenate([_tiles(query)[0], up_kv[h]], axis=1))
    put("w_lora_up", np.stack(rows))
    put("w_branches", np.concatenate([_tiles(given["w_br_mla"][0]), _tiles(given["w_br_dil"][0])], axis=2))
    put("w_out", _tiles(given["w_out"][0]))

    nc = bacc.Bacc("TRN2", target_bir_lowering=False, num_devices=1)
    a = {n: nc.dram_tensor("in_" + n, v.shape, mybir.dt.from_np(v.dtype), kind="ExternalInput").ap() for n, v in arrays.items()}
    skew = nc.dram_tensor("skew", (GROUP_HEADS, P * (T5_END + 1)), F32, kind="Internal").ap()
    y_t = nc.dram_tensor("y_t", (KM, P, SEQ), F32, kind="ExternalOutput").ap()
    ffn = [[a[f"{f}_{w}"] for w in ("gate", "up", "down")] for f in ("ffn1", "ffn2")]
    decoder_layer(nc, a["x_t"], a["positions"], a["rel_bias"], a["gains"], a["tables"], a["onehot"], a["t5_masks"],
                  ffn, a["w_latent"], a["w_lora_up"], a["w_mla_gates"], a["w_dil"], a["w_branches"], a["w_out"],
                  skew, y_t)
    result = run_bass_kernel_spmd(nc, [{"in_" + n: v for n, v in arrays.items()}], core_ids=[0]).results[0]["y_t"]
    return np.ascontiguousarray(result.reshape(D_MODEL, SEQ).T).reshape(1, SEQ, D_MODEL)
```

```python
import math
from contextlib import ExitStack

import concourse.bass as bass
import numpy as np
from concourse import mybir

F32 = mybir.dt.float32
F32R = mybir.dt.float32r
I32 = mybir.dt.int32
ALU = mybir.AluOpType
ACT = mybir.ActivationFunctionType
AX = mybir.AxisListType

P = 128
SEQ = 512
BLOCKS = SEQ // P
D_MODEL = 1024
KM = D_MODEL // P
D_FF = 2816
KF = D_FF // P
EPS = 1e-6
MLA_HEADS, QK_NOPE, QK_ROPE, V_DIM = 8, 64, 32, 64
QK_DIM = QK_NOPE + QK_ROPE
Q_LORA, KV_LORA = 384, 256
KQ, KKV = Q_LORA // P, KV_LORA // P
ROPE_THETA = 10000.0
GROUPS, GROUP_HEADS, HEAD_DIM = 3, 8, 64
PAIRS = GROUP_HEADS // 2
DIL_QKV = GROUPS * GROUP_HEADS * HEAD_DIM
NUM_BUCKETS, MAX_DISTANCE = 32, 2048
STRIDES = (1, 4, 16)
NEG_INF = -1e30
MLA_SCALE = QK_DIM ** -0.5
DIL_SCALE = HEAD_DIM ** -0.5



def _few_bits(value, bits, parts):
    out = []
    for _ in range(parts - 1):
        unit = 2.0 ** (math.floor(math.log2(value)) + 1 - bits)
        out.append(math.floor(value / unit) * unit)
        value -= out[-1]
    return out + [value]


TWO_PI = _few_bits(2 * math.pi, 9, 4)

IN_KV = Q_LORA
IN_ROPE = IN_KV + KV_LORA
IN_Q = IN_ROPE + QK_ROPE
IN_K = IN_Q + DIL_QKV
IN_V = IN_K + DIL_QKV
IN_GATES = IN_V + DIL_QKV

TILES = 8
HALF = TILES // 2
RAW, SPLIT = 4, 2
DOWN_PARTS = ((0, 8), (8, 15), (15, 22))
LORA_TILES = KQ + KKV
WARM_UP = 6
UP_BANKS = 4
SPLIT_FIRST = ((1, 2), (), (3,), (4,))
SPLIT_AT_START = ((3,), (), (4,), ())
UP_SAFE = 3
PIECES = {}
CHUNKS = {}


def _lay_out_stream():
    n = c = 0
    for name, pieces, chunks in (
        ("up1", 2 * KF, 2 * KF), ("down1", 3 * KM, KM), ("latent", 6, 6), ("mla", 2 * MLA_HEADS, 3 * MLA_HEADS),
        ("dil", 12 * PAIRS, 11 * PAIRS), ("merge", KM, 2 * KM), ("out", KM, KM),
        ("up2", 2 * KF, 2 * KF), ("down2", 3 * KM, KM),
    ):
        PIECES[name], CHUNKS[name] = n, c
        n, c = n + pieces, c + chunks
    PIECES["end"], CHUNKS["end"] = n, c


_lay_out_stream()



def first_chunk(h):
    return CHUNKS["mla"] + 3 * h


def gate_chunk(h):
    return CHUNKS["mla"] + 3 * h + 5


LATENTS = (KQ, KQ + 1, 0, 1, 2, None)

C_IDENT, C_ONES, C_EXPAND, C_FOLD = 0, P, 2 * P, 2 * P + SEQ
C_MOD = C_FOLD + SEQ
C_DIV = C_MOD + BLOCKS
C_CAUSAL = C_DIV + BLOCKS
C_FREQ = C_CAUSAL + P
C_TURN, C_PHASE, C_SIGN, C_EPS = C_FREQ + 1, C_FREQ + 2, C_FREQ + 3, C_FREQ + 4
C_END = C_FREQ + 5
G_FFN1, G_MIX, G_FFN2, G_FINAL, G_Q, G_KV = 0, KM, 2 * KM, 3 * KM, 4 * KM, 4 * KM + KQ
G_BIAS = G_KV + KKV
G_END = G_BIAS + 2 * KM
T5_LEN = (3 * P - 1, 2 * P - 1, 2 * P - 1)
T5_AT = (0, T5_LEN[0], T5_LEN[0] + T5_LEN[1])
T5_END = sum(T5_LEN)


def t5_bucket(distance):
    exact = NUM_BUCKETS // 2
    d = np.maximum(distance, 1).astype(np.float32)
    scaled = np.log(d / np.float32(exact)) / np.float32(math.log(MAX_DISTANCE / exact))
    large = exact + (scaled * np.float32(NUM_BUCKETS - exact)).astype(np.int32)
    return np.where(distance < exact, distance, np.minimum(large, NUM_BUCKETS - 1))


def shape_constants():
    c = np.zeros((P, C_END), np.float32)
    p = np.arange(P)
    j = np.arange(SEQ)
    c[:, C_IDENT:C_IDENT + P] = np.eye(P)
    c[:, C_ONES:C_ONES + P] = 1.0
    c[:, C_EXPAND:C_EXPAND + SEQ] = p[:, None] == j[None, :] // 4
    c[:, C_MOD:C_MOD + BLOCKS] = p[:, None] % 4 == np.arange(4)
    c[:, C_FOLD:C_FOLD + SEQ] = p[:, None] == (4 * (j % P) + j // P)[None, :] % P
    c[:, C_DIV:C_DIV + BLOCKS] = p[:, None] // 32 == np.arange(4)
    c[:, C_CAUSAL:C_CAUSAL + P] = np.where(p[None, :] <= p[:, None], 0.0, NEG_INF)
    freq = 1.0 / ROPE_THETA ** (np.arange(0, QK_ROPE, 2, dtype=np.float32) / np.float32(QK_ROPE))
    for row in range(QK_NOPE, P):
        c[row, C_FREQ] = freq.astype(np.float32)[row % 16]
        cosine = row < QK_DIM
        c[row, C_TURN] = 0.25 if cosine else 0.0
        c[row, C_PHASE] = math.pi / 2 if cosine else 0.0
        c[row, C_SIGN] = -1.0 if QK_DIM <= row < QK_DIM + 16 else 1.0
    c[:, C_EPS] = EPS
    onehot = np.zeros((NUM_BUCKETS, T5_END), np.float32)
    mask = np.full((GROUP_HEADS, T5_END), NEG_INF, np.float32)
    for g, stride in enumerate(STRIDES):
        apart = (T5_LEN[g] + 1) // 2 + (P // 2 if g == 0 else 0) - 1 - np.arange(T5_LEN[g])
        unit = 4 if g == 2 else 1
        ok = (apart >= 0) & (apart <= P) & (apart % unit == 0)
        bucket = t5_bucket(np.maximum(apart, 0) // unit * stride)
        at = T5_AT[g] + np.arange(T5_LEN[g])
        onehot[bucket[ok], at[ok]] = 1.0
        mask[:, at[ok]] = 0.0
    return c, onehot, mask


def decoder_layer(nc, x_t, positions, rel_bias, gains_in, tables, onehot_in, mask_in, ffn, w_latent, w_lora_up,
                  w_mla_gates, w_dil, w_branches, w_out, skew, y_t):
    ctx = ExitStack()
    held = []

    def sb(name, shape, dt=F32):
        return ctx.enter_context(nc.sbuf_tensor(name, shape, dt))

    def shared(name, shape, dt=F32):
        manager = nc.sbuf_tensor(name, shape, dt)
        held.append(manager)
        return manager.__enter__()

    def give_back(n):
        for _ in range(n):
            held.pop().__exit__(None, None, None)

    def sem(name):
        return ctx.enter_context(nc.semaphore(name))

    with ctx:
        x = sb("x", [P, KM, SEQ])
        act_hi = sb("act_hi", [P, KM, SEQ], F32R)
        act_lo = sb("act_lo", [P, KM, SEQ], F32R)
        raw = sb("raw", [P, RAW, TILES * P])
        w_hi = sb("w_hi", [P, SPLIT, TILES * P], F32R)
        w_lo = sb("w_lo", [P, SPLIT, TILES * P], F32R)
        const = sb("const", [P, C_END])
        gains = sb("gains", [P, G_END])
        half_bias = sb("half_bias", [P, 2 * KM])
        rstd = sb("rstd", [P, SEQ])
        sumsq = sb("sumsq", [P, SEQ])
        square = sb("square", [P, SEQ])
        work = sb("work", [P, 4, SEQ])
        rope = sb("rope", [P, SEQ])
        first_squares = (square[:, :], work[:, 1, :])
        ident = const[:, C_IDENT:C_IDENT + P]
        ones = const[:, C_ONES:C_ONES + P]
        causal = const[:, C_CAUSAL:C_CAUSAL + P]

        stats = sb("stats", [P, 2, GROUPS, 2, 2 * BLOCKS])
        exchanged = work[:, 3, 0:6 * 4 * 2 * BLOCKS]
        weight = sb("weight", [P, GROUPS, 4 * BLOCKS])
        neg_top = sb("neg_top", [P, 4 * BLOCKS])
        total = sb("total", [P, 4 * BLOCKS])
        mla_stats = sb("mla_stats", [P, 4, BLOCKS])

        hid_hi = shared("hid_hi", [P, KF, SEQ], F32R)
        hid_lo = shared("hid_lo", [P, KF, SEQ], F32R)
        give_back(2)
        shared("hid_head", [P, KF + KF // 2, SEQ])
        position_i = shared("position_i", [P, SEQ], I32)
        turns = shared("turns", [P, SEQ])
        t5_onehot = shared("t5_onehot", [NUM_BUCKETS, T5_END])
        t5_mask = shared("t5_mask", [GROUP_HEADS, T5_END])
        t5_row = shared("t5_row", [GROUP_HEADS, T5_END])
        t5_rel = shared("t5_rel", [NUM_BUCKETS, GROUPS * GROUP_HEADS])
        give_back(7)
        mixed = shared("mixed", [P, 2 * PAIRS, SEQ])
        gates = shared("gates", [P, 2 * KM, SEQ])
        probs_t = shared("probs_t", [P, 2, SEQ])
        lat_hi = shared("lat_hi", [P, KQ + KKV, SEQ], F32R)
        lat_lo = shared("lat_lo", [P, KQ + KKV, SEQ], F32R)
        sumsq_kv = shared("sumsq_kv", [P, SEQ])
        rstd_q = shared("rstd_q", [P, SEQ])
        rstd_kv = shared("rstd_kv", [P, SEQ])
        rope_q = shared("rope_q", [P, SEQ])
        rotated = shared("rotated", [P, SEQ])
        mla_q = shared("mla_q", [P, 2, SEQ])
        mla_k = shared("mla_k", [P, 2, SEQ])
        mla_vt = shared("mla_vt", [P, SEQ])
        mla_v = shared("mla_v", [P, BLOCKS, V_DIM])
        mla_p = shared("mla_p", [P, 10 * P])
        mask_ident = shared("mask_ident", [P, P], F32R)
        mask_causal = shared("mask_causal", [P, P], F32R)
        give_back(14)
        bias0 = shared("bias0", [P, GROUP_HEADS, 2 * P])
        bias12 = shared("bias12", [P, 2, GROUP_HEADS, P])
        dil_q = shared("dil_q", [P, GROUPS, SEQ])
        dil_k = shared("dil_k", [P, GROUPS, SEQ])
        dil_vt = shared("dil_vt", [P, 2, SEQ])
        dil_v = shared("dil_v", [P, GROUPS, BLOCKS, P])
        dil_p = shared("dil_p", [P, 2, 15 * P])
        give_back(7)
        merged_hi = shared("merged_hi", [P, KM, SEQ], F32R)
        merged_lo = shared("merged_lo", [P, KM, SEQ], F32R)
        give_back(2)
        give_back(3)
        bank = [ctx.enter_context(nc.psum_tensor(f"bank{i}", [P, SEQ], F32)) for i in range(8)]

        raw_loaded = [sem(f"raw_loaded{i}") for i in range(RAW)]
        hi_ready, lo_ready = sem("hi_ready"), sem("lo_ready")
        piece_done = sem("piece_done")
        inner_done, chunk_taken = sem("inner_done"), sem("chunk_taken")
        x_loaded = [sem(f"x_loaded{k}") for k in range(KM)]
        gains_loaded, scalars_loaded = sem("gains_loaded"), sem("scalars_loaded")
        zeros_ready, position_loaded = sem("zeros_ready"), sem("position_loaded")
        const_loaded, table_loaded = sem("const_loaded"), sem("table_loaded")
        act_rounded, act_split = sem("act_rounded"), sem("act_split")
        squared, sumsq_added = sem("squared"), sem("sumsq_added")
        norm_full, root_ready, rstd_ready = sem("norm_full"), sem("root_ready"), sem("rstd_ready")
        silu_ready, hid_rounded, hid_split = sem("silu_ready"), sem("hid_rounded"), sem("hid_split")
        angle_ready, rows_ready = sem("angle_ready"), sem("rows_ready")
        setup_act, setup_pe = sem("setup_act"), sem("setup_pe")
        skew_stored, bias_loaded = sem("skew_stored"), sem("bias_loaded")
        own = sem("own")
        gate_ready = sem("gate_ready")
        head_ready, mask_ready = sem("head_ready"), sem("mask_ready")
        mla_scores, mla_max, mla_exp, mla_scaled = sem("mla_scores"), sem("mla_max"), sem("mla_exp"), sem("mla_scaled")
        turned, turned_taken, pv_done = sem("turned"), sem("turned_taken"), sem("pv_done")
        mixed_taken = sem("mixed_taken")
        dil_scores, dil_taken = sem("dil_scores"), sem("dil_taken")
        dil_max, dil_exp, dil_scaled = sem("dil_max"), sem("dil_exp"), sem("dil_scaled")
        v_turned, v_taken = sem("v_turned"), sem("v_taken")
        stats_moved, weight_ready, weight_exp = sem("stats_moved"), sem("weight_ready"), sem("weight_exp")
        mixed_rounded, mixed_split = sem("mixed_rounded"), sem("mixed_split")
        merge_ready, merged_rounded, merged_split = sem("merge_ready"), sem("merged_rounded"), sem("merged_split")
        y_ready, stored = sem("y_ready"), sem("stored")


        def load(sp, s, d, source, tiles):
            if s >= RAW:
                sp.wait_ge(lo_ready, s + d - (RAW - 1))
            sp.dma_start(raw[:, s % RAW, 0:tiles * P], source).then_inc(raw_loaded[s % RAW], 16)

        def split_hi(act, s, d, tiles):
            act.wait_ge(raw_loaded[s % RAW], 16 * (s // RAW + 1) + 16 // RAW * d)
            if s >= SPLIT:
                act.wait_ge(piece_done, s + d - (SPLIT - 1))
            nc.scalar.activation(w_hi[:, s % SPLIT, 0:tiles * P], raw[:, s % RAW, 0:tiles * P],
                                 ACT.Copy).then_inc(hi_ready, 1)

        def split_lo(dve, s, d, tiles):
            dve.wait_ge(hi_ready, s + d + 1)
            nc.vector.tensor_tensor(w_lo[:, s % SPLIT, 0:tiles * P], raw[:, s % RAW, 0:tiles * P],
                                    w_hi[:, s % SPLIT, 0:tiles * P].bitcast(F32),
                                    ALU.subtract).then_inc(lo_ready, 1)

        def multiply(s, tiles, out, hi, lo, start=True, stop=True, before=None):
            last = None
            for k, t in enumerate(tiles):
                if before is not None:
                    before(k)
                a = w_hi[:, s % SPLIT, t * P:(t + 1) * P]
                b = w_lo[:, s % SPLIT, t * P:(t + 1) * P]
                first, end = start and k == 0, stop and k == len(tiles) - 1
                nc.tensor.matmul(out, a, hi(k), start=first, stop=False)
                nc.tensor.matmul(out, a, lo(k), start=False, stop=False)
                last = nc.tensor.matmul(out, b, hi(k), start=False, stop=end)
            return last

        def free_chunk(pe, c, banks=2):
            pe.wait_ge(chunk_taken, c + 1 - banks)

        block = ctx.enter_context(nc.Block())

        @block.sync
        def _(sp):
            def load_up_turn(f, turn, i):
                for q in range(4):
                    if f == 0 and turn == 0 and q == 0:
                        continue
                    source = ffn[f][q % 2][bass.ds(2 * (turn + i) + q // 2, 1)]
                    load(sp, PIECES[f"up{f + 1}"] + 4 * turn + q, 4 * i, source.rearrange("a p n -> p (a n)"), TILES)

            def load_down(f):
                with sp.Fori(0, KM // 4) as i:
                    for m in range(4):
                        row = ffn[f][2][bass.ds(4 * i + m, 1)].rearrange("a p n -> p (a n)")
                        for part, (a, b) in enumerate(DOWN_PARTS):
                            load(sp, PIECES[f"down{f + 1}"] + 3 * m + part, 12 * i, row[:, a * P:b * P], b - a)

            def load_ffn(f):
                load_up_turn(f, 0, 0)
                with sp.Fori(0, KF // 2 - 1) as i:
                    load_up_turn(f, 1, i)
                load_down(f)

            for k in range(KM):
                sp.dma_start(x[:, k, :], x_t[k]).then_inc(x_loaded[k], 16)
                if k == 0:
                    load(sp, 0, 0, ffn[0][0][0], TILES)
            load_ffn(0)
            for q in range(6):
                load(sp, PIECES["latent"] + q, 0, w_latent[q], TILES)
            s = PIECES["mla"]
            load(sp, s, 0, w_lora_up[0], LORA_TILES)
            load(sp, s + 1, 0, w_mla_gates[0], TILES)
            with sp.Fori(0, PAIRS - 1) as i:
                for h in range(2):
                    up, gate = (w[bass.ds(2 * i + h + 1, 1)].rearrange("a p n -> p (a n)") for w in (w_lora_up, w_mla_gates))
                    load(sp, s + 2 + 2 * h, 4 * i, up, LORA_TILES)
                    load(sp, s + 3 + 2 * h, 4 * i, gate, TILES)
            load(sp, s + 2 * MLA_HEADS - 2, 0, w_lora_up[MLA_HEADS - 1], LORA_TILES)
            load(sp, s + 2 * MLA_HEADS - 1, 0, w_mla_gates[MLA_HEADS - 1], TILES)
            with sp.Fori(0, PAIRS) as i:
                for q in range(10):
                    load(sp, PIECES["dil"] + q, 12 * i, w_dil[bass.ds(i, 1), q].rearrange("a p n -> p (a n)"), TILES)
                last_gate = w_dil[bass.ds(i, 1), 10].rearrange("a p n -> p (a n)")
                for part in range(2):
                    load(sp, PIECES["dil"] + 10 + part, 12 * i, last_gate[:, part * HALF * P:(part + 1) * HALF * P], HALF)
            for phase, source in (("merge", w_branches), ("out", w_out)):
                with sp.Fori(0, KM // 4) as i:
                    for q in range(4):
                        load(sp, PIECES[phase] + q, 4 * i, source[bass.ds(4 * i + q, 1)].rearrange("a p n -> p (a n)"), TILES)
            load_ffn(1)
            for k in range(KM):
                sp.wait_ge(y_ready, k + 1)
                sp.dma_start(y_t[k], x[:, k, :]).then_inc(stored, 16)
            sp.wait_ge(stored, 16 * KM)

        @block.gpsimd
        def _(pool):
            pool.dma_start(position_i[QK_NOPE:P, :], positions.to_broadcast([P - QK_NOPE, SEQ])).then_inc(position_loaded, 16)
            pool.dma_start(const[:, 0:C_FREQ], tables[:, 0:C_FREQ]).then_inc(const_loaded, 16)
            pool.dma_start(t5_onehot[:, :], onehot_in).then_inc(table_loaded, 16)
            pool.dma_start(t5_mask[:, :], mask_in).then_inc(table_loaded, 16)
            pool.dma_start(t5_rel[:, :], rel_bias).then_inc(table_loaded, 16)
            pool.wait_ge(rows_ready, 1)
            copies = skew.rearrange("h (p n) -> h p n", p=P)[:, :, 0:T5_END]
            row = t5_row[:, :].rearrange("h (a n) -> h a n", a=1).to_broadcast([GROUP_HEADS, P, T5_END])
            pool.dma_start(copies, row).then_inc(skew_stored, 16)
            pool.wait_ge(skew_stored, 16)
            pool.wait_ge(mixed_taken, PAIRS)
            for g, width in enumerate((2 * P, P, P)):
                source = bass.AP(skew.tensor, T5_AT[g] + P - 1,
                                 [[T5_END, P], [P * (T5_END + 1), GROUP_HEADS], [1, width]])
                table = bias0[:, :, :] if g == 0 else bias12[:, g - 1, :, :]
                pool.dma_start(table, source).then_inc(bias_loaded, 16)

        @block.tensor
        def _(pe):
            def norm(k, source, out):
                pe.wait_ge(const_loaded, 16)
                pe.wait_ge(sumsq_added, k)
                nc.tensor.matmul(out, ones, source, start=True, stop=True).then_inc(norm_full, 1)

            def up_turn(f, turn, i, first=False):
                for q in range(4):
                    s = PIECES[f"up{f + 1}"] + 4 * turn + q
                    c = CHUNKS[f"up{f + 1}"] + 4 * turn + q
                    if c >= UP_BANKS:
                        free_chunk(pe, c + 4 * i, UP_BANKS)
                    pe.wait_ge(lo_ready, s + 4 * i + 1)

                    def before(k):
                        if q == 0:
                            pe.wait_ge(act_split, (0, 2 * KM + KQ + KKV)[f] + k + 1)
                        if f == 0 and q == 2 and k == 4:
                            norm(KM, sumsq[:, :], bank[7][:, :])

                    multiply(s, range(TILES), bank[c % UP_BANKS][:, :], lambda k: act_hi[:, k, :],
                             lambda k: act_lo[:, k, :], before=before if first else None).then_inc(piece_done, 1)
                    if first and f and q == 0:
                        norm(3 * KM + KQ + KKV, sumsq[:, :], bank[7][:, :])
                    if first and f == 0 and q == 2:
                        pe.wait_ge(table_loaded, 48)
                        for g in range(GROUPS):
                            last = nc.tensor.matmul(bank[4 + g][0:GROUP_HEADS, 0:T5_LEN[g]],
                                                    t5_rel[:, g * GROUP_HEADS:(g + 1) * GROUP_HEADS],
                                                    t5_onehot[:, T5_AT[g]:T5_AT[g] + T5_LEN[g]], start=True, stop=True)
                        last.then_inc(setup_pe, 1)

            def down_turn(f, turn, i):
                for m in range(4):
                    c = CHUNKS[f"down{f + 1}"] + 4 * turn + m
                    free_chunk(pe, c + 4 * i)
                    for part, (a, b) in enumerate(DOWN_PARTS):
                        s = PIECES[f"down{f + 1}"] + 12 * turn + 3 * m + part
                        pe.wait_ge(lo_ready, s + 12 * i + 1)
                        pe.wait_ge(hid_split, KF * f + b)
                        multiply(s, range(b - a), bank[c % 2][:, :], lambda k: hid_hi[:, a + k, :],
                                 lambda k: hid_lo[:, a + k, :], start=part == 0, stop=part == 2).then_inc(piece_done, 1)

            def ffn_products(f):
                up_turn(f, 0, 0, first=True)
                with pe.Fori(0, KF // 2 - 1) as i:
                    up_turn(f, 1, i)
                with pe.Fori(0, 2) as i:
                    down_turn(f, 0, i)

            def project(s, d, c, bank_of, before=None):
                free_chunk(pe, c)
                pe.wait_ge(lo_ready, s + d + 1)
                multiply(s, range(TILES), bank_of, lambda k: act_hi[:, k, :], lambda k: act_lo[:, k, :],
                         before=before).then_inc(piece_done, 1)

            pe.wait_ge(zeros_ready, 1)
            for _ in range(WARM_UP):
                nc.tensor.matmul(bank[7][:, :], work[:, 0, 0:P], work[:, 0, :], start=True, stop=True)
            ffn_products(0)

            for q in range(6):
                c = CHUNKS["latent"] + q
                def before(k):
                    if q == 0:
                        pe.wait_ge(act_split, KM + k + 1)
                    if q == 3 and k == 4:
                        norm(2 * KM + KKV, sumsq_kv[:, :], bank[4][:, :])

                free_chunk(pe, c, UP_BANKS)
                pe.wait_ge(lo_ready, PIECES["latent"] + q + 1)
                multiply(PIECES["latent"] + q, range(TILES), bank[c % UP_BANKS][:, :], lambda k: act_hi[:, k, :],
                         lambda k: act_lo[:, k, :], before=before).then_inc(piece_done, 1)
                if q == 0:
                    norm(2 * KM, sumsq[:, :], bank[7][:, :])
            norm(2 * KM + KQ + KKV, sumsq[:, :], bank[7][:, :])

            def lora(s, d, h, i):
                pe.wait_ge(lo_ready, s + d + 1)
                c = first_chunk(h)
                for part, tiles in enumerate((range(KQ, LORA_TILES), range(KQ))):
                    free_chunk(pe, c + part + 6 * i)
                    base = tiles[0]
                    multiply(s, tiles, bank[(c + part) % 2][:, :], lambda k: lat_hi[:, base + k, :],
                             lambda k: lat_lo[:, base + k, :]).then_inc(piece_done if part else inner_done, 1)

            def turn_values(h, i):
                unit = 4 * h
                for b in range(BLOCKS):
                    last = nc.tensor.transpose(bank[5 + unit % 2][:, b * V_DIM:(b + 1) * V_DIM],
                                               mla_vt[QK_NOPE:P, b * P:(b + 1) * P], ident[QK_NOPE:P, QK_NOPE:P])
                last.then_inc(turned, 1)

            def score(h, i):
                pe.wait_ge(head_ready, h + 2 * i + 1)
                for b, (out, diagonal) in enumerate(((bank[2][:, 0:P], bank[2][:, 0:P]),
                                                     (bank[3][:, 0:2 * P], bank[3][:, P:2 * P]),
                                                     (bank[2][:, P:SEQ], bank[2][:, 3 * P:SEQ]),
                                                     (bank[4][:, :], bank[4][:, 3 * P:SEQ]))):
                    nc.tensor.matmul(out, mla_q[0:QK_DIM, h % 2, b * P:(b + 1) * P],
                                     mla_k[0:QK_DIM, h % 2, 0:(b + 1) * P], start=True, stop=False, skip_group_check=True)
                    last = nc.tensor.matmul(diagonal, mask_ident[:, :], mask_causal[:, :], start=False, stop=True,
                                            skip_group_check=True)
                last.then_inc(mla_scores, 1)

            def turn_probs(h, i, part):
                unit = 4 * h + 1 + part
                pe.wait_ge(mla_scaled, 4 * h + 8 * i + 4)
                pe.wait_ge(turned_taken, unit + 8 * i - (1 if part else 0))
                at = 0
                for key in ((0,), (1,), (2, 3))[part]:
                    for b in range(key, BLOCKS):
                        row = b * (b + 1) // 2 + key
                        last = nc.tensor.transpose(bank[5 + unit % 2][:, at:at + P], mla_p[:, row * P:(row + 1) * P], ident)
                        at += P
                last.then_inc(turned, 1)

            def attend(h, i, part):
                unit = 4 * h + 1 + part
                pe.wait_ge(turned_taken, unit + 8 * i + 1)
                row = V_DIM * (h % 2)
                at = 0
                for key in ((0,), (1,), (2, 3))[part]:
                    width = SEQ - key * P
                    last = nc.tensor.matmul(bank[7][row:row + V_DIM, key * P:SEQ], mla_v[:, key, :],
                                            probs_t[:, (3 * h + part) % 2, at:at + width],
                                            start=key == 0, stop=key == 3, skip_group_check=True)
                    at += width
                last.then_inc(pv_done, 1)

            def attention(h, i, s, d):
                score(h, i)
                turn_values(h, i)

                def turn_early(k):
                    if k == 6:
                        turn_probs(h, i, 0)
                        turn_probs(h, i, 1)

                if h < MLA_HEADS - 1:
                    lora(s, d, h + 1, i)
                    c = gate_chunk(h)
                    project(s + 1, d, c + 6 * i, bank[c % 2][:, :], turn_early)
                else:
                    c = CHUNKS["dil"]
                    project(PIECES["dil"], 0, c, bank[c % 2][:, :], turn_early)
                turn_probs(h, i, 2)
                for part in range(3):
                    attend(h, i, part)

            s = PIECES["mla"]
            pe.wait_ge(mask_ready, 2)
            pe.wait_ge(act_split, 2 * KM + KQ + KKV)
            lora(s, 0, 0, 0)
            project(s + 1, 0, gate_chunk(-1), bank[gate_chunk(-1) % 2][:, :])
            with pe.Fori(0, PAIRS - 1) as i:
                attention(0, i, s + 2, 4 * i)
                attention(1, i, s + 4, 4 * i)
            attention(MLA_HEADS - 2, 0, s + 2 * MLA_HEADS - 2, 0)
            attention(MLA_HEADS - 1, 0, None, 0)

            def tokens(g, b):
                return slice(b * P, (b + 1) * P) if g == 0 else slice(b, SEQ, BLOCKS)

            def dil_score(g, i):
                for e in range(2):
                    unit = 2 * g + e
                    if unit >= 2:
                        pe.wait_ge(dil_taken, unit + 6 * i - 1)
                    rows = slice(HEAD_DIM * e, HEAD_DIM * (e + 1))
                    one, two = (bank[2], bank[3]) if e == 0 else (bank[4], bank[7])
                    for b in range(BLOCKS):
                        if g == 0:
                            out = (one[:, 0:P], one[:, P:3 * P], two[:, 0:2 * P], two[:, 2 * P:SEQ])[b]
                            keys = slice(max(b - 1, 0) * P, (b + 1) * P)
                        else:
                            out, keys = one[:, b * P:(b + 1) * P], tokens(g, b)
                        last = nc.tensor.matmul(out, dil_q[rows, g, tokens(g, b)], dil_k[rows, g, keys],
                                                start=True, stop=True, skip_group_check=True)
                    last.then_inc(dil_scores, 1)

            def turn_dil_values(g, i):
                if g:
                    pe.wait_ge(v_taken, g + 3 * i)
                for b in range(BLOCKS):
                    last = nc.tensor.transpose(bank[3][:, b * P:(b + 1) * P], dil_vt[:, g % 2, tokens(g, b)], ident)
                last.then_inc(v_turned, 1)

            def turn_dil(e, part, i):
                unit = 4 * e + part
                pe.wait_ge(turned_taken, 4 * MLA_HEADS + unit + 8 * i - 1)
                pe.wait_ge(dil_scaled, (4 * e + (2, 2, 3, 4)[part]) + 8 * i)
                if part < 2:
                    columns = [(0, P, 2 * P, 3 * P), (4 * P, 5 * P, 6 * P)][part]
                else:
                    columns = [(7 + 4 * (part - 2) + b) * P for b in range(BLOCKS)]
                for at, column in enumerate(columns):
                    last = nc.tensor.transpose(bank[5 + unit % 2][:, at * P:(at + 1) * P],
                                               dil_p[:, e, column:column + P], ident)
                last.then_inc(turned, 1)

            def attend_dil(e, part, i):
                unit = 4 * e + part
                pe.wait_ge(turned_taken, 4 * MLA_HEADS + unit + 8 * i + 1)
                rows = slice(HEAD_DIM * e, HEAD_DIM * (e + 1))
                pt = probs_t[:, unit % 2, :]
                if part < 2:
                    for n in range(2):
                        key = 2 * part + n
                        width = min(2 * P, SEQ - key * P)
                        last = nc.tensor.matmul(bank[2][rows, key * P:key * P + width], dil_v[:, 0, key, rows],
                                                pt[:, 2 * n * P:2 * n * P + width], start=key == 0, stop=False,
                                                skip_group_check=True)
                else:
                    for b in range(BLOCKS):
                        last = nc.tensor.matmul(bank[2][rows, b:SEQ:BLOCKS], dil_v[:, part - 1, b, rows],
                                                pt[:, b * P:(b + 1) * P], start=False,
                                                stop=part == 3 and b == BLOCKS - 1, skip_group_check=True)
                last.then_inc(pv_done, 1)

            def dilated_pair(i, first=False):
                s, d, c, e = PIECES["dil"], 12 * i, CHUNKS["dil"], 11 * i

                def dil_project(q):
                    free_chunk(pe, c + e + (q or -1))
                    pe.wait_ge(lo_ready, s + d + q + 1)
                    multiply(s + q, range(TILES), bank[(c + q) % 2][:, :], lambda k: act_hi[:, k, :],
                             lambda k: act_lo[:, k, :]).then_inc(piece_done, 1)

                def use(unit):
                    attend_dil(unit // 4, unit % 4, i)
                    if unit < 6:
                        turn_dil((unit + 2) // 4, (unit + 2) % 4, i)

                def last_gate(part):
                    pe.wait_ge(lo_ready, s + d + 10 + part + 1)
                    base = part * HALF
                    multiply(s + 10 + part, range(HALF), bank[4][:, :], lambda k: act_hi[:, base + k, :],
                             lambda k: act_lo[:, base + k, :], start=part == 0, stop=part == 1,
                             before=lambda k: use(base + k - 1) if k else None).then_inc(piece_done, 1)

                if not first:
                    dil_project(0)
                dil_project(1)
                dil_project(2)
                pe.wait_ge(mixed_taken, PAIRS + i)
                pe.wait_ge(chunk_taken, c + e + 2)
                dil_score(0, i)
                dil_project(3)
                dil_project(4)
                pe.wait_ge(chunk_taken, c + e + 4)
                dil_score(1, i)
                dil_project(5)
                dil_project(6)
                pe.wait_ge(chunk_taken, c + e + 6)
                dil_score(2, i)
                dil_project(7)
                pe.wait_ge(chunk_taken, c + e + 7)
                turn_dil_values(0, i)
                dil_project(8)
                pe.wait_ge(chunk_taken, c + e + 8)
                turn_dil_values(1, i)
                pe.wait_ge(dil_exp, 24 * i + 24)
                for b in range(BLOCKS):
                    nc.tensor.matmul(bank[7][:, b * 16:(b + 1) * 16], const[:, C_FOLD + b * P:C_FOLD + (b + 1) * P],
                                     stats[:, :, 0, 0, :], start=True, stop=True, skip_group_check=True)
                for b in range(BLOCKS):
                    last = nc.tensor.matmul(bank[7][:, 64 + b * 32:96 + b * 32],
                                            const[:, C_EXPAND + b * P:C_EXPAND + (b + 1) * P],
                                            stats[:, :, 1:3, 1, :], start=True, stop=True, skip_group_check=True)
                last.then_inc(stats_moved, 1)
                dil_project(9)
                pe.wait_ge(chunk_taken, c + e + 9)
                turn_dil_values(2, i)
                turn_dil(0, 0, i)
                turn_dil(0, 1, i)
                pe.wait_ge(v_taken, 3 * i + 3)
                for part in range(2):
                    last_gate(part)
                    use(HALF * part + HALF - 1)

            dilated_pair(0, first=True)
            with pe.Fori(1, PAIRS) as i:
                dilated_pair(i)

            with pe.Fori(0, KM // 4) as i:
                for q in range(4):
                    s, c = PIECES["merge"] + q, CHUNKS["merge"] + 2 * q
                    pe.wait_ge(lo_ready, s + 4 * i + 1)
                    for branch in range(2):
                        base = branch * PAIRS
                        free_chunk(pe, c + branch + 8 * i)
                        last = multiply(s, range(base, base + PAIRS), bank[branch][:, :], lambda k: act_hi[:, base + k, :],
                                        lambda k: act_lo[:, base + k, :],
                                        before=(lambda k: pe.wait_ge(mixed_split, base + k + 1)) if q == 0 else None)
                        last.then_inc(piece_done if branch else inner_done, 1)
            with pe.Fori(0, KM // 4) as i:
                for q in range(4):
                    s, c = PIECES["out"] + q, CHUNKS["out"] + q
                    free_chunk(pe, c + 4 * i)
                    pe.wait_ge(lo_ready, s + 4 * i + 1)
                    multiply(s, range(TILES), bank[c % 2][:, :], lambda k: merged_hi[:, k, :], lambda k: merged_lo[:, k, :],
                             before=(lambda k: pe.wait_ge(merged_split, k + 1)) if q == 0 else None).then_inc(piece_done, 1)
            ffn_products(1)
            pe.wait_ge(sumsq_added, 4 * KM + KQ + KKV - 1)
            nc.tensor.matmul(bank[7][:, :], ones, sumsq[:, :], start=True, stop=False)
            pe.wait_ge(squared, 4 * KM + KQ + KKV)
            nc.tensor.matmul(bank[7][:, :], ones, square[:, :], start=False, stop=True).then_inc(norm_full, 1)

        @block.scalar
        def _(act):
            act.dma_start(gains[:, :], gains_in).then_inc(gains_loaded, 16)
            act.dma_start(const[:, C_FREQ:C_END], tables[:, C_FREQ:C_END]).then_inc(scalars_loaded, 16)

            def round_scaled(source, gain, hi):
                act.wait_ge(gains_loaded, 16)
                nc.scalar.activation(hi, source, ACT.Copy, scale=gain).then_inc(act_rounded, 1)

            def round_chunk(k, source, gain, hi):
                if hi is not None:
                    round_scaled(source, gain, hi)
                act.wait_ge(gains_loaded, 16)
                if not isinstance(k, int) or k:
                    act.wait_ge(sumsq_added, k)
                nc.scalar.activation(square[:, :], source, ACT.Square).then_inc(squared, 1)

            def root(n, sums, features, out):
                act.wait_ge(scalars_loaded, 16)
                act.wait_ge(norm_full, n + 1)
                nc.scalar.activation(out, sums, ACT.Sqrt, bias=const[:, C_EPS:C_EPS + 1],
                                     scale=1.0 / features).then_inc(root_ready, 1)

            def split_first(q, s, d, step):
                for n in SPLIT_FIRST[q] if s > q else SPLIT_AT_START[q]:
                    split_hi(act, s - q + n, d, TILES)
                if q == 0:
                    step()

            def up_turn(f, turn, i, first=False):
                for q in range(4):
                    s = PIECES[f"up{f + 1}"] + 4 * turn + q
                    c = CHUNKS[f"up{f + 1}"] + 4 * turn + q
                    if first:
                        split_first(q, s, 4 * i, lambda: root((0, 4)[f], bank[7][:, :], D_MODEL, square[:, :]))
                    else:
                        split_hi(act, s + 1, 4 * i, TILES)
                    j = 2 * turn + q // 2
                    act.wait_ge(chunk_taken, c + 4 * i + 1)
                    act.wait_ge(gains_loaded, 16)
                    if q % 2 == 0:
                        nc.scalar.activation(work[:, 1, :], work[:, 0, :], ACT.Silu).then_inc(silu_ready, 1)
                    else:
                        nc.scalar.activation(hid_hi[:, bass.ds(2 * i + j, 1), :],
                                             work[:, 3:4, :], ACT.Copy).then_inc(hid_rounded, 1)

            def down_turn(f, turn, i, gain, final):
                for m in range(4):
                    for part in range(3):
                        s = PIECES[f"down{f + 1}"] + 12 * turn + 3 * m + part
                        if not (final and m == 3 and part == 2):
                            following = DOWN_PARTS[(part + 1) % 3]
                            split_hi(act, s + 1, 12 * i, following[1] - following[0])
                    act.wait_ge(chunk_taken, CHUNKS[f"down{f + 1}"] + 4 * turn + m + 4 * i + 1)
                    k = 4 * turn + m
                    chunk = bass.ds(4 * i + k, 1)
                    before = (KM, 3 * KM + KQ + KKV)[f]
                    if final and m == 2:
                        nc.scalar.activation(mla_stats[:, 0, 0:1], const[:, C_EPS:C_EPS + 1], ACT.Sqrt)
                    if gain is None:
                        round_chunk(4 * i + k + before, x[:, chunk, :], None, None)
                    else:
                        round_chunk(4 * i + k + before, x[:, chunk, :], gains[:, bass.ds(4 * i + k + gain, 1)],
                                    act_hi[:, chunk, :])

            for k in range(KM):
                act.wait_ge(x_loaded[k], 16)
                round_scaled(x[:, k, :], gains[:, G_FFN1 + k:G_FFN1 + k + 1], act_hi[:, k, :])
                if k == 0:
                    split_hi(act, 0, 0, TILES)
            split_hi(act, 1, 0, TILES)
            for k in range(KM):
                if k >= 2:
                    act.wait_ge(sumsq_added, k - 1)
                nc.scalar.activation(first_squares[k % 2], x[:, k, :], ACT.Square).then_inc(squared, 1)
                if k == 3:
                    split_hi(act, 2, 0, TILES)
            nc.scalar.mul(half_bias[:, :], gains[:, G_BIAS:G_BIAS + 2 * KM], 0.5).then_inc(setup_act, 1)
            up_turn(0, 0, 0, first=True)
            with act.Fori(0, KF // 2 - 1) as i:
                up_turn(0, 1, i)
            act.wait_ge(angle_ready, 1)
            nc.scalar.activation(rope[QK_NOPE:P, :], rope[QK_NOPE:P, :], ACT.Sin,
                                 scale=const[QK_NOPE:P, C_SIGN:C_SIGN + 1]).then_inc(setup_act, 1)
            with act.Fori(0, 2) as i:
                down_turn(0, 0, i, G_MIX, False)

            for q in range(6):
                s = PIECES["latent"] + q
                if q == 0:
                    split_hi(act, s + 1, 0, TILES)
                if q != 1:
                    split_hi(act, s + 2, 0, LORA_TILES if q == 4 else TILES)
                if q == 5:
                    act.wait_ge(sumsq_added, 2 * KM + KQ + KKV)
                    root(3, bank[7][:, :], Q_LORA, square[:, :])
                if q == 0:
                    root(1, bank[7][:, :], D_MODEL, square[:, :])
                    split_hi(act, s + 3, 0, TILES)
                n = LATENTS[q]
                if n is not None:
                    act.wait_ge(chunk_taken, CHUNKS["latent"] + q + 1)
                    round_chunk(2 * KM + q, work[:, q % 2, :], gains[:, G_Q + n:G_Q + n + 1], lat_hi[:, n, :])
                if q == 0:
                    act.wait_ge(const_loaded, 16)
                    nc.scalar.copy(mask_ident[:, :], ident).then_inc(mask_ready, 1)
                    nc.scalar.copy(mask_causal[:, :], causal).then_inc(mask_ready, 1)
                if q == 2:
                    root(2, bank[4][:, :], KV_LORA, sumsq_kv[:, :])

            def gate_tanh(c, k):
                act.wait_ge(chunk_taken, c + 1)
                act.wait_ge(setup_act, 1)
                nc.scalar.activation(gates[:, bass.ds(k, 1), :], work[:, 0:1, :], ACT.Tanh,
                                     bias=half_bias[:, bass.ds(k, 1)], scale=0.5).then_inc(gate_ready, 1)

            def take_values(h, i):
                act.wait_ge(turned, 4 * h + 8 * i + 1)
                nc.scalar.copy(mla_v[:, :, :].rearrange("p b n -> p (b n)"),
                               bank[5 + (4 * h) % 2][:, 0:BLOCKS * V_DIM]).then_inc(turned_taken, 1)

            def exponentials(h, i):
                for b, source in enumerate((bank[2][:, 0:P], bank[3][:, 0:2 * P], bank[2][:, P:SEQ], bank[4][:, :])):
                    if b == 0:
                        act.wait_ge(mla_max, h + 2 * i + 1)
                    row = b * (b + 1) // 2
                    nc.scalar.activation(mla_p[:, row * P:(row + b + 1) * P], source, ACT.Exp,
                                         bias=mla_stats[:, 1, b:b + 1], scale=MLA_SCALE,
                                         accum_out=mla_stats[:, 2, b:b + 1]).then_inc(mla_exp, 1)

            def take_probs(h, i):
                for part, width in enumerate((4 * P, 3 * P, 3 * P)):
                    unit = 4 * h + 1 + part
                    act.wait_ge(turned, unit + 8 * i + 1)
                    n = 3 * h + part
                    if n >= 2:
                        act.wait_ge(pv_done, n + 6 * i - 1)
                    nc.scalar.copy(probs_t[:, n % 2, 0:width], bank[5 + unit % 2][:, 0:width]).then_inc(turned_taken, 1)

            def attention(h, i, s, d, following):
                take_values(h, i)
                exponentials(h, i)
                split_hi(act, s + 2, d, following[0])
                take_probs(h, i)
                if h < MLA_HEADS - 1:
                    gate_tanh(gate_chunk(h) + 6 * i, h + 1 + 2 * i)
                if following[1]:
                    split_hi(act, s + 3, d, following[1])

            s = PIECES["mla"]
            split_hi(act, s + 2, 0, LORA_TILES)
            gate_tanh(gate_chunk(-1), 0)
            split_hi(act, s + 3, 0, TILES)
            with act.Fori(0, PAIRS - 1) as i:
                attention(0, i, s + 2, 4 * i, (LORA_TILES, TILES))
                attention(1, i, s + 4, 4 * i, (LORA_TILES, TILES))
            attention(MLA_HEADS - 2, 0, s + 2 * MLA_HEADS - 2, 0, (TILES, 0))
            attention(MLA_HEADS - 1, 0, s + 2 * MLA_HEADS - 1, 0, (TILES, 0))

            def dil_exponentials(g, i):
                for e in range(2):
                    unit = 2 * g + e
                    act.wait_ge(dil_max, unit + 6 * i + 1)
                    for b in range(BLOCKS):
                        first, blocks = ((0, 1), (1, 2), (3, 2), (5, 2))[b] if g == 0 else (3 + 4 * g + b, 1)
                        p = dil_p[:, e, first * P:(first + blocks) * P]
                        order, at = min(g, 1), 2 * b + e
                        nc.scalar.activation(p, p, ACT.Exp, bias=stats[:, 0, g, order, at:at + 1],
                                             accum_out=stats[:, 1, g, order, at:at + 1]).then_inc(dil_exp, 1)

            def take_dil_values(g, i):
                act.wait_ge(v_turned, g + 3 * i + 1)
                nc.scalar.copy(dil_v[:, g, :, :].rearrange("p b n -> p (b n)"), bank[3][:, :]).then_inc(v_taken, 1)

            def take_dil_probs(unit, i):
                width = 3 * P if unit % 4 == 1 else SEQ
                act.wait_ge(turned, 4 * MLA_HEADS + unit + 8 * i + 1)
                act.wait_ge(pv_done, 3 * MLA_HEADS + unit + 8 * i - 1)
                nc.scalar.copy(probs_t[:, unit % 2, 0:width], bank[5 + unit % 2][:, 0:width]).then_inc(turned_taken, 1)

            def dilated_pair(i, first=False):
                s, d, c, e = PIECES["dil"], 12 * i, CHUNKS["dil"], 11 * i
                for q in range(10):
                    if q or not first:
                        split_hi(act, s + q + 1, d, HALF if q == 9 else TILES)
                    if q == 0 and not first:
                        gate_tanh(c + e - 1, MLA_HEADS - 1 + 2 * i)
                    if q in (3, 5, 7):
                        dil_exponentials(q // 2 - 1, i)
                    if q in (7, 8):
                        take_dil_values(q - 7, i)
                act.wait_ge(weight_ready, i + 1)
                nc.scalar.activation(weight[:, :, :], weight[:, :, :], ACT.Exp).then_inc(weight_exp, 1)
                take_dil_values(2, i)
                split_hi(act, s + 11, d, HALF)
                for unit in range(8):
                    take_dil_probs(unit, i)
                    if unit == 1:
                        gate_tanh(c + e + 9, MLA_HEADS + 2 * i)
                    if unit == 4:
                        split_hi(act, s + 12, d, TILES)

            dilated_pair(0, first=True)
            with act.Fori(1, PAIRS) as i:
                dilated_pair(i)

            act.wait_ge(piece_done, PIECES["merge"])
            for k in range(2 * PAIRS):
                if k == PAIRS:
                    gate_tanh(CHUNKS["merge"] - 1, 2 * KM - 1)
                act.wait_ge(mixed_taken, k + 1)
                nc.scalar.copy(act_hi[:, k, :], mixed[:, k, :]).then_inc(mixed_rounded, 1)
            with act.Fori(0, KM // 4) as i:
                for q in range(4):
                    split_hi(act, PIECES["merge"] + q + 1, 4 * i, TILES)
                    act.wait_ge(merge_ready, q + 4 * i + 1)
                    act.wait_ge(gains_loaded, 16)
                    nc.scalar.copy(merged_hi[:, bass.ds(4 * i + q, 1), :], work[:, 2:3, :]).then_inc(merged_rounded, 1)
            for k in range(KM):
                split_hi(act, PIECES["out"] + k + 1, 0, TILES)
                act.wait_ge(chunk_taken, CHUNKS["out"] + k + 1)
                round_chunk(2 * KM + KQ + KKV + k, x[:, k, :], gains[:, G_FFN2 + k:G_FFN2 + k + 1], act_hi[:, k, :])
            up_turn(1, 0, 0, first=True)
            with act.Fori(0, KF // 2 - 1) as i:
                up_turn(1, 1, i)
            down_turn(1, 0, 0, None, False)
            down_turn(1, 1, 0, None, True)
            root(5, bank[7][:, :], D_MODEL, square[:, :])

        @block.vector
        def _(dve):
            count = {"before": 0, "turn": 0, "earlier": 0, "per": 0}

            def one():
                count["turn"] += 1
                return 1

            def so_far():
                return count["before"] + count["turn"] + count["earlier"]

            def enter_loop(i, per):
                count.update(before=count["before"] + count["turn"], turn=0, earlier=i * per, per=per)

            def leave_loop(turns):
                assert count["turn"] == count["per"], count
                count.update(before=count["before"] + turns * count["per"], turn=0, earlier=0)

            def split_scaled(k, source, gain, hi, lo):
                dve.wait_ge(act_rounded, k + 1)
                nc.vector.scalar_tensor_tensor(out=lo, in0=source, scalar=gain, in1=hi.bitcast(F32),
                                               op0=ALU.mult, op1=ALU.subtract).then_inc(act_split, 1)

            def split_chunk(k, source, gain, hi, lo, sums, first):
                if lo is not None:
                    split_scaled(k, source, gain, hi, lo)
                dve.wait_ge(squared, k + 1)
                if first:
                    nc.vector.tensor_copy(sums, square[:, :]).then_inc(sumsq_added, 1)
                else:
                    dve.wait_ge(sumsq_added, k)
                    nc.vector.tensor_tensor(sums, sums, square[:, :], ALU.add).then_inc(sumsq_added, 1)

            def reciprocal_root(n, root, out):
                dve.wait_ge(root_ready, n + 1)
                nc.vector.reciprocal(out, root).then_inc(rstd_ready, 1)
                dve.wait_ge(rstd_ready, n + 1)

            def split_first(q, s, d, step):
                for n in SPLIT_FIRST[q] if s > q else SPLIT_AT_START[q]:
                    split_lo(dve, s - q + n, d, TILES)
                if q == 0:
                    step()

            def rotation_angles(q):
                rows = slice(QK_NOPE, P)
                a, n = rope[rows, :], turns[rows, :]

                def less_turns(part):
                    dve.wait_ge(own, so_far())
                    nc.vector.scalar_tensor_tensor(out=a, in0=n, scalar=-part, in1=a, op0=ALU.mult,
                                                   op1=ALU.add).then_inc(own, one())

                if q == 0:
                    dve.wait_ge(position_loaded, 16)
                    dve.wait_ge(scalars_loaded, 16)
                    nc.vector.tensor_copy(n, position_i[rows, :]).then_inc(own, one())
                    dve.wait_ge(own, so_far())
                    nc.vector.tensor_scalar(a, n, const[rows, C_FREQ:C_FREQ + 1], None, ALU.mult).then_inc(own, one())
                elif q == 1:
                    dve.wait_ge(own, so_far())
                    nc.vector.tensor_scalar(n, a, 1.0 / (2 * math.pi), const[rows, C_TURN:C_TURN + 1],
                                            ALU.mult, ALU.add).then_inc(own, one())
                    for magic in (1.5 * 2 ** 23, -1.5 * 2 ** 23):
                        dve.wait_ge(own, so_far())
                        nc.vector.tensor_scalar(n, n, magic, None, ALU.add).then_inc(own, one())
                elif q == 2:
                    for part in TWO_PI:
                        less_turns(part)
                else:
                    dve.wait_ge(own, so_far())
                    nc.vector.tensor_scalar(a, a, const[rows, C_PHASE:C_PHASE + 1], None, ALU.add).then_inc(own, one())
                    dve.wait_ge(own, so_far())
                    nc.vector.tensor_scalar(a, a, 3.1415925, -3.1415925, ALU.min, ALU.max).then_inc(angle_ready, 1)

            def bias_rows():
                dve.wait_ge(setup_pe, 1)
                for g in range(GROUPS):
                    at = slice(T5_AT[g], T5_AT[g] + T5_LEN[g])
                    last = nc.vector.tensor_tensor(t5_row[:, at], bank[4 + g][0:GROUP_HEADS, 0:T5_LEN[g]],
                                                   t5_mask[:, at], ALU.add)
                last.then_inc(rows_ready, 1)

            def up_turn(f, turn, i, first=False, rotate=False):
                for q in range(4):
                    s = PIECES[f"up{f + 1}"] + 4 * turn + q
                    c = CHUNKS[f"up{f + 1}"] + 4 * turn + q
                    j = 2 * turn + q // 2
                    hidden = KF * f + j
                    if first:
                        split_first(q, s, 4 * i, lambda: reciprocal_root((0, 4)[f], square[:, :], rstd[:, :]))
                    else:
                        split_lo(dve, s + 1, 4 * i, TILES)
                    if q % 2 == 0:
                        dve.wait_ge(piece_done, s + 4 * i + 1)
                        nc.vector.tensor_tensor(work[:, 0, :], bank[c % UP_BANKS][:, :], rstd[:, :], ALU.mult).then_inc(chunk_taken, 1)
                    else:
                        dve.wait_ge(silu_ready, hidden + 2 * i + 1)
                        nc.vector.tensor_tensor(work[:, 2, :], work[:, 1, :], rstd[:, :], ALU.mult).then_inc(own, one())
                        dve.wait_ge(piece_done, s + 4 * i + 1)
                        dve.wait_ge(own, so_far())
                        nc.vector.tensor_tensor(work[:, 3, :], bank[c % UP_BANKS][:, :], work[:, 2, :], ALU.mult).then_inc(chunk_taken, 1)
                        chunk = bass.ds(2 * i + j, 1)
                        dve.wait_ge(chunk_taken, CHUNKS[f"up{f + 1}"] + 4 * turn + q + 4 * i + 1)
                        dve.wait_ge(hid_rounded, hidden + 2 * i + 1)
                        nc.vector.tensor_tensor(hid_lo[:, chunk, :], work[:, 3:4, :], hid_hi[:, chunk, :].bitcast(F32),
                                                ALU.subtract).then_inc(hid_split, 1)
                    if rotate:
                        rotation_angles(q)
                        if q == 3:
                            bias_rows()

            def down_turn(f, turn, i, gain, final):
                for m in range(4):
                    for part in range(3):
                        s = PIECES[f"down{f + 1}"] + 12 * turn + 3 * m + part
                        if not (final and m == 3 and part == 2):
                            following = DOWN_PARTS[(part + 1) % 3]
                            split_lo(dve, s + 1, 12 * i, following[1] - following[0])
                    c = CHUNKS[f"down{f + 1}"] + 4 * turn + m
                    k = 4 * turn + m
                    chunk = bass.ds(4 * i + k, 1)
                    dve.wait_ge(piece_done, s + 12 * i + 1)
                    nc.vector.scalar_tensor_tensor(out=x[:, chunk, :], in0=bank[c % 2][:, :].rearrange("p (a n) -> p a n", a=1),
                                                   scalar=0.5, in1=x[:, chunk, :],
                                                   op0=ALU.mult, op1=ALU.add).then_inc(chunk_taken, 1)
                    dve.wait_ge(chunk_taken, c + 4 * i + 1)
                    before = (KM, 3 * KM + KQ + KKV)[f]
                    hi, lo, g = None, None, None
                    if gain is not None:
                        hi, lo, g = act_hi[:, chunk, :], act_lo[:, chunk, :], gains[:, bass.ds(4 * i + k + gain, 1)]
                    if not (final and m == 3):
                        split_chunk(4 * i + k + before, x[:, chunk, :], g, hi, lo, sumsq[:, :], False)

            def clear_sums():
                nc.vector.memset(sumsq[:, :], 0.0).then_inc(own, one())
                dve.wait_ge(own, so_far())

            def gate_take(p, parity, before):
                dve.wait_ge(piece_done, p)
                if before is not None:
                    dve.wait_ge(gate_ready, before)
                nc.vector.tensor_tensor(work[:, 0, :], bank[parity][:, :], rstd[:, :], ALU.mult).then_inc(chunk_taken, 1)

            nc.vector.memset(work[:, 0, :], 0.0).then_inc(zeros_ready, 1)
            for k in range(KM):
                split_scaled(k, x[:, k, :], gains[:, G_FFN1 + k:G_FFN1 + k + 1], act_hi[:, k, :], act_lo[:, k, :])
                if k == 0:
                    split_lo(dve, 0, 0, TILES)
            split_lo(dve, 1, 0, TILES)
            for k in range(KM):
                dve.wait_ge(squared, k + 1)
                if k == 0:
                    nc.vector.tensor_copy(sumsq[:, :], first_squares[0]).then_inc(sumsq_added, 1)
                else:
                    dve.wait_ge(sumsq_added, k)
                    nc.vector.tensor_tensor(sumsq[:, :], sumsq[:, :], first_squares[k % 2], ALU.add).then_inc(sumsq_added, 1)
                if k == 3:
                    split_lo(dve, 2, 0, TILES)
            up_turn(0, 0, 0, first=True)
            up_turn(0, 1, 0, rotate=True)
            with dve.Fori(0, UP_SAFE) as i:
                enter_loop(i, 2)
                up_turn(0, 2, i)
            leave_loop(UP_SAFE)
            dve.wait_ge(skew_stored, 16)
            with dve.Fori(0, KF // 2 - 2 - UP_SAFE) as i:
                enter_loop(i, 2)
                up_turn(0, 2 + UP_SAFE, i)
            leave_loop(KF // 2 - 2 - UP_SAFE)
            clear_sums()
            with dve.Fori(0, 2) as i:
                down_turn(0, 0, i, G_MIX, False)

            s, c = PIECES["latent"], CHUNKS["latent"]
            low, high = slice(QK_NOPE, QK_DIM), slice(QK_DIM, P)
            split_lo(dve, s + 1, 0, TILES)
            for q in range(5):
                if q != 1:
                    split_lo(dve, s + q + 2, 0, LORA_TILES if q == 4 else TILES)
                if q == 0:
                    reciprocal_root(1, square[:, :], rstd[:, :])
                    split_lo(dve, s + 3, 0, TILES)
                dve.wait_ge(piece_done, s + q + 1)
                n = LATENTS[q]
                latent = work[:, q % 2, :]
                nc.vector.tensor_tensor(latent, bank[(c + q) % UP_BANKS][:, :], rstd[:, :], ALU.mult).then_inc(chunk_taken, 1)
                dve.wait_ge(chunk_taken, c + q + 1)
                split_chunk(2 * KM + q, latent, gains[:, G_Q + n:G_Q + n + 1], lat_hi[:, n, :],
                            lat_lo[:, n, :], sumsq[:, :] if n < KQ else sumsq_kv[:, :], n in (0, KQ))
                if q == 2:
                    nc.vector.tensor_tensor(work[low, 2, :], rope[low, :], rstd[low, :], ALU.mult).then_inc(own, one())
                    nc.vector.tensor_tensor(work[high, 2, :], rope[high, :], rstd[high, :], ALU.mult).then_inc(own, one())
                    reciprocal_root(2, sumsq_kv[:, :], rstd_kv[:, :])
            source = bank[(c + 5) % UP_BANKS]
            dve.wait_ge(piece_done, s + 6)
            dve.wait_ge(own, so_far())
            nc.vector.tensor_tensor(mla_k[low, 0, :], source[low, :], work[low, 2, :], ALU.mult).then_inc(own, one())
            nc.vector.tensor_tensor(rotated[low, :], source[high, :], work[high, 2, :], ALU.mult).then_inc(chunk_taken, 1)
            split_lo(dve, s + 7, 0, TILES)

            def query_norm_and_rotary_key():
                reciprocal_root(3, square[:, :], rstd_q[:, :])
                nc.vector.tensor_tensor(rope_q[QK_NOPE:P, :], rope[QK_NOPE:P, :], rstd_q[QK_NOPE:P, :],
                                        ALU.mult).then_inc(own, one())
                dve.wait_ge(chunk_taken, c + 6)
                dve.wait_ge(own, so_far())
                nc.vector.tensor_tensor(mla_k[low, 0, :], mla_k[low, 0, :], rotated[low, :], ALU.add).then_inc(own, one())
                dve.wait_ge(own, so_far())
                nc.vector.tensor_copy(mla_k[low, 1, :], mla_k[low, 0, :]).then_inc(own, one())
                dve.wait_ge(own, so_far())

            def take_query(h, i, parity):
                low, high = slice(QK_NOPE, QK_DIM), slice(QK_DIM, P)
                out = mla_q[:, h % 2, :]
                nc.vector.tensor_tensor(out[0:QK_NOPE, :], bank[parity][0:QK_NOPE, :], rstd_q[0:QK_NOPE, :], ALU.mult)
                nc.vector.tensor_tensor(out[low, :], bank[parity][low, :], rope_q[low, :], ALU.mult)
                if h:
                    dve.wait_ge(head_ready, h + 2 * i)
                nc.vector.tensor_tensor(rotated[low, :], bank[parity][high, :], rope_q[high, :], ALU.mult)\
                  .then_inc(chunk_taken, 1)

            def add_rotated(h, c):
                low = slice(QK_NOPE, QK_DIM)
                dve.wait_ge(chunk_taken, c)
                out = mla_q[low, h % 2, :]
                nc.vector.tensor_tensor(out, out, rotated[low, :], ALU.add).then_inc(head_ready, 1)

            def take_key_value(h, parity):
                nc.vector.tensor_tensor(mla_k[0:QK_NOPE, h % 2, :], bank[parity][0:QK_NOPE, :], rstd_kv[0:QK_NOPE, :], ALU.mult)
                nc.vector.tensor_tensor(mla_vt[QK_NOPE:P, :], bank[parity][QK_NOPE:P, :], rstd_kv[QK_NOPE:P, :], ALU.mult)\
                  .then_inc(chunk_taken, 1)

            def maxima(h, i):
                dve.wait_ge(mla_scores, h + 2 * i + 1)
                for b, source in enumerate((bank[2][:, 0:P], bank[3][:, 0:2 * P], bank[2][:, P:SEQ], bank[4][:, :])):
                    last = nc.vector.tensor_reduce(mla_stats[:, 0, b:b + 1], source, AX.X, ALU.max)
                last.then_inc(own, one())
                dve.wait_ge(own, so_far())
                nc.vector.tensor_scalar(mla_stats[:, 1, :], mla_stats[:, 0, :], -MLA_SCALE, None, ALU.mult).then_inc(mla_max, 1)

            def normalize(h, i):
                dve.wait_ge(mla_exp, 4 * h + 8 * i + 4)
                nc.vector.reciprocal(mla_stats[:, 3, :], mla_stats[:, 2, :]).then_inc(own, one())
                dve.wait_ge(own, so_far())
                for b in range(BLOCKS):
                    row = b * (b + 1) // 2
                    p = mla_p[:, row * P:(row + b + 1) * P]
                    nc.vector.tensor_scalar(p, p, mla_stats[:, 3, b:b + 1], None, ALU.mult).then_inc(mla_scaled, 1)

            def take_mixed(k, units, source):
                dve.wait_ge(pv_done, units)
                nc.vector.tensor_copy(mixed[:, bass.ds(k, 1), :], source.rearrange("p (a n) -> p a n", a=1)).then_inc(mixed_taken, 1)

            def take_lora(s, d, h, i, between=None):
                c = first_chunk(h)
                dve.wait_ge(inner_done, h + 2 * i + 1)
                take_key_value(h, c % 2)
                if between is not None:
                    between()
                dve.wait_ge(piece_done, s + d + 1)
                take_query(h, i, (c + 1) % 2)
                add_rotated(h, c + 6 * i + 2)

            def attention(h, i, s, d, following):
                maxima(h, i)
                if h < MLA_HEADS - 1:
                    take_lora(s, d, h + 1, i, lambda: normalize(h, i))
                    split_lo(dve, s + 2, d, following[0])
                    gate_take(s + d + 2, gate_chunk(h) % 2, h + 1 + 2 * i)
                    if following[1]:
                        split_lo(dve, s + 3, d, following[1])
                else:
                    normalize(h, i)
                    split_lo(dve, s + 2, d, following[0])
                if h % 2:
                    take_mixed(h // 2 + i, 3 * h + 3 + 6 * i, bank[7][:, :])

            s = PIECES["mla"]
            take_lora(s, 0, 0, 0, query_norm_and_rotary_key)
            split_lo(dve, s + 2, 0, LORA_TILES)
            gate_take(s + 2, gate_chunk(-1) % 2, None)
            split_lo(dve, s + 3, 0, TILES)
            with dve.Fori(0, PAIRS - 1) as i:
                enter_loop(i, 2 * 2)
                attention(0, i, s + 2, 4 * i, (LORA_TILES, TILES))
                attention(1, i, s + 4, 4 * i, (LORA_TILES, TILES))
            leave_loop(PAIRS - 1)
            attention(MLA_HEADS - 2, 0, s + 2 * MLA_HEADS - 2, 0, (TILES, 0))
            attention(MLA_HEADS - 1, 0, s + 2 * MLA_HEADS - 1, 0, (TILES, 0))

            def dil_maxima(g, i):
                dve.wait_ge(bias_loaded, 16 * GROUPS)
                for e in range(2):
                    dve.wait_ge(dil_scores, 2 * g + e + 6 * i + 1)
                    one, two = (bank[2], bank[3]) if e == 0 else (bank[4], bank[7])
                    head = bass.ds(2 * i + e, 1)

                    def biased(out, source, bias):
                        return nc.vector.scalar_tensor_tensor(out=out, in0=source, scalar=DIL_SCALE, in1=bias,
                                                              op0=ALU.mult, op1=ALU.add)

                    p = dil_p[:, e, :]
                    if g == 0:
                        biased(p[:, 0:P].rearrange("p (a n) -> p a n", a=1), one[:, 0:P].rearrange("p (a n) -> p a n", a=1),
                               bias0[:, head, P:2 * P])
                        biased(p[:, P:3 * P].rearrange("p (a n) -> p a n", a=1),
                               one[:, P:3 * P].rearrange("p (a n) -> p a n", a=1), bias0[:, head, :])
                        last = biased(p[:, 3 * P:7 * P].rearrange("p (a n) -> p a n", a=2),
                                      two[:, :].rearrange("p (a n) -> p a n", a=2),
                                      bias0[:, head, :].to_broadcast([P, 2, 2 * P]))
                        spans = ((0, p[:, 0:P].rearrange("p (a n) -> p a n", a=1)),
                                 (1, p[:, P:7 * P].rearrange("p (a n) -> p a n", a=3)))
                    else:
                        first = (3 + 4 * g) * P
                        view = p[:, first:first + SEQ].rearrange("p (a n) -> p a n", a=BLOCKS)
                        last = biased(view, one[:, :].rearrange("p (a n) -> p a n", a=BLOCKS),
                                      bias12[:, g - 1, head, :].to_broadcast([P, BLOCKS, P]))
                        spans = ((0, view),)
                    last.then_inc(dil_taken, 1)
                    dve.wait_ge(dil_taken, 2 * g + e + 6 * i + 1)
                    for b, view in spans:
                        last = nc.vector.tensor_reduce(stats[:, 0, g, min(g, 1), 2 * b + e:2 * (b + view.shape[1]) + e - 1:2],
                                                       view, AX.X, ALU.max, negate=True)
                    last.then_inc(dil_max, 1)

            def take_projection(out, s, d, parity):
                dve.wait_ge(piece_done, s + d + 1)
                nc.vector.tensor_tensor(out, bank[parity][:, :], rstd[:, :], ALU.mult).then_inc(chunk_taken, 1)

            def group_weights(i):
                dve.wait_ge(stats_moved, i + 1)
                moved = exchanged
                mod, div = const[:, C_MOD:C_MOD + BLOCKS], const[:, C_DIV:C_DIV + BLOCKS]
                for at, n, mask in ((0, 8, div), (64, 16, mod)):
                    size = n * 8
                    view = "p (r k e) -> p r k e"
                    nc.vector.tensor_tensor(
                        moved[:, at:at + size].rearrange(view, k=BLOCKS, e=2),
                        bank[7][:, at:at + size].rearrange(view, k=BLOCKS, e=2),
                        mask.rearrange("p (a k e) -> p a k e", a=1, e=1).to_broadcast([P, n, BLOCKS, 2]), ALU.mult).then_inc(own, one())
                dve.wait_ge(own, so_far())
                for t in range(2):
                    for e in range(2):
                        source = moved[:, 0:64].rearrange("p (a t k e) -> p t e a k", a=BLOCKS, t=2, e=2)[:, t, e]
                        nc.vector.tensor_reduce(stats[:, t, 0, 1, e:8:2], source, AX.X, ALU.add)
                        for g in (1, 2):
                            source = moved[:, 64:192].rearrange("p (b t g k e) -> p t g e b k", b=BLOCKS, t=2, g=2, e=2)
                            last = nc.vector.tensor_reduce(stats[:, t, g, 0, e:8:2], source[:, t, g - 1, e], AX.X, ALU.add)
                last.then_inc(own, one())
                dve.wait_ge(own, so_far())
                maxima_of = stats[:, 0, :, :, :].rearrange("p g o n -> p g (o n)")
                sums_of = stats[:, 1, :, :, :].rearrange("p g o n -> p g (o n)")
                nc.vector.tensor_tensor(neg_top[:, :], maxima_of[:, 0], maxima_of[:, 1], ALU.min).then_inc(own, one())
                dve.wait_ge(own, so_far())
                nc.vector.tensor_tensor(neg_top[:, :], neg_top[:, :], maxima_of[:, 2], ALU.min).then_inc(own, one())
                dve.wait_ge(own, so_far())
                top = neg_top[:, :].rearrange("p (a n) -> p a n", a=1).to_broadcast([P, GROUPS, 4 * BLOCKS])
                nc.vector.tensor_tensor(weight[:, :, :], top, maxima_of, ALU.subtract).then_inc(weight_ready, 1)
                dve.wait_ge(weight_exp, i + 1)
                parts = exchanged[:, 0:GROUPS * 4 * BLOCKS]
                nc.vector.tensor_tensor(parts.rearrange("p (g n) -> p g n", g=GROUPS), weight[:, :, :],
                                                    sums_of, ALU.mult).then_inc(own, one())
                dve.wait_ge(own, so_far())
                nc.vector.tensor_reduce(total[:, :], parts.rearrange("p (g n) -> p n g", g=GROUPS), AX.X, ALU.add).then_inc(own, one())
                dve.wait_ge(own, so_far())
                nc.vector.reciprocal(total[:, :], total[:, :]).then_inc(own, one())
                dve.wait_ge(own, so_far())
                inverse = total[:, :].rearrange("p (a n) -> p a n", a=1).to_broadcast([P, GROUPS, 4 * BLOCKS])
                nc.vector.tensor_tensor(weight[:, :, :], weight[:, :, :], inverse, ALU.mult).then_inc(own, one())
                dve.wait_ge(own, so_far())

            def scale_probs(e):
                for g, order, b, blocks, first, width in ((0, 0, 0, 1, 0, P), (0, 0, 1, 3, P, 2 * P),
                                                          (1, 1, 0, 4, 7 * P, P), (2, 1, 0, 4, 11 * P, P)):
                    view = dil_p[:, e, first:first + blocks * width].rearrange("p (b n) -> p b n", b=blocks)
                    at = 8 * order + 2 * b + e
                    by = weight[:, g, at:at + 2 * blocks - 1:2].rearrange("p (b n) -> p b n", n=1)
                    nc.vector.tensor_tensor(view, view, by.to_broadcast([P, blocks, width]), ALU.mult).then_inc(dil_scaled, 1)

            def dilated_pair(i, first=False):
                s, d, c, e = PIECES["dil"], 12 * i, CHUNKS["dil"], 11 * i
                for q in range(12):
                    tiles = HALF if q in (9, 10) else TILES
                    if q or not first:
                        split_lo(dve, s + q + 1, d, tiles)
                    if q in (3, 5, 7):
                        dil_maxima(q // 2 - 1, i)
                    if q < 6:
                        out = (dil_q, dil_k)[q % 2][:, q // 2, :]
                    else:
                        out = dil_vt[:, q % 2, :]
                    if q == 0 and not first:
                        take_mixed(PAIRS - 1 + i, 3 * MLA_HEADS + 8 * i, bank[2][:, :])
                    if q < 9:
                        take_projection(out, s + q, d, (c + q) % 2)
                    if q == 9:
                        group_weights(i)
                        scale_probs(0)
                        gate_take(s + d + 10, (c + 9) % 2, MLA_HEADS + 2 * i)
                        scale_probs(1)
                gate_take(s + d + 12, 4, MLA_HEADS + 2 * i + 1)
            dilated_pair(0, first=True)
            with dve.Fori(1, PAIRS) as i:
                enter_loop(i - 1, 2 + 1 + 2 + 4)
                dilated_pair(i)
            leave_loop(PAIRS - 1)

            for k in range(2 * PAIRS):
                if k == PAIRS:
                    take_mixed(2 * PAIRS - 1, 3 * MLA_HEADS + 8 * PAIRS, bank[2][:, :])
                dve.wait_ge(mixed_rounded, k + 1)
                nc.vector.tensor_tensor(act_lo[:, k, :], mixed[:, k, :], act_hi[:, k, :].bitcast(F32),
                                        ALU.subtract).then_inc(mixed_split, 1)
            with dve.Fori(0, KM // 4) as i:
                for q in range(4):
                    s, c = PIECES["merge"] + q, CHUNKS["merge"] + 2 * q
                    m = 4 * i + q
                    split_lo(dve, s + 1, 4 * i, TILES)
                    dve.wait_ge(inner_done, MLA_HEADS + q + 4 * i + 1)
                    nc.vector.scalar_tensor_tensor(out=work[:, 0:1, :], in0=gates[:, bass.ds(m, 1), :], scalar=1.0,
                                                   in1=bank[0][:, :].rearrange("p (a n) -> p a n", a=1),
                                                   op0=ALU.add, op1=ALU.mult).then_inc(chunk_taken, 1)
                    dve.wait_ge(piece_done, s + 4 * i + 1)
                    nc.vector.scalar_tensor_tensor(out=work[:, 1:2, :], in0=gates[:, bass.ds(m + KM, 1), :], scalar=1.0,
                                                   in1=bank[1][:, :].rearrange("p (a n) -> p a n", a=1),
                                                   op0=ALU.add, op1=ALU.mult).then_inc(chunk_taken, 1)
                    dve.wait_ge(chunk_taken, c + 8 * i + 2)
                    nc.vector.tensor_tensor(work[:, 2, :], work[:, 0, :], work[:, 1, :], ALU.add).then_inc(merge_ready, 1)
                    dve.wait_ge(merge_ready, q + 4 * i + 1)
                    dve.wait_ge(merged_rounded, q + 4 * i + 1)
                    nc.vector.tensor_tensor(merged_lo[:, bass.ds(m, 1), :], work[:, 2:3, :],
                                            merged_hi[:, bass.ds(m, 1), :].bitcast(F32), ALU.subtract).then_inc(merged_split, 1)
            clear_sums()
            with dve.Fori(0, KM // 4) as i:
                for q in range(4):
                    s, c = PIECES["out"] + q, CHUNKS["out"] + q
                    chunk = bass.ds(4 * i + q, 1)
                    split_lo(dve, s + 1, 4 * i, TILES)
                    dve.wait_ge(piece_done, s + 4 * i + 1)
                    nc.vector.scalar_tensor_tensor(out=x[:, chunk, :], in0=bank[c % 2][:, :].rearrange("p (a n) -> p a n", a=1),
                                                   scalar=0.5, in1=x[:, chunk, :],
                                                   op0=ALU.mult, op1=ALU.add).then_inc(chunk_taken, 1)
                    dve.wait_ge(chunk_taken, c + 4 * i + 1)
                    split_chunk(4 * i + q + 2 * KM + KQ + KKV, x[:, chunk, :], gains[:, bass.ds(4 * i + q + G_FFN2, 1)],
                                act_hi[:, chunk, :], act_lo[:, chunk, :], sumsq[:, :], False)
            up_turn(1, 0, 0, first=True)
            with dve.Fori(0, KF // 2 - 1) as i:
                enter_loop(i, 2)
                up_turn(1, 1, i)
            leave_loop(KF // 2 - 1)
            clear_sums()
            down_turn(1, 0, 0, None, False)
            down_turn(1, 1, 0, None, True)
            reciprocal_root(5, square[:, :], rstd[:, :])
            for k in range(KM):
                nc.vector.scalar_tensor_tensor(out=x[:, k, :], in0=x[:, k, :], scalar=gains[:, G_FINAL + k:G_FINAL + k + 1],
                                               in1=rstd[:, :], op0=ALU.mult, op1=ALU.mult).then_inc(y_ready, 1)


def _tiles(w):
    k, n = w.shape
    return w.reshape(k // P, P, n // P, P).transpose(2, 1, 0, 3).reshape(n // P, P, k)


def _swapped(w):
    half = QK_ROPE // 2
    return np.concatenate([w, w[:, half:], w[:, :half]], axis=1)


def kernel(**inputs):
    import concourse.bacc as bacc
    from concourse.bass_utils import run_bass_kernel_spmd

    given = {k: np.asarray(v) for k, v in inputs.items()}
    arrays = {}

    def put(name, a):
        arrays[name] = np.ascontiguousarray(a)

    put("x_t", given["x"][0].T.reshape(KM, P, SEQ))
    put("positions", given["positions"])
    put("rel_bias", given["rel_bias"])
    columns = [given[n].reshape(-1, P).T for n in
               ("ffn1_norm", "mix_norm", "ffn2_norm", "norm_final", "q_norm", "kv_norm", "b_gate")]
    put("gains", np.concatenate(columns, axis=1))
    for name, a in zip(("tables", "onehot", "t5_masks"), shape_constants()):
        put(name, a)
    for f in ("ffn1", "ffn2"):
        for w in ("gate", "up", "down"):
            put(f"{f}_{w}", _tiles(given[f"{f}_w_{w}"][0]))
    w_in = given["w_in"][0]
    rotary = _swapped(w_in[:, IN_ROPE:IN_Q])
    put("w_latent", _tiles(np.concatenate([w_in[:, IN_KV:IN_ROPE], w_in[:, :IN_KV], rotary, rotary], axis=1)))
    gates = _tiles(w_in[:, IN_GATES:])
    put("w_mla_gates", gates[:MLA_HEADS])
    pairs = []
    for pair in range(PAIRS):
        def heads(start, g):
            at = start + (g * GROUP_HEADS + 2 * pair) * HEAD_DIM
            return _tiles(w_in[:, at:at + 2 * HEAD_DIM])
        qk = [heads(start, g) for g in range(GROUPS) for start in (IN_Q, IN_K)]
        pairs.append(np.concatenate([*qk, *(heads(IN_V, g) for g in range(GROUPS)), gates[MLA_HEADS + 2 * pair:MLA_HEADS + 2 * pair + 2]]))
    put("w_dil", np.stack(pairs))
    up_q = given["w_uq"][0].reshape(Q_LORA, MLA_HEADS, QK_DIM)
    up_kv = _tiles(given["w_ukv"][0])
    rows = []
    for h in range(MLA_HEADS):
        query = np.concatenate([up_q[:, h, :QK_NOPE], _swapped(up_q[:, h, QK_NOPE:])], axis=1)
        rows.append(np.concatenate([_tiles(query)[0], up_kv[h]], axis=1))
    put("w_lora_up", np.stack(rows))
    put("w_branches", np.concatenate([_tiles(given["w_br_mla"][0]), _tiles(given["w_br_dil"][0])], axis=2))
    put("w_out", _tiles(given["w_out"][0]))

    nc = bacc.Bacc("TRN2", target_bir_lowering=False, num_devices=1)
    a = {n: nc.dram_tensor("in_" + n, v.shape, mybir.dt.from_np(v.dtype), kind="ExternalInput").ap() for n, v in arrays.items()}
    skew = nc.dram_tensor("skew", (GROUP_HEADS, P * (T5_END + 1)), F32, kind="Internal").ap()
    y_t = nc.dram_tensor("y_t", (KM, P, SEQ), F32, kind="ExternalOutput").ap()
    ffn = [[a[f"{f}_{w}"] for w in ("gate", "up", "down")] for f in ("ffn1", "ffn2")]
    decoder_layer(nc, a["x_t"], a["positions"], a["rel_bias"], a["gains"], a["tables"], a["onehot"], a["t5_masks"],
                  ffn, a["w_latent"], a["w_lora_up"], a["w_mla_gates"], a["w_dil"], a["w_branches"], a["w_out"],
                  skew, y_t)
    result = run_bass_kernel_spmd(nc, [{"in_" + n: v for n, v in arrays.items()}], core_ids=[0]).results[0]["y_t"]
    return np.ascontiguousarray(result.reshape(D_MODEL, SEQ).T).reshape(1, SEQ, D_MODEL)
```
